# Optimizing a Trainium2 kernel written in Bass

```python
import jax, jax.numpy as jnp
from jax import lax
import numpy as np

D_MODEL = 1024
BATCH = 1
SEQ = 2048
DEPTH = 1

CHUNK = 64
POOL_WIDTH = D_MODEL // 2
N_POOL_GROUPS = 4
POOL_GROUP = POOL_WIDTH // N_POOL_GROUPS
POOL_WINDOWS = (2, 4, 8, 16)
CONV_WIDTH = D_MODEL // 2
CONV_K = 3
N_BRANCHES = 2
N_EXPERTS = 64
TOP_K = 8
EXPERT_HIDDEN = 256
SHARED_HIDDEN = 256
ROUTED_SCALE = 2.5
ROW_BLOCK = 128
EPS = 1e-6
IN_COLS = POOL_WIDTH + 3 * CONV_WIDTH + N_BRANCHES * D_MODEL

kernel_name = "hybrid_pool_shortconv_moe_block"

def rmsnorm(x, g):
    xf = x.astype(jnp.float32)
    r = lax.rsqrt(jnp.mean(xf * xf, axis=-1, keepdims=True) + EPS)
    return (xf * r).astype(x.dtype) * g

def pool_mixer(u, w_group, scale):
    b, s, _ = u.shape
    ug = u.reshape(b, s, N_POOL_GROUPS, POOL_GROUP)
    cs = jnp.cumsum(ug.astype(jnp.float32), axis=1)
    t = jnp.arange(s)
    outs = []
    for gi, w in enumerate(POOL_WINDOWS):
        c = cs[:, :, gi]
        prev = jnp.pad(c, ((0, 0), (w, 0), (0, 0)))[:, :s]
        cnt = jnp.minimum(t + 1, w).astype(jnp.float32)[None, :, None]
        outs.append((c - prev) / cnt)
    pooled = jnp.stack(outs, axis=2).astype(u.dtype) - ug
    mixed = jnp.einsum('bsgc,gcd->bsgd', pooled, w_group)
    return mixed.reshape(b, s, POOL_WIDTH) * scale

def causal_depthwise_conv3(u, w):
    s = u.shape[1]
    up = jnp.pad(u, ((0, 0), (CONV_K - 1, 0), (0, 0)))
    return up[:, 0:s] * w[0] + up[:, 1:s + 1] * w[1] + up[:, 2:s + 2] * w[2]

def swiglu(h, w_gate, w_up, w_down):
    return (jax.nn.silu(h @ w_gate) * (h @ w_up)) @ w_down

def routed_experts(h, w_router, router_bias, e_gate, e_up, e_down):
    t_tok, d = h.shape
    logits = (h.astype(jnp.float32) @ w_router.astype(jnp.float32))
    scores = jax.nn.sigmoid(logits)
    _, idx = lax.top_k(scores + router_bias.astype(jnp.float32), TOP_K)
    wsel = jnp.take_along_axis(scores, idx, axis=1)
    wsel = wsel / jnp.sum(wsel, axis=1, keepdims=True) * ROUTED_SCALE

    n_assign = t_tok * TOP_K
    flat_e = idx.reshape(n_assign)
    flat_tok = jnp.repeat(jnp.arange(t_tok, dtype=jnp.int32), TOP_K)
    flat_w = wsel.reshape(n_assign)
    order = jnp.argsort(flat_e, stable=True)
    sorted_e = flat_e[order]
    counts = jnp.bincount(flat_e, length=N_EXPERTS)
    padded = (counts + ROW_BLOCK - 1) // ROW_BLOCK * ROW_BLOCK
    start = jnp.cumsum(counts) - counts
    pad_end = jnp.cumsum(padded)
    pad_start = pad_end - padded
    rank = jnp.arange(n_assign) - start[sorted_e]
    dest = pad_start[sorted_e] + rank

    n_rows = n_assign + N_EXPERTS * ROW_BLOCK
    n_blk = n_rows // ROW_BLOCK
    row_tok = jnp.zeros((n_rows,), jnp.int32).at[dest].set(flat_tok[order])
    row_w = jnp.zeros((n_rows,), jnp.float32).at[dest].set(flat_w[order])
    blk_e = jnp.clip(jnp.searchsorted(pad_end, jnp.arange(n_blk) * ROW_BLOCK, side='right'),
                     0, N_EXPERTS - 1)
    xs = h[row_tok].reshape(n_blk, ROW_BLOCK, d)

    def expert_block(args):
        xb, e = args
        return swiglu(xb, e_gate[e], e_up[e], e_down[e])

    ys = lax.map(expert_block, (xs, blk_e)).reshape(n_rows, d)
    ys = ys * row_w[:, None].astype(ys.dtype)
    return jax.ops.segment_sum(ys, row_tok, num_segments=t_tok)

def setup_inputs(seed: int = 0) -> dict:
    key = jax.random.key(seed)
    ks = jax.random.split(key, 24)
    f32 = jnp.float32
    nrm = lambda k, shape, fan_in: jax.random.normal(k, shape, f32) * (fan_in ** -0.5)
    d = D_MODEL
    return {
        "x": jax.random.normal(ks[0], (BATCH, SEQ, d), f32),
        "g_mix": 1.0 + 0.05 * jax.random.normal(ks[1], (d,), f32),
        "w_in": nrm(ks[2], (d, IN_COLS), d),
        "b_gate": 0.05 * jax.random.normal(ks[3], (N_BRANCHES * d,), f32),
        "w_pool_group": nrm(ks[4], (N_POOL_GROUPS, POOL_GROUP, POOL_GROUP), POOL_GROUP),
        "pool_scale": 1.0 + 0.1 * jax.random.normal(ks[5], (POOL_WIDTH,), f32),
        "w_pool_out": nrm(ks[6], (POOL_WIDTH, d), POOL_WIDTH),
        "conv_w": nrm(ks[7], (CONV_K, CONV_WIDTH), CONV_K),
        "w_conv_out": nrm(ks[8], (CONV_WIDTH, d), CONV_WIDTH),
        "w_o": nrm(ks[9], (d, d), d),
        "g_ffn": 1.0 + 0.05 * jax.random.normal(ks[10], (d,), f32),
        "w_router": nrm(ks[11], (d, N_EXPERTS), d),
        "router_bias": 0.01 * jax.random.normal(ks[12], (N_EXPERTS,), f32),
        "e_gate": nrm(ks[13], (N_EXPERTS, d, EXPERT_HIDDEN), d),
        "e_up": nrm(ks[14], (N_EXPERTS, d, EXPERT_HIDDEN), d),
        "e_down": nrm(ks[15], (N_EXPERTS, EXPERT_HIDDEN, d), EXPERT_HIDDEN),
        "s_gate": nrm(ks[16], (d, SHARED_HIDDEN), d),
        "s_up": nrm(ks[17], (d, SHARED_HIDDEN), d),
        "s_down": nrm(ks[18], (SHARED_HIDDEN, d), SHARED_HIDDEN),
        "g_final": 1.0 + 0.05 * jax.random.normal(ks[19], (d,), f32),
    }

def reference(x, g_mix, w_in, b_gate, w_pool_group, pool_scale, w_pool_out, conv_w,
              w_conv_out, w_o, g_ffn, w_router, router_bias, e_gate, e_up, e_down,
              s_gate, s_up, s_down, g_final):
    b, s, d = x.shape
    for _ in range(DEPTH):
        h = rmsnorm(x, g_mix)
        proj = h @ w_in
        o0 = POOL_WIDTH
        o1 = o0 + CONV_WIDTH
        o2 = o1 + CONV_WIDTH
        o3 = o2 + CONV_WIDTH
        u_pool = proj[..., :o0]
        gb = proj[..., o0:o1]
        gc = proj[..., o1:o2]
        v = proj[..., o2:o3]
        gates = jax.nn.sigmoid(proj[..., o3:] + b_gate)
        gate_a = gates[..., :d]
        gate_b = gates[..., d:]

        branch_a = pool_mixer(u_pool, w_pool_group, pool_scale) @ w_pool_out
        branch_b = (gb * causal_depthwise_conv3(gc * v, conv_w)) @ w_conv_out
        merged = gate_a * branch_a + gate_b * branch_b
        x = x + merged @ w_o

        h2 = rmsnorm(x, g_ffn).reshape(b * s, d)
        shared = swiglu(h2, s_gate, s_up, s_down)
        routed = routed_experts(h2, w_router, router_bias, e_gate, e_up, e_down)
        x = x + (shared + routed).reshape(b, s, d)
    return rmsnorm(x, g_final)


_drawn_inputs = setup_inputs


def setup_inputs(seed=0):
    import zlib

    import numpy as np

    out = dict(_drawn_inputs(seed))
    spreads = {}
    factors = {}
    for name, (base, spread) in spreads.items():
        noise = np.random.default_rng([zlib.crc32(name.encode()), seed]).standard_normal(out[name].shape)
        drawn = base * np.exp(spread * noise) if base else spread * noise
        out[name] = __import__('jax').numpy.asarray(drawn.astype(out[name].dtype))
    for name, factor in factors.items():
        out[name] = (out[name] * factor).astype(out[name].dtype)
    return out
```

```python
from contextlib import ExitStack

import numpy as np

import concourse.bass as bass
from concourse import mybir

F32 = mybir.dt.float32
F32R = mybir.dt.float32r
BF16 = mybir.dt.bfloat16
I32 = mybir.dt.int32
U32 = mybir.dt.uint32
ALU = mybir.AluOpType
ACT = mybir.ActivationFunctionType
AX = mybir.AxisListType

P = 128
D = 1024
S = 2048
KD = D // P
T = 512
NCH = S // T
TT = T // P
NT = S // P
G = 4
WINDOWS = (2, 4, 8, 16)
HALO = 16
MT = D // P
UNITS = 48
CONV0, MERGE0, BACK0 = G, 4 * G, 4 * G + 3 * MT
NE = 64
TOPK = 8
H = 256
SCALE = 2.5
EPS = 1e-6
SHARED_BLOCKS = S // P
NBMAX = S * TOPK // P + NE + SHARED_BLOCKS
NB = NBMAX + 4
ROWS = S
LISTS = NE + 2
PIECES = 6


def wait(eng, sem, value):
    if isinstance(value, int) and value <= 0:
        return
    eng.wait_ge(sem, value)


def carry(eng, marks):
    eng.sem_inc(marks[eng.engine.name], 1)


def ds1(i):
    return bass.ds(i, 1)


def inverse_root(nc, pool, dst, src, minus_half):
    nc.gpsimd.tensor_scalar(dst, src, EPS, None, ALU.add)
    pool.drain()
    return nc.gpsimd.tensor_tensor(dst, dst, minus_half[:, :], ALU.pow)


def build(nc, x, units, wgroup, pool_scale, conv_w, b_gate, g_mix, g_ffn, g_final, w_router,
          router_bias, experts, inv_count, ident, tri, iotas, out):
    acc = nc.dram_tensor("acc", [S + P, D], F32, kind="Internal").ap()
    h2_dram = nc.dram_tensor("h2_dram", [S + P, D], F32, kind="Internal").ap()
    lists = nc.dram_tensor("lists", [LISTS * ROWS, 2], I32, kind="Internal").ap()

    with ExitStack() as ctx:
        def sem(name):
            return ctx.enter_context(nc.semaphore(name))

        marks = {n: sem(f"mark_{n}") for n in ("Pool", "PE", "DVE", "SP")}
        table = ctx.enter_context(nc.sbuf_tensor("table", [1, 2 * NB + 2], I32))
        route(nc, sem, marks, table, acc, h2_dram, lists, x, units, wgroup, pool_scale, conv_w, b_gate,
              g_mix, g_ffn, w_router, router_bias, inv_count, ident, tri, iotas)
        mixture(nc, sem, marks, table, acc, h2_dram, lists, experts, ident)
        final_norm(nc, sem, marks, acc, g_final, out)


def route(nc, sem, marks, table, acc, h2_dram, lists, x, units, wgroup, pool_scale, conv_w, b_gate,
          g_mix, g_ffn, w_router, router_bias, inv_count, ident_in, tri_in, iotas):
    x_tiles = x.rearrange("(n p) d -> n p d", p=P)
    acc_chunks = acc[0:S, :].rearrange("(c i p) d -> c p i d", p=P, i=TT)
    x_chunks = x.rearrange("(c i p) d -> c p i d", p=P, i=TT)
    h2_tiles = h2_dram.rearrange("(n p) d -> n p d", p=P)

    with ExitStack() as ctx:
        def sb(name, shape, dt=F32):
            return ctx.enter_context(nc.sbuf_tensor(name, shape, dt))

        ident = sb("eye", [P, P])
        tri = sb("triangle", [P, P])
        ones = sb("ones", [P, P])
        iota_e = sb("iota_e", [P, NE])
        iota_j = sb("iota_j", [NE, NB])
        from16 = sb("from16", [1, NB])
        gmix = sb("gmix", [P, D])
        gffn = sb("gffn", [P, D])
        wr = sb("wr", [P, KD, NE])
        rbias = sb("rbias", [P, NE])
        pscale = sb("pscale", [P, G])
        cw = sb("cw", [P, G, 3])
        bg = sb("bg", [P, 2 * MT])
        icnt = sb("icnt", [P, G, HALO])
        wg = sb("wg", [P, G, P])
        wgh = sb("wgh", [P, G, P], F32R)
        wgl = sb("wgl", [P, G, P], F32R)
        raw = sb("raw", [P, 2, D])
        uh = [sb(f"uh{s}", [P, KD, P], F32R) for s in range(2)]
        ul = [sb(f"ul{s}", [P, KD, P], F32R) for s in range(2)]
        hh = sb("hh", [P, KD, T], F32R)
        hl = sb("hl", [P, KD, T], F32R)
        ah = sb("ah", [P, G, T], F32R)
        al = sb("al", [P, G, T], F32R)
        bh = sb("bh", [P, G, T], F32R)
        bl = sb("bl", [P, G, T], F32R)
        mh = sb("mh", [P, MT, T], F32R)
        ml = sb("ml", [P, MT, T], F32R)
        xin = [sb(f"xin{s}", [P, D]) for s in range(2)]
        x2 = sb("x2", [P, TT, D])
        h2 = [sb(f"h2{s}", [P, D]) for s in range(2)]
        h2t = sb("h2t", [P, KD, P])
        junk = sb("junk", [P, D], BF16)
        mean = sb("mean", [P, 2 * TT])
        rstd = sb("rstd", [P, 2 * TT])
        minus_half = sb("minus_half", [P, 1])
        ubuf = sb("ubuf", [P, HALO + T])
        uhalo = sb("uhalo", [P, G, HALO])
        win = [sb(f"win{s}", [P, HALO + T]) for s in range(2)]
        pooled = sb("pooled", [P, T])
        ph = sb("ph", [P, T], F32R)
        pl = sb("pl", [P, T], F32R)
        csb = sb("csb", [P, T])
        cv = sb("cv", [P, 2 + T])
        cvhalo = sb("cvhalo", [P, G, 2])
        tap = win[0][:, 0:T]
        bcv = pooled[:, :]
        siga = sb("siga", [P, T])
        sigb = sb("sigb", [P, T])
        m1 = win[0][:, 0:T]
        m2 = win[1][:, 0:T]
        sc = sb("sc", [P, NE])
        biased = sb("biased", [P, NE])
        top = sb("top", [P, TOPK])
        idx = sb("idx", [P, TOPK], U32)
        idxf = sb("idxf", [P, TOPK])
        hot = sb("hot", [P, TOPK, NE])
        hotx = win[1][:, 0:TOPK * NE].rearrange("p (k e) -> p k e", k=TOPK)
        mask = sb("mask", [P, NE])
        w8 = sb("w8", [P, TOPK])
        den = sb("den", [P, 1])
        rank = sb("rank", [P, NE])
        r8 = sb("r8", [P, TOPK])
        taken = sb("taken", [P, NE])
        total = sb("total", [NE, 1])
        tokid = sb("tokid", [P, NT], I32)
        pay = [sb(f"pay{s}", [P, TOPK, 2], I32) for s in range(2)]
        dest = [sb(f"dest{s}", [P, TOPK], I32) for s in range(2)]
        blank = x2[:, :, :].rearrange("p i d -> p (i d)").bitcast(I32)[:, 0:LISTS * ROWS // P * 2]
        blank = blank.rearrange("p (r two) -> p r two", two=2)
        shared_list = pay[0][:, :, :]
        shared_list2 = pay[1][:, :, :]
        zero_rows = xin[0]
        nblk_i = sb("nblk_i", [NE, 1], I32)
        nblk = sb("nblk", [NE, 1])
        bend = sb("bend", [NE, 1])
        over = sb("over", [NE, NB])
        eid_f = sb("eid_f", [1, NB])
        bst_f = sb("bst_f", [1, NB])
        row_f = sb("row_f", [1, NB])

        banks = [ctx.enter_context(nc.psum_tensor(f"bank{b}", [P, 512], F32)) for b in range(4)]
        ps_t = ctx.enter_context(nc.psum_tensor("ps_t", [P, 2, 512], F32))
        proj = [ps_t[:, 0, :], ps_t[:, 1, :]]
        ps_t8 = ps_t[:, :, :].rearrange("p b (k t) -> p (b k) t", t=P)
        ps_a = ctx.enter_context(nc.psum_tensor("ps_a", [P, 512], F32))
        ps_b = ctx.enter_context(nc.psum_tensor("ps_b", [P, 512], F32))

        const_in = sem("const_in")
        halo_zero = sem("halo_zero")
        blank_made = sem("blank_made")
        dram_set = sem("dram_set")
        raw_in = [sem("raw_in0"), sem("raw_in1")]
        unit_hi = sem("unit_hi")
        unit_ready = sem("unit_ready")
        unit_done = sem("unit_done")
        x_in = [sem("x_in0"), sem("x_in1")]
        res_in = sem("res_in")
        acc_out = sem("acc_out")
        h2_out = [sem("h2_out0"), sem("h2_out1")]
        x_mean = sem("x_mean")
        x_rstd = sem("x_rstd")
        x_normed = sem("x_normed")
        x_turned = sem("x_turned")
        x_hi = sem("x_hi")
        x_split = sem("x_split")
        grp_hi = sem("grp_hi")
        grp_split = sem("grp_split")
        u_copied = sem("u_copied")
        pooled_split = sem("pooled_split")
        mixed_done = sem("mixed_done")
        a_hi = sem("a_hi")
        a_split = sem("a_split")
        c_copied = sem("c_copied")
        cv_done = sem("cv_done")
        b_split = sem("b_split")
        gate_a = sem("gate_a")
        gate_b = sem("gate_b")
        branches_read = sem("branches_read")
        merged = sem("merged")
        wo_done = sem("wo_done")
        x2_added = sem("x2_added")
        y_mean = sem("y_mean")
        y_rstd = sem("y_rstd")
        y_normed = sem("y_normed")
        y_turned = sem("y_turned")
        y_copied = sem("y_copied")
        logits_done = sem("logits_done")
        scored = sem("scored")
        masked = sem("masked")
        ranked = sem("ranked")
        dest_ready = sem("dest_ready")
        list_out = [sem("list_out0"), sem("list_out1")]
        tab_a = sem("tab_a")
        tab_b = sem("tab_b")
        tab_c = sem("tab_c")
        tab_d = sem("tab_d")

        NCONST = 16 * 15
        SETS = 16 * 5

        block = ctx.enter_context(nc.Block())

        @block.sync
        def _(sp):
            def load_unit(u, k):
                wait(sp, unit_ready, u - 1)
                sp.dma_start(raw[:, k % 2, :], units[k % UNITS]).then_inc(raw_in[k % 2], 16)

            def load_units_loop(c, lo, n, base):
                with sp.Fori(0, n) as i:
                    for s in range(2):
                        k = i * 2 + (lo + s)
                        sp.wait_ge(unit_ready, k + (base - 1))
                        sp.dma_start(raw[:, s, :], units[ds1(k % UNITS)].rearrange("a p f -> p (a f)")
                                     ).then_inc(raw_in[s], 16)

            load_unit(0, 0)
            load_unit(1, 1)
            for dst, src in ((ident, ident_in), (tri, tri_in), (iota_j, iotas[2, 0:NE, :]),
                             (from16, iotas[3, 0:1, :]), (iota_e, iotas[1, :, 0:NE]),
                             (gmix, g_mix), (gffn, g_ffn), (wr, w_router), (rbias, router_bias),
                             (pscale, pool_scale), (cw, conv_w), (bg, b_gate), (icnt, inv_count),
                             (wg, wgroup)):
                sp.dma_start(dst[tuple(slice(None) for _ in dst.shape)], src).then_inc(const_in, 16)
            sp.dma_start(ones[:, :], iotas[0, :, 0:P]).then_inc(const_in, 16)

            def stage(c, tiles, b=None):
                with sp.Fori(0, MERGE0 // 2) as i:
                    for s in range(2):
                        k = i * 2 + s + 2
                        sp.wait_ge(unit_ready, k + (c * UNITS - 1))
                        sp.dma_start(raw[:, s, :], units[ds1(k)].rearrange("a p f -> p (a f)")
                                     ).then_inc(raw_in[s], 16)
                if tiles:
                    sp.wait_ge(x2_added, c * 8 + 4)
                    sp.dma_start(acc_chunks[ds1(b)].rearrange("a p i d -> p (a i) d"),
                                 x2[:, :, :]).then_inc(acc_out, 16)
                    sp.wait_ge(acc_out, c * 16)
                    carry(sp, marks)
                    sp.wait_ge(y_normed, c * TT)
                    carry(sp, marks)
                    sp.dma_start(x2[:, :, :], x_chunks[ds1(c)].rearrange("a p i d -> p (a i) d")
                                 ).then_inc(res_in, 16)
                else:
                    sp.wait_ge(dram_set, SETS)
                    sp.dma_start(x2[:, :, :], x_chunks[c]).then_inc(res_in, 16)
                with sp.Fori(0, (UNITS - MERGE0) // 2) as i:
                    for s in range(2):
                        k = i * 2 + s + 2 + MERGE0
                        sp.wait_ge(unit_ready, k + (c * UNITS - 1))
                        sp.dma_start(raw[:, s, :], units[ds1(k % UNITS)].rearrange("a p f -> p (a f)")
                                     ).then_inc(raw_in[s], 16)

            stage(0, False)
            with sp.Fori(0, NCH - 1) as b:
                stage(b + 1, True, b)
            sp.wait_ge(x2_added, NCH * 8 + 4)
            sp.dma_start(acc_chunks[NCH - 1], x2[:, :, :]).then_inc(acc_out, 16)
            sp.wait_ge(acc_out, NCH * 16)

        @block.gpsimd
        def _(pool):
            def x_tile(n, s, first=False):
                if first:
                    pool.dma_start(xin[s][:, :], x_tiles[n]).then_inc(x_in[s], 16)
                    return
                pool.dma_start(xin[s][:, :], x_tiles[ds1(n % NT)].rearrange("a p d -> p (a d)")
                               ).then_inc(x_in[s], 16)

            def x_norm(n, s, col):
                pool.wait_ge(x_mean, n + 1)
                carry(pool, marks)
                inverse_root(nc, pool, rstd[:, col:col + 1], mean[:, col:col + 1], minus_half
                             ).then_inc(x_rstd, 1)
                wait(pool, x_turned, n)
                x_tile(n + 1, 1 - s, first=isinstance(n, int) and n + 1 < NT)

            def y_norm(n, q):
                pool.wait_ge(y_mean, n + 1)
                carry(pool, marks)
                inverse_root(nc, pool, rstd[:, TT + q:TT + q + 1], mean[:, TT + q:TT + q + 1],
                             minus_half).then_inc(y_rstd, 1)

            def scatter(n, q):
                pool.wait_ge(dest_ready, n + 1)
                carry(pool, marks)
                for k in range(TOPK):
                    nc.gpsimd.indirect_dma_start(
                        lists, bass.IndirectOffsetOnAxis(ap=dest[q % 2][:, k:k + 1], axis=0),
                        pay[q % 2][:, k, :], None).then_inc(list_out[q % 2], 16)

            nc.gpsimd.iota(blank[:, :, 0], pattern=[[1, LISTS * ROWS // P]], base=0,
                           channel_multiplier=(LISTS * ROWS // P) % P)
            nc.gpsimd.memset(blank[:, :, 1], 0)
            nc.gpsimd.memset(minus_half[:, :], -0.5)
            nc.gpsimd.iota(tokid[:, :], pattern=[[P, NT]], base=0, channel_multiplier=1)
            nc.gpsimd.memset(xin[0][:, :], 0.0).then_inc(blank_made, 1)
            pool.wait_ge(blank_made, 2)
            pool.dma_start(lists.rearrange("(p r) two -> p r two", p=P), blank
                           ).then_inc(dram_set, 16)
            pool.dma_start(acc[S:S + P, :], xin[0][:, :]).then_inc(dram_set, 16)
            pool.dma_start(h2_dram[S:S + P, :], xin[0][:, :]).then_inc(dram_set, 16)
            pool.wait_ge(dram_set, 48)
            for s in range(2):
                pool.dma_start(lists[s * (S // 2):(s + 1) * (S // 2), :]
                               .rearrange("(p r) two -> p r two", p=P), pay[s][:, :, :]
                               ).then_inc(dram_set, 16)
            x_tile(0, 0, True)
            for i in range(TT):
                x_norm(i, i % 2, i)
            pool.wait_ge(dram_set, SETS)

            def prep(c):
                for i in range(TT):
                    x_norm((c + 1) * TT + i, i % 2, i)

            prep(0)
            with pool.Fori(0, NCH - 1) as b:
                c, n = b + 1, b * TT
                y_norm(n, 0)
                y_norm(n + 1, 1)
                y_norm(n + 2, 2)
                scatter(n, 0)
                y_norm(n + 3, 3)
                scatter(n + 1, 1)
                scatter(n + 2, 2)
                x_norm((c + 1) * TT, 0, 0)
                scatter(n + 3, 3)
                for i in range(1, TT):
                    x_norm((c + 1) * TT + i, i % 2, i)
            n = (NCH - 1) * TT
            for q in range(TT):
                y_norm(n + q, q)
                scatter(n + q, q)
            for s in range(2):
                pool.wait_ge(list_out[s], 16 * TOPK * NT // 2)
            pool.wait_ge(x_in[0], 16 * ((NCH + 1) * TT // 2 + 1))

        @block.tensor
        def _(pe):
            def three(out_, sh, sl, vh, vl, first, last):
                nc.tensor.matmul(out_, sl, vh, start=first, stop=False)
                nc.tensor.matmul(out_, sh, vl, start=False, stop=False)
                return nc.tensor.matmul(out_, sh, vh, start=False, stop=last)

            def unit(u, k, out_):
                pe.wait_ge(unit_ready, u + 1)
                s = k % 2
                for kd in range(KD):
                    last = three(out_, uh[s][:, kd, :], ul[s][:, kd, :], hh[:, kd, :], hl[:, kd, :],
                                 kd == 0, kd == KD - 1)
                last.then_inc(unit_done, 1)

            def group(c, g):
                pe.wait_ge(pooled_split, c * G + g + 1)
                wait(pe, a_split, c * G + g)
                if g == 0:
                    pe.wait_ge(branches_read, c * MT + 1)
                three(ps_a[:, :], wgh[:, g, :], wgl[:, g, :], ph[:, :], pl[:, :], True, True
                      ).then_inc(mixed_done, 1)

            def turn_x(n, s):
                pe.wait_ge(x_normed, n + 1)
                wait(pe, x_split, n)
                for kd in range(KD):
                    last = nc.tensor.transpose(ps_t8[:, kd, :], xin[s][:, kd * P:(kd + 1) * P],
                                               ident[:, :])
                last.then_inc(x_turned, 1)

            def turn_y(n, q):
                pe.wait_ge(y_normed, n + 1)
                wait(pe, y_copied, n)
                for kd in range(KD):
                    last = nc.tensor.transpose(
                        banks[kd // 4][:, kd % 4 * P:(kd % 4 + 1) * P],
                        h2[q % 2][:, kd * P:(kd + 1) * P], ident[:, :])
                last.then_inc(y_turned, 1)

            def router(n):
                pe.wait_ge(y_copied, n + 1)
                wait(pe, scored, n)
                for kd in range(KD):
                    last = nc.tensor.matmul(banks[2][:, 0:NE], h2t[:, kd, :], wr[:, kd, :],
                                            start=kd == 0, stop=kd == KD - 1)
                last.then_inc(logits_done, 1)

            def count(n):
                pe.wait_ge(masked, n + 1)
                wait(pe, dest_ready, n)
                nc.tensor.matmul(banks[3][:, 0:NE], tri[:, :], mask[:, :], start=True, stop=True)
                nc.tensor.matmul(banks[3][:, NE:2 * NE], ones[:, :], mask[:, :], start=True, stop=True)
                nc.tensor.matmul(banks[3][0:NE, 2 * NE:2 * NE + 1], mask[:, :], ones[:, 0:1],
                                 start=True, stop=True).then_inc(ranked, 1)

            def front(c, tiles, before=None):
                u = c * UNITS
                n = before * TT if tiles else None
                pe.wait_ge(x_split, (c + 1) * TT)
                for g in range(G):
                    if g >= 2:
                        pe.wait_ge(u_copied, c * G + g - 1)
                    unit(u + g, g, proj[g % 2])
                    if g >= 1:
                        group(c, g - 1)
                if tiles:
                    pe.wait_ge(x2_added, c * 8 + 4)
                for q in range(G):
                    k = CONV0 + 3 * q
                    b = q % 2
                    if q == 0:
                        pe.wait_ge(u_copied, c * G + 3)
                    else:
                        pe.wait_ge(cv_done, c * G + q)
                    unit(u + k, k, proj[b])
                    if tiles:
                        turn_y(n + q, q)
                    if q == 0:
                        pe.wait_ge(u_copied, c * G + 4)
                    else:
                        pe.wait_ge(b_split, c * G + q)
                    unit(u + k + 1, k + 1, proj[1 - b])
                    if tiles and q >= 1:
                        count(n + q - 1)
                    pe.wait_ge(c_copied, c * G + q + 1)
                    unit(u + k + 2, k + 2, proj[b])
                    if tiles:
                        router(n + q)
                group(c, G - 1)
                pe.wait_ge(cv_done, c * G + G)
                pe.wait_ge(b_split, c * G + G)
                pe.wait_ge(a_split, c * G + G)
                carry(pe, marks)
                with pe.Fori(0, MT // 2) as i:
                    for d in range(2):
                        k = MERGE0 + 3 * d
                        m = i * 2 + d
                        uu = i * 6 + (u + k)
                        pe.wait_ge(gate_a, m + (c * MT + 1))
                        unit(uu, k, proj[0])
                        pe.wait_ge(gate_b, m + (c * MT + 1))
                        unit(uu + 1, k + 1, proj[1])
                        pe.wait_ge(unit_ready, uu + 3)
                        pe.wait_ge(branches_read, m + (c * MT + 1))
                        s = (k + 2) % 2
                        for dst, vh, vl, k0 in ((ps_a, ah, al, 0), (ps_b, bh, bl, G)):
                            for g in range(G):
                                last = three(dst[:, :], uh[s][:, k0 + g, :], ul[s][:, k0 + g, :],
                                             vh[:, g, :], vl[:, g, :], g == 0, g == G - 1)
                        last.then_inc(unit_done, 1)
                if tiles:
                    count(n + TT - 1)

            def back(c):
                u = c * UNITS + BACK0
                wait(pe, dest_ready, c * TT)
                pe.wait_ge(gate_a, c * MT + MT + 1)
                pe.wait_ge(gate_b, c * MT + MT + 1)
                pe.wait_ge(merged, c * MT + MT)
                carry(pe, marks)
                with pe.Fori(0, 2) as h:
                    for v in range(4):
                        s = v % 2
                        pe.wait_ge(unit_ready, h * 4 + (u + v + 1))
                        vh = uh[s][:, :, :].rearrange("p (a b) n -> p a (b n)", a=2)
                        vl = ul[s][:, :, :].rearrange("p (a b) n -> p a (b n)", a=2)
                        for i in range(TT):
                            if v == 0:
                                pe.wait_ge(x2_added, h * 4 + (c * 8 + i + 1))
                            for kk in range(2):
                                kd = 2 * v + kk
                                tok = slice(i * P, (i + 1) * P)
                                last = three(banks[i][:, :], mh[:, kd, tok], ml[:, kd, tok],
                                             vh[:, kk, :], vl[:, kk, :], kd == 0, kd == KD - 1)
                            if v == 3 and i < TT - 1:
                                last.then_inc(wo_done, 1)
                        last.then_inc(unit_done, 1)
                        if v % 2 == 1:
                            turn_x(h * 2 + ((c + 1) * TT + v // 2), v // 2)

            def tiles_alone(c):
                n = c * TT
                pe.wait_ge(x2_added, (c + 1) * 8 + 4)
                for q in range(TT):
                    turn_y(n + q, q)
                    router(n + q)
                    count(n + q)

            pe.wait_ge(const_in, NCONST)
            for i in range(TT):
                turn_x(i, i % 2)
            pe.wait_ge(grp_split, 1)
            front(0, False)
            back(0)
            with pe.Fori(0, NCH - 1) as b:
                front(b + 1, True, b)
                back(b + 1)
            tiles_alone(NCH - 1)
            pe.wait_ge(tab_a, 1)
            nc.tensor.matmul(banks[0][0:NE, 0:1], over[:, 0:NE], nblk[:, :], start=True, stop=True).then_inc(tab_b, 1)
            pe.wait_ge(tab_c, 1)
            nc.tensor.matmul(banks[1][0:1, 0:NB], ones[0:NE, 0:1], over[:, :], start=True, stop=True)
            nc.tensor.matmul(banks[2][0:1, 0:NB], nblk[:, 0:1], over[:, :], start=True, stop=True
                             ).then_inc(tab_d, 1)

        @block.scalar
        def _(act):
            def copy(dst, src, **kw):
                return nc.scalar.activation(dst, src, ACT.Copy, **kw)

            def split_hi(u, k):
                s = k % 2
                if isinstance(u, int):
                    act.wait_ge(raw_in[s], 16 * (u // 2 + 1))
                wait(act, unit_done, u - 1)
                copy(uh[s][:, :, :].rearrange("p k n -> p (k n)"), raw[:, s, :]).then_inc(unit_hi, 1)

            def split_next(base, k):
                u = base + k + 2
                if not isinstance(u, int):
                    act.wait_ge(raw_in[k % 2], 8 * base + 16 * (k // 2 + 2))
                split_hi(u, k)

            def x_square(n, s, col):
                act.drain()
                act.wait_ge(x_in[s], 16 * (n // 2 + 1))
                nc.scalar.activation(junk[:, :], xin[s][:, :], ACT.Square, scale=float(D) ** -0.5,
                                     accum_out=mean[:, col:col + 1]).then_inc(x_mean, 1)

            def x_high(n, tok):
                act.wait_ge(x_turned, n + 1)
                copy(hh[:, :, tok], ps_t8[:, :, :]).then_inc(x_hi, 1)

            def y_square(n, q):
                act.drain()
                act.wait_ge(x2_added, n * 2 + (12 - 2 * q))
                nc.scalar.activation(junk[:, :], x2[:, q, :], ACT.Square, scale=float(D) ** -0.5,
                                     accum_out=mean[:, TT + q:TT + q + 1]).then_inc(y_mean, 1)

            def y_copy(n, q):
                act.wait_ge(y_turned, n + 1)
                wait(act, logits_done, n)
                for b in range(2):
                    last = copy(h2t[:, 4 * b:4 * b + 4, :].rearrange("p k t -> p (k t)"), banks[b][:, :])
                last.then_inc(y_copied, 1)
                act.dma_start(h2_tiles[n] if isinstance(n, int) else
                              h2_tiles[ds1(n)].rearrange("a p d -> p (a d)"),
                              h2[q % 2][:, :]).then_inc(h2_out[q % 2], 16)

            def score(n):
                act.wait_ge(logits_done, n + 1)
                wait(act, masked, n)
                nc.scalar.activation(sc[:, :], banks[2][:, 0:NE], ACT.Sigmoid).then_inc(scored, 1)

            def a_high(c, g):
                act.wait_ge(mixed_done, c * G + g + 1)
                copy(ah[:, g, :], ps_a[:, :], scale=pscale[:, g:g + 1]).then_inc(a_hi, 1)

            def front(c, tiles, before=None):
                base = c * UNITS
                n = before * TT if tiles else None
                for g in range(G):
                    act.wait_ge(unit_done, base + g + 1)
                    wait(act, pooled_split, c * G + g)
                    copy(ubuf[:, 0:HALO], uhalo[:, g, :])
                    copy(ubuf[:, HALO:], proj[g % 2])
                    act.drain()
                    copy(uhalo[:, g, :], proj[g % 2][:, T - HALO:T]).then_inc(u_copied, 1)
                    split_next(base, g)
                    if g >= 1:
                        a_high(c, g - 1)
                if tiles:
                    y_square(n, 0)
                for q in range(G):
                    k = CONV0 + 3 * q
                    act.wait_ge(unit_done, base + k + 1)
                    wait(act, cv_done, c * G + q)
                    copy(csb[:, :], proj[q % 2]).then_inc(c_copied, 1)
                    split_next(base, k)
                    split_next(base, k + 1)
                    if tiles:
                        y_copy(n + q, q)
                    split_next(base, k + 2)
                    if tiles:
                        if q < TT - 1:
                            y_square(n + q + 1, q + 1)
                        score(n + q)
                a_high(c, G - 1)
                with act.Fori(0, MT // 2) as i:
                    for d in range(2):
                        k = MERGE0 + 3 * d
                        m = i * 2 + d
                        ub = i * 6 + base
                        for j, (sig, bank, sm) in enumerate(((siga, 0, gate_a), (sigb, 1, gate_b))):
                            act.wait_ge(unit_done, ub + (k + j + 1))
                            act.wait_ge(branches_read, m + (c * MT + 1))
                            nc.scalar.activation(sig[:, :], proj[bank], ACT.Sigmoid,
                                                 bias=bg[:, bass.ds(m + j * MT, 1)]).then_inc(sm, 1)
                            act.wait_ge(raw_in[(k + j) % 2], 8 * ub + 16 * ((k + j) // 2 + 2))
                            split_hi(ub + (k + j + 2), k + j)
                        act.wait_ge(raw_in[k % 2], 8 * ub + 16 * ((k + 2) // 2 + 2))
                        split_hi(ub + (k + 4), k + 2)

            def back(c):
                base = c * UNITS + BACK0
                with act.Fori(0, 2) as h:
                    for v in range(4):
                        ub = h * 4 + base
                        act.wait_ge(raw_in[v % 2], 8 * ub + 16 * (v // 2 + 2))
                        split_hi(ub + (v + 2), v)
                        n = h * 2 + ((c + 1) * TT + v // 2)
                        s = v // 2
                        if v % 2 == 0:
                            act.drain()
                            act.wait_ge(x_in[s], h * 16 + ((c + 1) * (8 * TT) + 16))
                            nc.scalar.activation(
                                junk[:, :], xin[s][:, :], ACT.Square, scale=float(D) ** -0.5,
                                accum_out=mean[:, bass.ds(h * 2 + s, 1)]).then_inc(x_mean, 1)
                        else:
                            act.wait_ge(x_turned, n + 1)
                            copy(hh[:, :, bass.ds(h * (2 * P) + s * P, P)], ps_t8[:, :, :]
                                 ).then_inc(x_hi, 1)

            split_hi(0, 0)
            split_hi(1, 1)
            for i in range(TT):
                x_square(i, i % 2, i)
                x_high(i, slice(i * P, (i + 1) * P))
            act.wait_ge(const_in, NCONST)
            copy(wgh[:, :, :], wg[:, :, :]).then_inc(grp_hi, 1)
            act.sem_inc(gate_a, 1)
            act.sem_inc(gate_b, 1)
            act.wait_ge(halo_zero, 1)
            front(0, False)
            back(0)
            with act.Fori(0, NCH - 1) as b:
                front(b + 1, True, b)
                back(b + 1)
            n = (NCH - 1) * TT
            for q in range(TT):
                y_square(n + q, q)
                y_copy(n + q, q)
                score(n + q)
            for s in range(2):
                act.wait_ge(h2_out[s], 16 * NT // 2)

        @block.vector
        def _(dve):
            V = nc.vector

            def split_lo(u, k):
                s = k % 2
                dve.wait_ge(unit_hi, u + 1)
                V.tensor_tensor(ul[s][:, :, :].rearrange("p k n -> p (k n)"), raw[:, s, :],
                                uh[s][:, :, :].rearrange("p k n -> p (k n)"), ALU.subtract
                                ).then_inc(unit_ready, 1)

            def x_scale(n, s, col):
                dve.wait_ge(x_rstd, n + 1)
                V.scalar_tensor_tensor(out=xin[s][:, :], in0=xin[s][:, :], scalar=col,
                                       in1=gmix[:, :], op0=ALU.mult, op1=ALU.mult
                                       ).then_inc(x_normed, 1)

            def x_low(n, tok):
                dve.wait_ge(x_hi, n + 1)
                V.tensor_tensor(hl[:, :, tok], ps_t8[:, :, :], hh[:, :, tok], ALU.subtract
                                ).then_inc(x_split, 1)

            def y_scale(chunk, q):
                n = chunk * TT + q
                dve.wait_ge(y_rstd, n + 1)
                wait(dve, h2_out[q % 2], chunk * (8 * TT) + 16 * (q // 2))
                V.scalar_tensor_tensor(out=h2[q % 2][:, :], in0=x2[:, q, :],
                                       scalar=rstd[:, TT + q:TT + q + 1], in1=gffn[:, :],
                                       op0=ALU.mult, op1=ALU.mult).then_inc(y_normed, 1)

            def pool_group(c, g):
                w = WINDOWS[g]
                dve.wait_ge(u_copied, c * G + g + 1)
                src, width, turn = ubuf, 1, 0
                while width < w:
                    lo = 2 * width - 1 + (HALO - w)
                    V.tensor_tensor(win[turn][:, lo:], src[:, lo:], src[:, lo - width:HALO + T - width],
                                    ALU.add)
                    dve.drain()
                    src, width, turn = win[turn], 2 * width, 1 - turn
                V.scalar_tensor_tensor(out=pooled[:, :], in0=src[:, HALO:], scalar=1.0 / w,
                                       in1=ubuf[:, HALO:], op0=ALU.mult, op1=ALU.subtract)
                if isinstance(c, int):
                    dve.drain()
                    V.tensor_tensor(src[:, HALO:2 * HALO], src[:, HALO:2 * HALO], icnt[:, g, :], ALU.mult)
                    dve.drain()
                    V.tensor_tensor(pooled[:, 0:HALO], src[:, HALO:2 * HALO], ubuf[:, HALO:2 * HALO],
                                    ALU.subtract)
                dve.drain()
                wait(dve, mixed_done, c * G + g)
                V.tensor_copy(ph[:, :], pooled[:, :])
                dve.drain()
                V.tensor_tensor(pl[:, :], pooled[:, :], ph[:, :], ALU.subtract).then_inc(pooled_split, 1)
                dve.drain()

            def a_low(c, g):
                dve.wait_ge(a_hi, c * G + g + 1)
                V.scalar_tensor_tensor(out=al[:, g, :], in0=ps_a[:, :], scalar=pscale[:, g:g + 1],
                                       in1=ah[:, g, :], op0=ALU.mult, op1=ALU.subtract
                                       ).then_inc(a_split, 1)

            def conv_cv(c, q):
                dve.wait_ge(unit_done, c * UNITS + CONV0 + 3 * q + 2)
                dve.wait_ge(c_copied, c * G + q + 1)
                V.tensor_copy(cv[:, 0:2], cvhalo[:, q, :])
                V.tensor_tensor(cv[:, 2:], csb[:, :], proj[1 - q % 2], ALU.mult).then_inc(cv_done, 1)
                dve.drain()
                V.tensor_copy(cvhalo[:, q, :], cv[:, T:T + 2])
                V.tensor_scalar(tap, cv[:, 0:T], cw[:, q, 0:1], None, ALU.mult)
                for j in (1, 2):
                    dve.drain()
                    V.scalar_tensor_tensor(out=tap, in0=cv[:, j:j + T], scalar=cw[:, q, j:j + 1],
                                           in1=tap, op0=ALU.mult, op1=ALU.add)
                dve.drain()

            def conv_b(c, q):
                dve.wait_ge(unit_done, c * UNITS + CONV0 + 3 * q + 3)
                V.tensor_tensor(bcv, proj[q % 2], tap, ALU.mult)
                dve.drain()
                V.tensor_copy(bh[:, q, :], bcv)
                dve.drain()
                V.tensor_tensor(bl[:, q, :], bcv, bh[:, q, :], ALU.subtract).then_inc(b_split, 1)
                dve.drain()

            def choose(chunk, q):
                n = chunk * TT + q
                dve.wait_ge(scored, n + 1)
                V.tensor_tensor(biased[:, :], sc[:, :], rbias[:, :], ALU.add)
                dve.drain()
                V.max(top[:, :], biased[:, :])
                dve.drain()
                V.max_index(idx[:, :], top[:, :], biased[:, :])
                dve.drain()
                V.tensor_copy(idxf[:, :], idx[:, :])
                dve.drain()
                V.tensor_tensor(hot[:, :, :], iota_e[:, None, :].to_broadcast([P, TOPK, NE]),
                                idxf[:, :, None].to_broadcast([P, TOPK, NE]), ALU.is_equal)
                dve.drain()
                wait(dve, ranked, n)
                V.tensor_tensor(hotx, hot[:, :, :], sc[:, None, :].to_broadcast([P, TOPK, NE]), ALU.mult)
                V.tensor_reduce(mask[:, :], hot[:, :, :].rearrange("p k e -> p e k"), AX.X, ALU.add
                                ).then_inc(masked, 1)
                dve.drain()
                V.tensor_reduce(w8[:, :], hotx, AX.X, ALU.add)
                dve.drain()
                V.tensor_reduce(den[:, :], w8[:, :], AX.X, ALU.add)
                dve.drain()
                V.reciprocal(den[:, :], den[:, :])
                dve.drain()
                wait(dve, list_out[q % 2], (chunk * (8 * TT) + 16 * (q // 2)) * TOPK)
                V.tensor_copy(pay[q % 2][:, :, 0], tokid[:, (slice(n, n + 1) if isinstance(n, int) else ds1(n))]
                              .to_broadcast([P, TOPK]))
                V.tensor_scalar(pay[q % 2][:, :, :].bitcast(F32)[:, :, 1], w8[:, :], den[:, 0:1], SCALE,
                                ALU.mult, ALU.mult)
                dve.drain()

            def place(n, q):
                dve.wait_ge(ranked, n + 1)
                V.tensor_tensor(rank[:, :], banks[3][:, 0:NE], taken[:, :], ALU.add)
                dve.drain()
                V.tensor_tensor(taken[:, :], taken[:, :], banks[3][:, NE:2 * NE], ALU.add)
                V.tensor_tensor(total[:, :], total[:, :], banks[3][0:NE, 2 * NE:2 * NE + 1], ALU.add)
                V.tensor_tensor(hotx, hot[:, :, :], rank[:, None, :].to_broadcast([P, TOPK, NE]), ALU.mult)
                dve.drain()
                V.tensor_reduce(r8[:, :], hotx, AX.X, ALU.add)
                dve.drain()
                V.scalar_tensor_tensor(out=dest[q % 2][:, :], in0=idxf[:, :], scalar=float(ROWS),
                                       in1=r8[:, :], op0=ALU.mult, op1=ALU.add).then_inc(dest_ready, 1)
                dve.drain()

            def front(c, tiles, before=None):
                base = c * UNITS
                n = before * TT if tiles else None
                for g in range(G):
                    split_lo(base + g + 2, g)
                    if g >= 1:
                        a_low(c, g - 1)
                    pool_group(c, g)
                if tiles:
                    y_scale(before, 0)
                for q in range(G):
                    k = CONV0 + 3 * q
                    split_lo(base + k + 2, k)
                    if tiles and q >= 1:
                        choose(before, q - 1)
                    split_lo(base + k + 3, k + 1)
                    conv_cv(c, q)
                    split_lo(base + k + 4, k + 2)
                    conv_b(c, q)
                    if tiles and q < TT - 1:
                        y_scale(before, q + 1)
                    if tiles and q >= 1:
                        place(n + q - 1, q - 1)
                a_low(c, G - 1)
                if tiles:
                    choose(before, TT - 1)
                with dve.Fori(0, MT // 2) as i:
                    for d in range(2):
                        k = MERGE0 + 3 * d
                        m = i * 2 + d
                        ub = i * 6 + base
                        split_lo(ub + (k + 2), k)
                        split_lo(ub + (k + 3), k + 1)
                        split_lo(ub + (k + 4), k + 2)
                        dve.wait_ge(gate_a, m + (c * MT + 2))
                        dve.wait_ge(gate_b, m + (c * MT + 2))
                        dve.wait_ge(unit_done, ub + (k + 3))
                        V.tensor_tensor(m1, siga[:, :], ps_a[:, :], ALU.mult)
                        V.tensor_tensor(m2, sigb[:, :], ps_b[:, :], ALU.mult).then_inc(branches_read, 1)
                        dve.drain()
                        V.tensor_tensor(m1, m1, m2, ALU.add)
                        dve.drain()
                        mm = mh[:, ds1(m), :].rearrange("p a t -> p (a t)")
                        V.tensor_copy(mm, m1)
                        dve.drain()
                        V.tensor_tensor(ml[:, ds1(m), :].rearrange("p a t -> p (a t)"), m1, mm,
                                        ALU.subtract).then_inc(merged, 1)
                        dve.drain()
                if tiles:
                    place(n + TT - 1, TT - 1)

            def back(c):
                base = c * UNITS + BACK0
                dve.wait_ge(res_in, (c + 1) * 16)
                carry(dve, marks)
                with dve.Fori(0, 2) as h:
                    for v in range(4):
                        ub = h * 4 + base
                        split_lo(ub + (v + 2), v)
                        n = h * 2 + ((c + 1) * TT + v // 2)
                        s = v // 2
                        if v % 2 == 0:
                            x_scale(n, s, rstd[:, bass.ds(h * 2 + s, 1)])
                        if v == 3:
                            for i in range(TT):
                                if i < TT - 1:
                                    dve.wait_ge(wo_done, h * 3 + (c * 6 + i + 1))
                                else:
                                    dve.wait_ge(unit_done, ub + 4)
                                part = x2[:, i, bass.ds(h * (D // 2), D // 2)]
                                V.tensor_tensor(part, part, banks[i][:, :], ALU.add
                                                ).then_inc(x2_added, 1)
                        if v % 2 == 1:
                            x_low(n, bass.ds(h * (2 * P) + s * P, P))

            V.memset(uhalo[:, :, :], 0.0)
            V.memset(cvhalo[:, :, :], 0.0)
            V.memset(taken[:, :], float(ROWS))
            V.memset(total[:, :], 0.0).then_inc(halo_zero, 1)
            dve.wait_ge(blank_made, 1)
            bids = blank[:, :, 0]
            V.tensor_scalar(bids, bids, P - 1, None, ALU.bitwise_and)
            for s in range(2):
                for r in range(TOPK):
                    V.tensor_scalar(pay[s][:, r:r + 1, 0], tokid[:, 0:1], TOPK, s * (S // 2) + r,
                                    ALU.mult, ALU.add)
                V.memset(pay[s][:, :, :].bitcast(F32)[:, :, 1], 1.0)
            dve.drain()
            V.tensor_scalar(bids, bids, S, None, ALU.add).then_inc(blank_made, 1)
            split_lo(0, 0)
            split_lo(1, 1)
            dve.wait_ge(const_in, NCONST)
            for i in range(TT):
                x_scale(i, i % 2, rstd[:, i:i + 1])
                x_low(i, slice(i * P, (i + 1) * P))
            dve.wait_ge(grp_hi, 1)
            V.tensor_tensor(wgl[:, :, :], wg[:, :, :], wgh[:, :, :], ALU.subtract).then_inc(grp_split, 1)
            dve.sem_inc(branches_read, 1)
            dve.sem_inc(x2_added, TT)
            dve.wait_ge(dram_set, SETS)
            front(0, False)
            back(0)
            with dve.Fori(0, NCH - 1) as b:
                front(b + 1, True, b)
                back(b + 1)
            n = (NCH - 1) * TT
            for q in range(TT):
                y_scale(NCH - 1, q)
                choose(NCH - 1, q)
                place(n + q, q)

            V.tensor_scalar(total[:, :], total[:, :], float(P - 1), None, ALU.add)
            dve.drain()
            V.tensor_copy(nblk_i[:, :], total[:, :])
            dve.drain()
            V.tensor_scalar(nblk_i[:, :], nblk_i[:, :], 7, None, ALU.logical_shift_right)
            V.tensor_tensor(over[:, 0:NE], tri[0:NE, 0:NE], ident[0:NE, 0:NE], ALU.add)
            dve.drain()
            V.tensor_scalar(nblk[:, :], nblk_i[:, :], 1, None, ALU.max).then_inc(tab_a, 1)
            dve.wait_ge(tab_b, 1)
            V.tensor_scalar(bend[:, :], banks[0][0:NE, 0:1], float(SHARED_BLOCKS), None, ALU.add)
            dve.drain()
            V.tensor_scalar(over[:, :], iota_j[:, :], bend[:, 0:1], None, ALU.is_ge).then_inc(tab_c, 1)
            dve.wait_ge(tab_d, 1)
            V.tensor_tensor(eid_f[:, :], banks[1][0:1, 0:NB], from16[:, :], ALU.add)
            V.scalar_tensor_tensor(out=bst_f[:, :], in0=from16[:, :], scalar=float(SHARED_BLOCKS),
                                   in1=banks[2][0:1, 0:NB], op0=ALU.mult, op1=ALU.add)
            dve.drain()
            V.tensor_scalar(table[:, 0:NB], eid_f[:, :], float(NE), None, ALU.min)
            V.scalar_tensor_tensor(out=row_f[:, :], in0=eid_f[:, :], scalar=float(ROWS // P),
                                   in1=iota_j[0:1, :], op0=ALU.mult, op1=ALU.add)
            V.tensor_copy(table[:, 2 * NB:2 * NB + 1], bst_f[:, NB - 1:NB])
            dve.drain()
            V.tensor_tensor(row_f[:, :], row_f[:, :], bst_f[:, :], ALU.subtract)
            V.tensor_scalar(table[:, 2 * NB + 1:2 * NB + 2], table[:, 2 * NB:2 * NB + 1], 1, None,
                            ALU.logical_shift_right)
            dve.drain()
            V.tensor_copy(table[:, NB:2 * NB], row_f[:, :])
            dve.drain()


def mixture(nc, sem, marks, table, acc, h2_dram, lists, experts, ident_in):
    list_blocks = lists.rearrange("(b p) two -> b p two", p=P)
    KP = KD // 2

    with ExitStack() as ctx:
        def sb(name, shape, dt=F32):
            return ctx.enter_context(nc.sbuf_tensor(name, shape, dt))

        ident = sb("eye2", [P, P])
        raw = sb("expert_raw", [P, PIECES, D])
        wh = sb("expert_hi", [P, 2 * PIECES, D], F32R)
        wl = sb("expert_lo", [P, 2 * PIECES, D], F32R)
        gidx = [sb(f"gidx{s}", [P, 2], I32) for s in range(2)]
        sidx = [sb(f"sidx{s}", [P, 2], I32) for s in range(2)]
        xs = [sb(f"xs{s}", [P, D]) for s in range(2)]
        xh = [sb(f"xh{s}", [P, KD, P], F32R) for s in range(2)]
        xl = [sb(f"xl{s}", [P, KD, P], F32R) for s in range(2)]
        sg = sb("sg", [P, H])
        hid = sb("hid", [P, H])
        hth = [sb(f"hth{s}", [P, 2, P], F32R) for s in range(2)]
        htl = [sb(f"htl{s}", [P, 2, P], F32R) for s in range(2)]
        y = [sb(f"y{s}", [P, D]) for s in range(2)]

        ps_x = ctx.enter_context(nc.psum_tensor("ps_x", [P, KD, P], F32))
        ps_gu = [ctx.enter_context(nc.psum_tensor(f"ps_gu{s}", [P, 512], F32)) for s in range(2)]
        ps_h = ctx.enter_context(nc.psum_tensor("ps_h", [P, 2, P], F32))
        ps_y = ctx.enter_context(nc.psum_tensor("ps_y", [P, D], F32))

        ident_ready = sem("ident_ready")
        piece_in = [sem(f"piece_in{p}") for p in range(PIECES)]
        piece_hi = sem("piece_hi")
        piece_ready = sem("piece_ready")
        gidx_in = [sem(f"gidx_in{s}") for s in range(2)]
        sidx_in = [sem(f"sidx_in{s}") for s in range(2)]
        xs_in = [sem(f"xs_in{s}") for s in range(2)]
        xs_turned = sem("xs_turned")
        xs_hi = sem("xs_hi")
        xs_split = sem("xs_split")
        gu_done = sem("gu_done")
        gate_sig = sem("gate_sig")
        hid_ready = sem("hid_ready")
        hid_turned = sem("hid_turned")
        hid_hi = sem("hid_hi")
        hid_split = sem("hid_split")
        down_done = sem("down_done")
        y_ready = sem("y_ready")
        y_out = [sem(f"y_out{s}") for s in range(2)]

        block = ctx.enter_context(nc.Block())

        def pairs(eng):
            return eng.value_load(table[0:1, 2 * NB + 1:2 * NB + 2], min_val=(SHARED_BLOCKS + NE) // 2,
                                  max_val=NBMAX // 2)

        def expert_of(eng, j):
            at = slice(j, j + 1) if isinstance(j, int) else ds1(j)
            return eng.value_load(table[0:1, at], min_val=0, max_val=NE)

        @block.sync
        def _(sp):
            def list_rows(j):
                at = slice(NB + j, NB + j + 1) if isinstance(j, int) else bass.ds(j + NB, 1)
                row = sp.value_load(table[0:1, at], min_val=0, max_val=(LISTS * ROWS // P - 1))
                return list_blocks[ds1(row)].rearrange("a p two -> p (a two)")

            def gather_list(j, s):
                sp.dma_start(gidx[s][:, :], list_rows(j)).then_inc(gidx_in[s], 16)

            def scatter_list(j, s):
                sp.dma_start(sidx[s][:, :], list_rows(j)).then_inc(sidx_in[s], 16)

            def load_expert(e, i):
                for p in range(PIECES):
                    wait(sp, piece_ready, (e - 1) * PIECES + p + 1)
                    src = experts[e] if isinstance(e, int) else experts[ds1(e % (NE + 1))].rearrange(
                        "a p f d -> p (a f) d")
                    sp.dma_start(raw[:, p, :], src[:, p, :]).then_inc(piece_in[p], 16)

            load_expert(0, 0)
            sp.dma_start(ident[:, :], ident_in).then_inc(ident_ready, 16)
            for j in range(3):
                if j == 2:
                    sp.wait_ge(xs_in[0], 16)
                gather_list(j, j % 2)
            scatter_list(0, 0)
            load_expert(1, 0)
            sp.wait_ge(xs_in[1], 16)
            gather_list(3, 1)
            load_expert(2, 0)
            n = pairs(sp)
            with sp.Fori(0, n) as i:
                for d in (1, 2):
                    j = i * 2 + d
                    s = d % 2
                    if d == 1:
                        sp.wait_ge(y_out[1], i * 16 + 16)
                    else:
                        sp.wait_ge(y_out[0], i * 16 + 32)
                    scatter_list(j, s)
                    sp.wait_ge(xs_in[1 - s], i * 16 + 32)
                    gather_list(j + 3, 1 - s)
                    e = expert_of(sp, j)
                    before = expert_of(sp, j - 1)
                    with sp.If(e > before):
                        load_expert(e + 2, i)
            for p in range(PIECES):
                sp.wait_ge(piece_in[p], 16 * (NE + 3))

        @block.gpsimd
        def _(pool):
            def gather(s):
                nc.gpsimd.indirect_dma_start(
                    xs[s][:, :], None, h2_dram,
                    bass.IndirectOffsetOnAxis(ap=gidx[s][:, 0:1], axis=0)).then_inc(xs_in[s], 16)

            def scatter(s):
                nc.gpsimd.indirect_dma_start(
                    acc, bass.IndirectOffsetOnAxis(ap=sidx[s][:, 0:1], axis=0), y[s][:, :], None,
                    compute_op=ALU.add).then_inc(y_out[s], 16)

            for s in range(2):
                pool.dma_start(y[s][:, :], h2_dram[S:S + P, :]).then_inc(y_out[s], 16)
            for j in range(3):
                pool.wait_ge(gidx_in[j % 2], 16 * (j // 2 + 1))
                if j == 2:
                    pool.wait_ge(xs_turned, 1)
                gather(j % 2)
            n = pairs(pool)
            with pool.Fori(0, n) as i:
                for d in (1, 2):
                    s = d % 2
                    pool.wait_ge(gidx_in[s], i * 16 + (32 if d == 1 else 48))
                    pool.wait_ge(xs_turned, i * 2 + (d + 1))
                    carry(pool, marks)
                    gather(s)
                    pool.wait_ge(y_ready, i * 2 + d)
                    pool.wait_ge(sidx_in[1 - s], i * 16 + 16)
                    pool.wait_ge(y_out[s], i * 16 + 16 * d)
                    carry(pool, marks)
                    scatter(1 - s)
            pool.wait_ge(y_ready, n * 2 + 1)
            pool.wait_ge(sidx_in[0], n * 16 + 16)
            pool.wait_ge(y_out[1], n * 16 + 16)
            carry(pool, marks)
            scatter(0)
            pool.wait_ge(y_out[0], n * 16 + 32)
            pool.wait_ge(xs_in[1], n * 16 + 16)
            pool.wait_ge(xs_in[0], n * 16 + 32)
            pool.wait_ge(gidx_in[1], n * 16 + 32)
            carry(pool, marks)

        @block.tensor
        def _(pe):
            def three(out_, sh, sl, vh, vl, first, last):
                nc.tensor.matmul(out_, sl, vh, start=first, stop=False)
                nc.tensor.matmul(out_, sh, vl, start=False, stop=False)
                return nc.tensor.matmul(out_, sh, vh, start=False, stop=last)

            def turn(j, s, filled):
                pe.wait_ge(xs_in[s], filled)
                wait(pe, xs_split, j)
                for kd in range(KD):
                    last = nc.tensor.transpose(ps_x[:, kd, :], xs[s][:, kd * P:(kd + 1) * P],
                                               ident[:, :])
                last.then_inc(xs_turned, 1)

            def piece(slot, p):
                if isinstance(slot, int):
                    return wh[:, slot * PIECES + p, :], wl[:, slot * PIECES + p, :]
                return tuple(w[:, ds1(slot * PIECES + p), :].rearrange("q a f -> q (a f)")
                             for w in (wh, wl))

            def gate_up(j, s, e):
                pe.wait_ge(xs_split, j + 1)
                wait(pe, hid_ready, j - 1)
                pe.wait_ge(piece_ready, e * PIECES + KP)
                slot = e % 2
                for p in range(KP):
                    ph_, pl_ = piece(slot, p)
                    for b in range(2):
                        kd = 2 * p + b
                        last = three(ps_gu[s][:, :], xh[s][:, kd, :], xl[s][:, kd, :],
                                     ph_[:, b * 512:(b + 1) * 512], pl_[:, b * 512:(b + 1) * 512],
                                     kd == 0, kd == KD - 1)
                last.then_inc(gu_done, 1)

            def down(j, s, e):
                pe.wait_ge(hid_split, j + 1)
                wait(pe, y_ready, j)
                pe.wait_ge(piece_ready, e * PIECES + PIECES)
                slot = e % 2
                for kk in range(2):
                    ph_, pl_ = piece(slot, KP + kk)
                    for b in range(2):
                        last = three(ps_y[:, b * 512:(b + 1) * 512], hth[s][:, kk, :],
                                     htl[s][:, kk, :], ph_[:, b * 512:(b + 1) * 512],
                                     pl_[:, b * 512:(b + 1) * 512], kk == 0, kk == 1)
                last.then_inc(down_done, 1)

            def turn_hidden(j):
                pe.wait_ge(hid_ready, j + 1)
                wait(pe, hid_split, j)
                for kk in range(2):
                    last = nc.tensor.transpose(ps_h[:, kk, :], hid[:, kk * P:(kk + 1) * P], ident[:, :])
                last.then_inc(hid_turned, 1)

            pe.wait_ge(ident_ready, 16)
            n = pairs(pe)
            turn(0, 0, 16)
            gate_up(0, 0, 0)
            turn(1, 1, 16)
            turn_hidden(0)
            with pe.Fori(0, n) as i:
                for d in (1, 2):
                    j = i * 2 + d
                    s = d % 2
                    e = expert_of(pe, j)
                    before = expert_of(pe, j - 1)
                    gate_up(j, s, e)
                    turn(j + 1, 1 - s, i * 16 + 32)
                    down(j - 1, 1 - s, before)
                    turn_hidden(j)
            down(n * 2, 0, expert_of(pe, n * 2))

        @block.scalar
        def _(act):
            def copy(dst, src, **kw):
                return nc.scalar.activation(dst, src, ACT.Copy, **kw)

            def pieces_hi(e, lo, hi, j):
                wait(act, gu_done if lo < KP else down_done, j)
                if hi > KP:
                    wait(act, down_done, j)
                for p in range(lo, hi):
                    act.wait_ge(piece_in[p], (e + 1) * 16)
                    at = (e % 2) * PIECES + p
                    dst = wh[:, at, :] if isinstance(at, int) else wh[:, ds1(at), :].rearrange(
                        "q a f -> q (a f)")
                    copy(dst, raw[:, p, :]).then_inc(piece_hi, 1)

            def x_high(j, s):
                act.wait_ge(xs_turned, j + 1)
                wait(act, gu_done, j - 1)
                copy(xh[s][:, :, :], ps_x[:, :, :]).then_inc(xs_hi, 1)

            def gate_sigmoid(j, s):
                act.wait_ge(gu_done, j + 1)
                wait(act, hid_ready, j)
                nc.scalar.activation(sg[:, :], ps_gu[s][:, 0:H], ACT.Sigmoid).then_inc(gate_sig, 1)

            def hidden_high(j, s):
                act.wait_ge(hid_turned, j + 1)
                wait(act, down_done, j - 1)
                copy(hth[s][:, :, :], ps_h[:, :, :]).then_inc(hid_hi, 1)

            def output(j, s, listed, added):
                act.wait_ge(down_done, j + 1)
                act.wait_ge(sidx_in[s], listed)
                wait(act, y_out[s], added)
                copy(y[s][:, :], ps_y[:, :], scale=sidx[s][:, :].bitcast(F32)[:, 1:2]
                     ).then_inc(y_ready, 1)

            pieces_hi(0, 0, PIECES, 0)
            x_high(0, 0)
            gate_sigmoid(0, 0)
            x_high(1, 1)
            pieces_hi(1, 0, PIECES, 0)
            hidden_high(0, 0)
            n = pairs(act)
            with act.Fori(0, n) as i:
                for d in (1, 2):
                    j = i * 2 + d
                    s = d % 2
                    e = expert_of(act, j)
                    before = expert_of(act, j - 1)
                    gate_sigmoid(j, s)
                    x_high(j + 1, 1 - s)
                    with act.If(e > before):
                        pieces_hi(e + 1, 0, KP, j)
                    output(j - 1, 1 - s, i * 16 + 16, i * 16 + 16)
                    hidden_high(j, s)
                    with act.If(e > before):
                        pieces_hi(e + 1, KP, PIECES, j)
            output(n * 2, 0, n * 16 + 16, n * 16 + 16)

        @block.vector
        def _(dve):
            V = nc.vector

            def pieces_lo(e, lo, hi):
                for p in range(lo, hi):
                    dve.wait_ge(piece_hi, e * PIECES + (p + 1))
                    at = (e % 2) * PIECES + p
                    h_, l_ = (w[:, at, :] if isinstance(at, int) else w[:, ds1(at), :].rearrange(
                        "q a f -> q (a f)") for w in (wh, wl))
                    V.tensor_tensor(l_, raw[:, p, :], h_, ALU.subtract).then_inc(piece_ready, 1)

            def x_low(j, s):
                dve.wait_ge(xs_hi, j + 1)
                V.tensor_tensor(xl[s][:, :, :], ps_x[:, :, :], xh[s][:, :, :], ALU.subtract
                                ).then_inc(xs_split, 1)

            def hidden(j, s):
                dve.wait_ge(gate_sig, j + 1)
                wait(dve, hid_turned, j)
                V.tensor_tensor(hid[:, :], ps_gu[s][:, 0:H], sg[:, :], ALU.mult)
                dve.drain()
                V.tensor_tensor(hid[:, :], hid[:, :], ps_gu[s][:, H:2 * H], ALU.mult
                                ).then_inc(hid_ready, 1)

            def hidden_low(j, s):
                dve.wait_ge(hid_hi, j + 1)
                V.tensor_tensor(htl[s][:, :, :], ps_h[:, :, :], hth[s][:, :, :], ALU.subtract
                                ).then_inc(hid_split, 1)

            pieces_lo(0, 0, PIECES)
            x_low(0, 0)
            hidden(0, 0)
            x_low(1, 1)
            pieces_lo(1, 0, PIECES)
            hidden_low(0, 0)
            n = pairs(dve)
            with dve.Fori(0, n) as i:
                for d in (1, 2):
                    j = i * 2 + d
                    s = d % 2
                    e = expert_of(dve, j)
                    before = expert_of(dve, j - 1)
                    hidden(j, s)
                    x_low(j + 1, 1 - s)
                    with dve.If(e > before):
                        pieces_lo(e + 1, 0, KP)
                    hidden_low(j, s)
                    with dve.If(e > before):
                        pieces_lo(e + 1, KP, PIECES)


def final_norm(nc, sem, marks, acc, g_final, out):
    a_tiles = acc[0:S, :].rearrange("(n p) d -> n p d", p=P)
    o_tiles = out.rearrange("(n p) d -> n p d", p=P)
    R = 4

    with ExitStack() as ctx:
        def sb(name, shape, dt=F32):
            return ctx.enter_context(nc.sbuf_tensor(name, shape, dt))

        gfin = sb("gfin", [P, D])
        a = [sb(f"a{s}", [P, D]) for s in range(R)]
        junk = sb("junk3", [P, D], BF16)
        mean = sb("mean3", [P, R])
        rstd = sb("rstd3", [P, R])
        minus_half = sb("minus_half3", [P, 1])
        g_in = sem("g_in")
        a_in = [sem(f"a_in{s}") for s in range(R)]
        a_mean = sem("a_mean")
        a_rstd = sem("a_rstd")
        a_normed = sem("a_normed")
        o_out = [sem(f"o_out{s}") for s in range(R)]

        block = ctx.enter_context(nc.Block())

        @block.sync
        def _(sp):
            for s in range(R):
                sp.dma_start(a[s][:, :], a_tiles[s]).then_inc(a_in[s], 16)
            sp.dma_start(gfin[:, :], g_final).then_inc(g_in, 16)
            with sp.Fori(1, NT // R) as i:
                for s in range(R):
                    sp.wait_ge(o_out[s], i * 16)
                    sp.dma_start(a[s][:, :], a_tiles[ds1(i * R + s)].rearrange("a p d -> p (a d)")
                                 ).then_inc(a_in[s], 16)
            for s in range(R):
                sp.wait_ge(o_out[s], 16 * NT // R)

        @block.gpsimd
        def _(pool):
            nc.gpsimd.memset(minus_half[:, :], -0.5)
            pool.drain()
            with pool.Fori(0, NT // R) as i:
                for s in range(R):
                    pool.wait_ge(a_mean, i * R + (s + 1))
                    carry(pool, marks)
                    inverse_root(nc, pool, rstd[:, s:s + 1], mean[:, s:s + 1], minus_half
                                 ).then_inc(a_rstd, 1)

        @block.scalar
        def _(act):
            with act.Fori(0, NT // R) as i:
                for s in range(R):
                    act.drain()
                    act.wait_ge(a_in[s], i * 16 + 16)
                    nc.scalar.activation(junk[:, :], a[s][:, :], ACT.Square, scale=float(D) ** -0.5,
                                         accum_out=mean[:, s:s + 1]).then_inc(a_mean, 1)
                for s in range(R):
                    act.wait_ge(a_normed, i * R + (s + 1))
                    act.dma_start(o_tiles[ds1(i * R + s)].rearrange("a p d -> p (a d)"), a[s][:, :]
                                  ).then_inc(o_out[s], 16)

        @block.vector
        def _(dve):
            dve.wait_ge(g_in, 16)
            with dve.Fori(0, NT // R) as i:
                for s in range(R):
                    dve.wait_ge(a_rstd, i * R + (s + 1))
                    nc.vector.scalar_tensor_tensor(out=a[s][:, :], in0=a[s][:, :],
                                                   scalar=rstd[:, s:s + 1], in1=gfin[:, :],
                                                   op0=ALU.mult, op1=ALU.mult).then_inc(a_normed, 1)


def lay_out(x, g_mix, w_in, b_gate, w_pool_group, pool_scale, w_pool_out, conv_w, w_conv_out, w_o,
            g_ffn, w_router, router_bias, e_gate, e_up, e_down, s_gate, s_up, s_down, g_final):
    a = {k: np.asarray(v) for k, v in locals().items()}
    rows = lambda v: np.ascontiguousarray(np.broadcast_to(v.reshape(1, -1), (P, v.size)))
    slices = lambda w: w.reshape(-1, P, w.shape[1]).transpose(1, 0, 2)

    def column(w, m):
        return slices(w)[:, :, m * P:(m + 1) * P]

    w_in = a["w_in"]
    o = [0, G, 2 * G, 3 * G, 4 * G, 4 * G + MT]
    units = [column(w_in, o[0] + g) for g in range(G)]
    for q in range(G):
        units += [column(w_in, o[2] + q), column(w_in, o[3] + q), column(w_in, o[1] + q)]
    for m in range(MT):
        units += [column(w_in, o[4] + m), column(w_in, o[5] + m),
                  np.concatenate([column(a["w_pool_out"], m), column(a["w_conv_out"], m)], axis=1)]
    wo = slices(a["w_o"])
    for h in range(2):
        for v in range(4):
            units.append(wo[:, 2 * v:2 * v + 2, h * 512:(h + 1) * 512])
    units = np.stack([u.reshape(P, D) for u in units])

    def expert(gate, up, down):
        gu = np.concatenate([slices(gate), slices(up)], axis=2).reshape(P, KD // 2, D)
        return np.concatenate([gu, slices(down)], axis=1)

    experts = np.empty((NE + 1, P, PIECES, D), np.float32)
    experts[0] = expert(a["s_gate"], a["s_up"], a["s_down"])
    for e in range(NE):
        experts[e + 1] = expert(a["e_gate"][e], a["e_up"][e], a["e_down"][e])

    t = np.arange(HALO)
    inv = np.stack([1.0 / np.minimum(t + 1, w) for w in WINDOWS]).astype(np.float32)
    iotas = np.zeros((4, P, NB), np.float32)
    iotas[0] = 1.0
    iotas[1:3] = np.arange(NB)
    iotas[3] = np.arange(NB) >= SHARED_BLOCKS
    return {
        "x": a["x"].reshape(S, D),
        "units": units,
        "wgroup": np.ascontiguousarray(a["w_pool_group"].transpose(1, 0, 2)),
        "pool_scale": np.ascontiguousarray(a["pool_scale"].reshape(G, P).T),
        "conv_w": np.ascontiguousarray(a["conv_w"].reshape(3, G, P).transpose(2, 1, 0)),
        "b_gate": np.ascontiguousarray(a["b_gate"].reshape(2 * MT, P).T),
        "g_mix": rows(a["g_mix"]),
        "g_ffn": rows(a["g_ffn"]),
        "g_final": rows(a["g_final"]),
        "w_router": np.ascontiguousarray(slices(a["w_router"])),
        "router_bias": rows(a["router_bias"]),
        "experts": experts,
        "inv_count": np.ascontiguousarray(np.broadcast_to(inv, (P, G, HALO))),
        "ident": np.eye(P, dtype=np.float32),
        "tri": np.triu(np.ones((P, P), np.float32), 1),
        "iotas": iotas,
    }


def kernel(**inputs):
    import concourse.bacc as bacc
    from concourse.bass_utils import run_bass_kernel_spmd

    arrays = lay_out(**inputs)
    nc = bacc.Bacc("TRN2", target_bir_lowering=False, num_devices=1)
    args = {n: nc.dram_tensor(n, v.shape, mybir.dt.from_np(v.dtype), kind="ExternalInput").ap()
            for n, v in arrays.items()}
    out = nc.dram_tensor("out", (S, D), F32, kind="ExternalOutput").ap()
    build(nc, out=out, **args)
    r = run_bass_kernel_spmd(nc, [arrays], core_ids=[0])
    return r.results[0]["out"].reshape(1, S, D)
```

```python
from contextlib import ExitStack

import numpy as np

import concourse.bass as bass
from concourse import mybir

F32 = mybir.dt.float32
F32R = mybir.dt.float32r
BF16 = mybir.dt.bfloat16
I32 = mybir.dt.int32
U32 = mybir.dt.uint32
ALU = mybir.AluOpType
ACT = mybir.ActivationFunctionType
AX = mybir.AxisListType

P = 128
D = 1024
S = 2048
KD = D // P
T = 512
NCH = S // T
TT = T // P
NT = S // P
G = 4
WINDOWS = (2, 4, 8, 16)
HALO = 16
MT = D // P
UNITS = 48
MERGE0, BACK0 = 4 * G, 4 * G + 3 * MT
NE = 64
TOPK = 8
H = 256
SCALE = 2.5
EPS = 1e-6
SHARED_BLOCKS = S // P
NBMAX = S * TOPK // P + NE + SHARED_BLOCKS
NB = NBMAX + 4
ROWS = S
LISTS = NE + 2
PIECES = 6


def wait(eng, sem, value):
    if isinstance(value, int) and value <= 0:
        return
    eng.wait_ge(sem, value)


def carry(eng, marks):
    eng.sem_inc(marks[eng.engine.name], 1)


def ds1(i):
    return bass.ds(i, 1)


def inverse_root(nc, pool, dst, src, minus_half):
    nc.gpsimd.tensor_scalar(dst, src, EPS, None, ALU.add)
    pool.drain()
    return nc.gpsimd.tensor_tensor(dst, dst, minus_half[:, :], ALU.pow)


def build(nc, x, units, wgroup, pool_scale, conv_w, b_gate, g_mix, g_ffn, g_final, w_router,
          router_bias, experts, inv_count, ident, tri, iotas, out):
    acc = nc.dram_tensor("acc", [S + P, D], F32, kind="Internal").ap()
    h2_dram = nc.dram_tensor("h2_dram", [S + P, D], F32, kind="Internal").ap()
    lists = nc.dram_tensor("lists", [LISTS * ROWS, 2], I32, kind="Internal").ap()

    with ExitStack() as ctx:
        def sem(name):
            return ctx.enter_context(nc.semaphore(name))

        marks = {n: sem(f"mark_{n}") for n in ("Pool", "PE", "DVE", "SP", "Activation")}
        table = ctx.enter_context(nc.sbuf_tensor("table", [1, 3 * NB + 2], I32))
        route(nc, sem, marks, table, acc, h2_dram, lists, x, units, wgroup, pool_scale, conv_w, b_gate,
              g_mix, g_ffn, w_router, router_bias, inv_count, ident, tri, iotas)
        mixture(nc, sem, marks, table, acc, h2_dram, lists, experts, ident)
        final_norm(nc, sem, marks, acc, g_final, out)


def route(nc, sem, marks, table, acc, h2_dram, lists, x, units, wgroup, pool_scale, conv_w, b_gate,
          g_mix, g_ffn, w_router, router_bias, inv_count, ident_in, tri_in, iotas):
    x_tiles = x.rearrange("(n p) d -> n p d", p=P)
    acc_chunks = acc[0:S, :].rearrange("(c i p) d -> c p i d", p=P, i=TT)
    x_chunks = x.rearrange("(c i p) d -> c p i d", p=P, i=TT)
    h2_tiles = h2_dram.rearrange("(n p) d -> n p d", p=P)

    with ExitStack() as ctx:
        def sb(name, shape, dt=F32):
            return ctx.enter_context(nc.sbuf_tensor(name, shape, dt))

        ident = sb("eye", [P, P])
        tri = sb("triangle", [P, P])
        ones = sb("ones", [P, P])
        iota_e = sb("iota_e", [P, NE])
        iota_j = sb("iota_j", [NE, NB])
        from16 = sb("from16", [1, NB])
        gmix = sb("gmix", [P, D])
        gffn = sb("gffn", [P, D])
        wr = sb("wr", [P, KD, NE])
        rbias = sb("rbias", [P, NE])
        pscale = sb("pscale", [P, G])
        cw = sb("cw", [P, G, 3])
        bg = sb("bg", [P, 2 * MT])
        icnt = sb("icnt", [P, G, HALO])
        wg = sb("wg", [P, G, P])
        wgh = sb("wgh", [P, G, P], F32R)
        wgl = sb("wgl", [P, G, P], F32R)
        raw = sb("raw", [P, 2, D])
        uh = [sb(f"uh{s}", [P, KD, P], F32R) for s in range(2)]
        ul = [sb(f"ul{s}", [P, KD, P], F32R) for s in range(2)]
        hh = sb("hh", [P, KD, T], F32R)
        hl = sb("hl", [P, KD, T], F32R)
        ah = sb("ah", [P, G, T], F32R)
        al = sb("al", [P, G, T], F32R)
        bh = sb("bh", [P, G, T], F32R)
        bl = sb("bl", [P, G, T], F32R)
        mh = sb("mh", [P, MT, T], F32R)
        ml = sb("ml", [P, MT, T], F32R)
        xin = [sb(f"xin{s}", [P, D]) for s in range(2)]
        x2 = sb("x2", [P, TT, D])
        h2 = sb("h2", [P, D])
        h2t = sb("h2t", [P, KD, P])
        junk = sb("junk", [P, D], BF16)
        mean = sb("mean", [P, TT + 2])
        rstd = sb("rstd", [P, TT + 2])
        YCOL = TT + 1
        minus_half = sb("minus_half", [P, 1])
        ubuf = sb("ubuf", [P, HALO + T])
        uhalo = sb("uhalo", [P, G, HALO])
        win = [sb(f"win{s}", [P, HALO + T]) for s in range(2)]
        pooled = sb("pooled", [P, T])
        ph = sb("ph", [P, T], F32R)
        pl = sb("pl", [P, T], F32R)
        csb = sb("csb", [P, T])
        cv = sb("cv", [P, 2 + T])
        cvhalo = sb("cvhalo", [P, G, 2])
        tap = win[0][:, 0:T]
        bcv = pooled[:, :]
        siga = sb("siga", [P, T])
        sigb = sb("sigb", [P, T])
        m1 = win[0][:, 0:T]
        m2 = win[1][:, 0:T]
        sc = sb("sc", [P, NE])
        biased = sb("biased", [P, NE])
        top = sb("top", [P, TOPK])
        idx = sb("idx", [P, TOPK], U32)
        idxf = sb("idxf", [P, TOPK])
        hot = sb("hot", [P, TOPK, NE])
        hotx = win[1][:, 0:TOPK * NE].rearrange("p (k e) -> p k e", k=TOPK)
        mask = sb("mask", [P, NE])
        w8 = sb("w8", [P, TOPK])
        den = sb("den", [P, 1])
        rank = sb("rank", [P, NE])
        r8 = sb("r8", [P, TOPK])
        taken = sb("taken", [P, NE])
        total = sb("total", [NE, 1])
        tokid = sb("tokid", [P, NT], I32)
        pay = sb("pay", [P, TOPK, 2], I32)
        dest = sb("dest", [P, TOPK], I32)
        blank = sb("blank", [P, P, 2], I32)
        shared_list = sb("shared_list", [P, S // P, 2], I32)
        nblk_i = sb("nblk_i", [NE, 1], I32)
        nblk = sb("nblk", [NE, 1])
        bend = sb("bend", [NE, 1])
        over = sb("over", [NE, NB])
        eid_f = sb("eid_f", [1, NB])
        bst_f = sb("bst_f", [1, NB])
        row_f = sb("row_f", [1, NB])
        first_f = sb("first_f", [1, NB])
        pairs_f = sb("pairs_f", [1, 1])

        banks = [ctx.enter_context(nc.psum_tensor(f"bank{b}", [P, 512], F32)) for b in range(4)]
        ps_t = ctx.enter_context(nc.psum_tensor("ps_t", [P, 2, 512], F32))
        proj = [ps_t[:, 0, :], ps_t[:, 1, :]]
        ps_t8 = ps_t[:, :, :].rearrange("p b (k t) -> p (b k) t", t=P)
        ps_a = ctx.enter_context(nc.psum_tensor("ps_a", [P, 512], F32))
        ps_b = ctx.enter_context(nc.psum_tensor("ps_b", [P, 512], F32))

        const_in = sem("const_in")
        halo_zero = sem("halo_zero")
        rows_made = sem("rows_made")
        dram_set = sem("dram_set")
        first_in = [sem("first_in0"), sem("first_in1")]
        gmix_in = sem("gmix_in")
        ident_in_sb = sem("ident_in_sb")
        raw_in = [sem("raw_in0"), sem("raw_in1")]
        unit_hi = sem("unit_hi")
        unit_ready = sem("unit_ready")
        unit_done = sem("unit_done")
        x_in = [sem("x_in0"), sem("x_in1")]
        res_in = sem("res_in")
        acc_out = sem("acc_out")
        h2_out = sem("h2_out")
        x_mean = sem("x_mean")
        x_rstd = sem("x_rstd")
        x_normed = sem("x_normed")
        x_turned = sem("x_turned")
        x_hi = sem("x_hi")
        x_split = sem("x_split")
        grp_hi = sem("grp_hi")
        grp_split = sem("grp_split")
        u_copied = sem("u_copied")
        pooled_split = sem("pooled_split")
        mixed_done = sem("mixed_done")
        a_hi = sem("a_hi")
        a_split = sem("a_split")
        c_copied = sem("c_copied")
        cv_done = sem("cv_done")
        b_split = sem("b_split")
        gate_a = sem("gate_a")
        gate_b = sem("gate_b")
        branches_read = sem("branches_read")
        merged = sem("merged")
        wo_done = sem("wo_done")
        x2_added = sem("x2_added")
        y_mean = sem("y_mean")
        y_rstd = sem("y_rstd")
        y_normed = sem("y_normed")
        y_turned = sem("y_turned")
        y_copied = sem("y_copied")
        logits_done = sem("logits_done")
        scored = sem("scored")
        masked = sem("masked")
        ranked = sem("ranked")
        dest_ready = sem("dest_ready")
        list_out = sem("list_out")
        tab_a = sem("tab_a")
        tab_b = sem("tab_b")
        tab_c = sem("tab_c")
        tab_d = sem("tab_d")

        NCONST = 16 * 13
        SETS = 16 * 10

        block = ctx.enter_context(nc.Block())

        @block.sync
        def _(sp):
            def load_unit(k, s, c):
                sp.wait_ge(unit_ready, k + (c * UNITS - 1))
                sp.dma_start(raw[:, s, :], units[ds1(k % UNITS)].rearrange("a p f -> p (a f)")
                             ).then_inc(raw_in[s], 16)

            def load_units(c, lo, hi):
                with sp.Fori(0, (hi - lo) // 2) as i:
                    for s in range(2):
                        load_unit(i * 2 + (lo + s), s, c)

            sp.dma_start(x2[:, 0:1, :], x_chunks[0][:, 0:1, :]).then_inc(first_in[0], 16)
            sp.dma_start(raw[:, 0, :], units[0]).then_inc(raw_in[0], 16)
            sp.dma_start(gmix[:, :], g_mix).then_inc(gmix_in, 16)
            sp.dma_start(x2[:, 1:2, :], x_chunks[0][:, 1:2, :]).then_inc(first_in[1], 16)
            sp.dma_start(ident[:, :], ident_in).then_inc(ident_in_sb, 16)
            sp.dma_start(raw[:, 1, :], units[1]).then_inc(raw_in[1], 16)
            sp.dma_start(x2[:, 2:TT, :], x_chunks[0][:, 2:TT, :]).then_inc(res_in, 16)
            for dst, src in ((wg, wgroup), (icnt, inv_count), (pscale, pool_scale), (cw, conv_w),
                             (bg, b_gate), (tri, tri_in), (iota_j, iotas[2, 0:NE, :]),
                             (from16, iotas[3, 0:1, :]), (iota_e, iotas[1, :, 0:NE]),
                             (gffn, g_ffn), (wr, w_router), (rbias, router_bias)):
                sp.dma_start(dst[tuple(slice(None) for _ in dst.shape)], src).then_inc(const_in, 16)
            sp.dma_start(ones[:, :], iotas[0, :, 0:P]).then_inc(const_in, 16)

            load_units(0, 2, UNITS + 2)
            with sp.Fori(0, NCH - 1) as b:
                c = b + 1
                load_units(c, 2, 6)
                sp.wait_ge(x2_added, c * 8 + 4)
                sp.dma_start(acc_chunks[ds1(b)].rearrange("a p i d -> p (a i) d"),
                             x2[:, :, :]).then_inc(acc_out, 16)
                load_units(c, 6, BACK0)
                sp.wait_ge(acc_out, c * 16)
                carry(sp, marks)
                sp.wait_ge(y_normed, c * TT)
                carry(sp, marks)
                sp.dma_start(x2[:, :, :], x_chunks[ds1(c)].rearrange("a p i d -> p (a i) d")
                             ).then_inc(res_in, 16)
                load_units(c, BACK0, UNITS + 2)
            sp.wait_ge(x2_added, NCH * 8 + 4)
            sp.dma_start(acc_chunks[NCH - 1], x2[:, :, :]).then_inc(acc_out, 16)
            sp.wait_ge(acc_out, NCH * 16)

        @block.gpsimd
        def _(pool):
            def x_load(n, s):
                pool.wait_ge(x_turned, n - 1)
                carry(pool, marks)
                pool.dma_start(xin[s][:, :], x_tiles[ds1(n % NT)].rearrange("a p d -> p (a d)")
                               ).then_inc(x_in[s], 16)

            def x_norm(n, col):
                pool.wait_ge(x_mean, n + 1)
                carry(pool, marks)
                inverse_root(nc, pool, rstd[:, col:col + 1], mean[:, col:col + 1], minus_half
                             ).then_inc(x_rstd, 1)

            def y_norm(n):
                pool.wait_ge(y_mean, n + 1)
                carry(pool, marks)
                inverse_root(nc, pool, rstd[:, YCOL:YCOL + 1], mean[:, YCOL:YCOL + 1],
                             minus_half).then_inc(y_rstd, 1)

            def scatter(n):
                pool.wait_ge(dest_ready, n + 2)
                carry(pool, marks)
                for k in range(TOPK):
                    nc.gpsimd.indirect_dma_start(
                        lists, bass.IndirectOffsetOnAxis(ap=dest[:, k:k + 1], axis=0),
                        pay[:, k, :], None).then_inc(list_out, 16)

            nc.gpsimd.memset(minus_half[:, :], -0.5)
            pool.drain()
            for i in range(TT):
                x_norm(i, i)
            x_load(TT, 0)
            nc.gpsimd.memset(h2[:, :], 0.0)
            nc.gpsimd.iota(blank[:, :, 0], pattern=[[1, P]], base=S, channel_multiplier=0)
            nc.gpsimd.memset(blank[:, :, 1], 0)
            nc.gpsimd.iota(shared_list[:, :, 0], pattern=[[1, S // P]], base=0,
                           channel_multiplier=S // P)
            nc.gpsimd.memset(shared_list[:, :, :].bitcast(F32)[:, :, 1], 1.0)
            nc.gpsimd.iota(tokid[:, :], pattern=[[P, NT]], base=0, channel_multiplier=1
                           ).then_inc(rows_made, 1)
            pool.wait_ge(rows_made, 1)
            carry(pool, marks)
            pool.dma_start(acc[S:S + P, :], h2[:, :]).then_inc(dram_set, 16)
            pool.dma_start(lists[0:S, :].rearrange("(p r) two -> p r two", p=P),
                           shared_list[:, :, :]).then_inc(dram_set, 16)
            at = S
            while at < LISTS * ROWS:
                parts = min(P, (LISTS * ROWS - at) // P)
                rows = lists[at:at + parts * P, :].rearrange("(p r) two -> p r two", p=parts)
                last = at + parts * P == LISTS * ROWS
                pool.dma_start(rows, blank[0:parts, :, :]).then_inc(list_out if last else dram_set, 16)
                at += parts * P
            x_norm(TT, TT)
            x_load(TT + 1, 1)

            def prep(c):
                for i in range(TT):
                    x_norm(c * TT + (TT + 1 + i), i + 1)
                    x_load(c * TT + (TT + 2 + i), i % 2)

            prep(0)
            pool.wait_ge(dram_set, SETS)
            pool.wait_ge(list_out, 16)
            pool.wait_ge(h2_out, 16)
            carry(pool, marks)
            with pool.Fori(0, NCH - 1) as b:
                n = b * TT
                y_norm(n)
                with pool.Fori(0, TT - 1) as i:
                    y_norm(i + n + 1)
                    scatter(i + n)
                scatter(n + (TT - 1))
                prep(b + 1)
            n = (NCH - 1) * TT
            y_norm(n)
            for q in range(1, TT):
                y_norm(n + q)
                scatter(n + q - 1)
            scatter(n + TT - 1)
            pool.wait_ge(list_out, 16 * TOPK * NT + 16)
            for s in range(2):
                pool.wait_ge(x_in[s], 16 * ((NCH + 1) * TT // 2 - 1))
            carry(pool, marks)

        @block.tensor
        def _(pe):
            def three(out_, sh, sl, vh, vl, first, last):
                nc.tensor.matmul(out_, sl, vh, start=first, stop=False)
                nc.tensor.matmul(out_, sh, vl, start=False, stop=False)
                return nc.tensor.matmul(out_, sh, vh, start=False, stop=last)

            def unit(u, k, out_):
                pe.wait_ge(unit_ready, u + 1)
                s = k % 2
                for kd in range(KD):
                    last = three(out_, uh[s][:, kd, :], ul[s][:, kd, :], hh[:, kd, :], hl[:, kd, :],
                                 kd == 0, kd == KD - 1)
                last.then_inc(unit_done, 1)

            def group(c, g):
                pe.wait_ge(pooled_split, c * G + g + 1)
                wait(pe, a_split, c * G + g)
                if g == 0:
                    pe.wait_ge(branches_read, c * MT + 1)
                three(ps_a[:, :], wgh[:, g, :], wgl[:, g, :], ph[:, :], pl[:, :], True, True
                      ).then_inc(mixed_done, 1)

            def turn_x(n, s):
                pe.wait_ge(x_normed, n + 1)
                wait(pe, x_split, n)
                for kd in range(KD):
                    last = nc.tensor.transpose(ps_t8[:, kd, :], xin[s][:, kd * P:(kd + 1) * P],
                                               ident[:, :])
                last.then_inc(x_turned, 1)

            def turn_y(n):
                pe.wait_ge(y_normed, n + 1)
                pe.wait_ge(y_copied, n + 1)
                for kd in range(KD):
                    last = nc.tensor.transpose(
                        banks[kd // 4][:, kd % 4 * P:(kd % 4 + 1) * P],
                        h2[:, kd * P:(kd + 1) * P], ident[:, :])
                last.then_inc(y_turned, 1)

            def router(n):
                pe.wait_ge(y_copied, n + 2)
                pe.wait_ge(scored, n + 1)
                for kd in range(KD):
                    last = nc.tensor.matmul(banks[2][:, 0:NE], h2t[:, kd, :], wr[:, kd, :],
                                            start=kd == 0, stop=kd == KD - 1)
                last.then_inc(logits_done, 1)

            def count(n):
                pe.wait_ge(masked, n + 2)
                pe.wait_ge(dest_ready, n + 1)
                nc.tensor.matmul(banks[3][:, 0:NE], tri[:, :], mask[:, :], start=True, stop=True)
                nc.tensor.matmul(banks[3][:, NE:2 * NE], ones[:, :], mask[:, :], start=True, stop=True)
                nc.tensor.matmul(banks[3][0:NE, 2 * NE:2 * NE + 1], mask[:, :], ones[:, 0:1],
                                 start=True, stop=True).then_inc(ranked, 1)

            def front(c, before=None):
                u = c * UNITS
                pe.wait_ge(x_split, (c + 1) * TT)
                carry(pe, marks)
                for q in range(G):
                    k = 4 * q
                    wait(pe, cv_done, c * G + q)
                    unit(u + k, k, proj[0])
                    wait(pe, b_split, c * G + q)
                    unit(u + k + 1, k + 1, proj[1])
                    pe.wait_ge(u_copied, c * G + q + 1)
                    unit(u + k + 2, k + 2, proj[0])
                    group(c, q)
                    pe.wait_ge(c_copied, c * G + q + 1)
                    unit(u + k + 3, k + 3, proj[1])
                if before is not None:
                    pe.wait_ge(x2_added, c * 8 + 4)
                    carry(pe, marks)
                with pe.Fori(0, MT // 2) as i:
                    for d in range(2):
                        k = MERGE0 + 3 * d
                        m = i * 2 + d
                        uu = i * 6 + (u + k)
                        if d == 0:
                            pe.wait_ge(cv_done, c * G + G)
                        pe.wait_ge(gate_a, m + (c * MT + 1))
                        unit(uu, k, proj[0])
                        if d == 0:
                            pe.wait_ge(b_split, c * G + G)
                        pe.wait_ge(gate_b, m + (c * MT + 1))
                        unit(uu + 1, k + 1, proj[1])
                        if before is not None and d == 0:
                            turn_y(i + before * TT)
                        pe.wait_ge(unit_ready, uu + 3)
                        pe.wait_ge(a_split, c * G + G)
                        pe.wait_ge(branches_read, m + (c * MT + 1))
                        s = (k + 2) % 2
                        for dst, vh, vl, k0 in ((ps_a, ah, al, 0), (ps_b, bh, bl, G)):
                            for g in range(G):
                                last = three(dst[:, :], uh[s][:, k0 + g, :], ul[s][:, k0 + g, :],
                                             vh[:, g, :], vl[:, g, :], g == 0, g == G - 1)
                        last.then_inc(unit_done, 1)
                        if before is not None:
                            (count if d else router)(i + before * TT)

            def back(c):
                u = c * UNITS + BACK0
                with pe.Fori(0, 2) as h:
                    for v in range(4):
                        s = v % 2
                        pe.wait_ge(unit_ready, h * 4 + (u + v + 1))
                        pe.wait_ge(merged, c * MT + 2 * v + 2)
                        vh = uh[s][:, :, :].rearrange("p (a b) n -> p a (b n)", a=2)
                        vl = ul[s][:, :, :].rearrange("p (a b) n -> p a (b n)", a=2)
                        for i in range(TT):
                            if v == 0:
                                pe.wait_ge(x2_added, h * 4 + (c * 8 + i + 1))
                            if v == 0 and i == TT - 1:
                                pe.wait_ge(dest_ready, c * TT + 1)
                            for kk in range(2):
                                kd = 2 * v + kk
                                tok = slice(i * P, (i + 1) * P)
                                last = three(banks[i][:, :], mh[:, kd, tok], ml[:, kd, tok],
                                             vh[:, kk, :], vl[:, kk, :], kd == 0, kd == KD - 1)
                            if v == 3 and i < TT - 1:
                                last.then_inc(wo_done, 1)
                        last.then_inc(unit_done, 1)
                        if v == 0:
                            pe.wait_ge(gate_a, c * MT + MT + 1)
                            pe.wait_ge(gate_b, c * MT + MT + 1)
                        if v % 2 == 0:
                            turn_x(h * 2 + ((c + 1) * TT + v // 2), v // 2)

            def tiles_alone(n):
                pe.wait_ge(x2_added, NCH * 8 + 4)
                turn_y(n)
                for q in range(TT):
                    router(n + q)
                    if q < TT - 1:
                        turn_y(n + q + 1)
                    count(n + q)

            pe.sem_inc(logits_done, 1)
            pe.sem_inc(ranked, 1)
            pe.wait_ge(ident_in_sb, 16)
            for i in range(TT):
                turn_x(i, i % 2)
            pe.wait_ge(const_in, NCONST)
            pe.wait_ge(grp_split, 1)
            front(0)
            back(0)
            with pe.Fori(0, NCH - 1) as b:
                front(b + 1, b)
                back(b + 1)
            tiles_alone((NCH - 1) * TT)
            pe.wait_ge(tab_a, 1)
            nc.tensor.matmul(banks[0][0:NE, 0:1], over[:, 0:NE], nblk[:, :], start=True, stop=True).then_inc(tab_b, 1)
            pe.wait_ge(tab_c, 1)
            nc.tensor.matmul(banks[1][0:1, 0:NB], ones[0:NE, 0:1], over[:, :], start=True, stop=True)
            nc.tensor.matmul(banks[2][0:1, 0:NB], nblk[:, 0:1], over[:, :], start=True, stop=True
                             ).then_inc(tab_d, 1)

        @block.scalar
        def _(act):
            def copy(dst, src, **kw):
                return nc.scalar.activation(dst, src, ACT.Copy, **kw)

            def split_hi(u, k):
                s = k % 2
                if isinstance(u, int):
                    act.wait_ge(raw_in[s], 16 * (u // 2 + 1))
                wait(act, unit_done, u - 1)
                copy(uh[s][:, :, :].rearrange("p k n -> p (k n)"), raw[:, s, :]).then_inc(unit_hi, 1)

            def split_next(base, k):
                u = base + k + 2
                if not isinstance(u, int):
                    act.wait_ge(raw_in[k % 2], 8 * base + 16 * (k // 2 + 2))
                split_hi(u, k)

            def square(src, col, signal):
                act.drain()
                nc.scalar.activation(junk[:, :], src, ACT.Square, scale=float(D) ** -0.5,
                                     accum_out=mean[:, col]).then_inc(signal, 1)

            def x_high(n, tok):
                act.wait_ge(x_turned, n + 1)
                copy(hh[:, :, tok], ps_t8[:, :, :]).then_inc(x_hi, 1)

            def y_square(i, added):
                act.wait_ge(x2_added, added)
                src = x2[:, i, :] if isinstance(i, int) else x2[:, ds1(i), :].rearrange(
                    "p a d -> p (a d)")
                carry(act, marks)
                square(src, slice(YCOL, YCOL + 1), y_mean)

            def y_copy(n):
                act.wait_ge(y_turned, n + 1)
                act.wait_ge(logits_done, n + 1)
                for b in range(2):
                    last = copy(h2t[:, 4 * b:4 * b + 4, :].rearrange("p k t -> p (k t)"), banks[b][:, :])
                last.then_inc(y_copied, 1)
                act.dma_start(h2_tiles[n] if isinstance(n, int) else
                              h2_tiles[ds1(n)].rearrange("a p d -> p (a d)"),
                              h2[:, :]).then_inc(h2_out, 16)

            def score(n):
                act.wait_ge(logits_done, n + 2)
                act.wait_ge(masked, n + 1)
                nc.scalar.activation(sc[:, :], banks[2][:, 0:NE], ACT.Sigmoid).then_inc(scored, 1)

            def a_high(c, g):
                act.wait_ge(mixed_done, c * G + g + 1)
                copy(ah[:, g, :], ps_a[:, :], scale=pscale[:, g:g + 1]).then_inc(a_hi, 1)

            def front(c, before=None):
                base = c * UNITS
                for q in range(G):
                    k = 4 * q
                    act.wait_ge(unit_done, base + k + 1)
                    wait(act, pooled_split, c * G + q)
                    copy(ubuf[:, 0:HALO], uhalo[:, q, :])
                    copy(ubuf[:, HALO:], proj[0])
                    act.drain()
                    copy(uhalo[:, q, :], proj[0][:, T - HALO:T]).then_inc(u_copied, 1)
                    split_next(base, k)
                    act.wait_ge(unit_done, base + k + 2)
                    wait(act, cv_done, c * G + q)
                    copy(csb[:, :], proj[1]).then_inc(c_copied, 1)
                    split_next(base, k + 1)
                    split_next(base, k + 2)
                    a_high(c, q)
                    split_next(base, k + 3)
                with act.Fori(0, MT // 2) as i:
                    if before is not None:
                        y_square(i, c * 8 + 4)
                    for d in range(2):
                        k = MERGE0 + 3 * d
                        m = i * 2 + d
                        ub = i * 6 + base
                        for j, (sig, bank, sm) in enumerate(((siga, 0, gate_a), (sigb, 1, gate_b))):
                            act.wait_ge(unit_done, ub + (k + j + 1))
                            act.wait_ge(branches_read, m + (c * MT + 1))
                            nc.scalar.activation(sig[:, :], proj[bank], ACT.Sigmoid,
                                                 bias=bg[:, bass.ds(m + j * MT, 1)]).then_inc(sm, 1)
                            act.wait_ge(raw_in[(k + j) % 2], 8 * ub + 16 * ((k + j) // 2 + 2))
                            split_hi(ub + (k + j + 2), k + j)
                        if before is not None and d == 0:
                            y_copy(i + before * TT)
                        act.wait_ge(raw_in[k % 2], 8 * ub + 16 * ((k + 2) // 2 + 2))
                        split_hi(ub + (k + 4), k + 2)
                        if before is not None and d == 0:
                            score(i + before * TT)

            def back(c):
                base = c * UNITS + BACK0
                with act.Fori(0, 2) as h:
                    for v in range(4):
                        ub = h * 4 + base
                        act.wait_ge(raw_in[v % 2], 8 * ub + 16 * (v // 2 + 2))
                        split_hi(ub + (v + 2), v)
                        if v % 2 == 0:
                            s = v // 2
                            x_high(h * 2 + ((c + 1) * TT + s), bass.ds(h * (2 * P) + s * P, P))
                            act.wait_ge(x_in[1 - s], h * 16 + ((c + 1) * (8 * TT) + 16 * (s - 1)))
                            carry(act, marks)
                            square(xin[1 - s][:, :], bass.ds(h * 2 + s + 1, 1), x_mean)

            act.sem_inc(gate_a, 1)
            act.sem_inc(gate_b, 1)
            act.sem_inc(y_copied, 1)
            act.sem_inc(scored, 1)
            for i in range(TT):
                act.wait_ge(first_in[i] if i < 2 else res_in, 16)
                carry(act, marks)
                square(x2[:, i, :], slice(i, i + 1), x_mean)
                if i == 1:
                    split_hi(0, 0)
                    split_hi(1, 1)
                if i >= 1:
                    x_high(i - 1, slice((i - 1) * P, i * P))
            x_high(TT - 1, slice((TT - 1) * P, TT * P))
            act.wait_ge(const_in, NCONST)
            copy(wgh[:, :, :], wg[:, :, :]).then_inc(grp_hi, 1)
            act.wait_ge(rows_made, 1)
            act.dma_start(h2_dram[S:S + P, :], h2[:, :]).then_inc(h2_out, 16)
            act.wait_ge(halo_zero, 1)
            act.wait_ge(x_in[0], 16)
            carry(act, marks)
            square(xin[0][:, :], slice(TT, TT + 1), x_mean)
            front(0)
            back(0)
            with act.Fori(0, NCH - 1) as b:
                front(b + 1, b)
                back(b + 1)
            n = (NCH - 1) * TT
            y_square(0, NCH * 8 + 1)
            for q in range(TT):
                y_copy(n + q)
                if q < TT - 1:
                    y_square(q + 1, NCH * 8 + q + 2)
                score(n + q)
            act.wait_ge(h2_out, 16 * NT + 16)

        @block.vector
        def _(dve):
            V = nc.vector

            def split_lo(u, k):
                s = k % 2
                dve.wait_ge(unit_hi, u + 1)
                V.tensor_tensor(ul[s][:, :, :].rearrange("p k n -> p (k n)"), raw[:, s, :],
                                uh[s][:, :, :].rearrange("p k n -> p (k n)"), ALU.subtract
                                ).then_inc(unit_ready, 1)

            def x_scale(n, src, s, col):
                dve.wait_ge(x_rstd, n + 1)
                V.scalar_tensor_tensor(out=xin[s][:, :], in0=src, scalar=rstd[:, col],
                                       in1=gmix[:, :], op0=ALU.mult, op1=ALU.mult
                                       ).then_inc(x_normed, 1)

            def x_low(n, tok):
                dve.wait_ge(x_hi, n + 1)
                V.tensor_tensor(hl[:, :, tok], ps_t8[:, :, :], hh[:, :, tok], ALU.subtract
                                ).then_inc(x_split, 1)

            def y_scale(i, n):
                dve.wait_ge(y_rstd, n + 1)
                dve.wait_ge(h2_out, n * 16 + 16)
                src = x2[:, i, :] if isinstance(i, int) else x2[:, ds1(i), :].rearrange(
                    "p a d -> p (a d)")
                V.scalar_tensor_tensor(out=h2[:, :], in0=src, scalar=rstd[:, YCOL:YCOL + 1],
                                       in1=gffn[:, :], op0=ALU.mult, op1=ALU.mult
                                       ).then_inc(y_normed, 1)

            def pool_group(c, g):
                w = WINDOWS[g]
                dve.wait_ge(u_copied, c * G + g + 1)
                src, width, turn = ubuf, 1, 0
                while width < w:
                    lo = 2 * width - 1 + (HALO - w)
                    V.tensor_tensor(win[turn][:, lo:], src[:, lo:], src[:, lo - width:HALO + T - width],
                                    ALU.add)
                    dve.drain()
                    src, width, turn = win[turn], 2 * width, 1 - turn
                V.scalar_tensor_tensor(out=pooled[:, :], in0=src[:, HALO:], scalar=1.0 / w,
                                       in1=ubuf[:, HALO:], op0=ALU.mult, op1=ALU.subtract)
                if isinstance(c, int):
                    dve.drain()
                    V.tensor_tensor(src[:, HALO:2 * HALO], src[:, HALO:2 * HALO], icnt[:, g, :], ALU.mult)
                    dve.drain()
                    V.tensor_tensor(pooled[:, 0:HALO], src[:, HALO:2 * HALO], ubuf[:, HALO:2 * HALO],
                                    ALU.subtract)
                dve.drain()
                wait(dve, mixed_done, c * G + g)
                V.tensor_copy(ph[:, :], pooled[:, :])
                dve.drain()
                V.tensor_tensor(pl[:, :], pooled[:, :], ph[:, :], ALU.subtract).then_inc(pooled_split, 1)
                dve.drain()

            def a_low(c, g):
                dve.wait_ge(a_hi, c * G + g + 1)
                V.scalar_tensor_tensor(out=al[:, g, :], in0=ps_a[:, :], scalar=pscale[:, g:g + 1],
                                       in1=ah[:, g, :], op0=ALU.mult, op1=ALU.subtract
                                       ).then_inc(a_split, 1)

            def conv_cv(c, q):
                dve.wait_ge(unit_done, c * UNITS + 4 * q + 3)
                dve.wait_ge(c_copied, c * G + q + 1)
                V.tensor_copy(cv[:, 0:2], cvhalo[:, q, :])
                V.tensor_tensor(cv[:, 2:], csb[:, :], proj[0], ALU.mult).then_inc(cv_done, 1)
                dve.drain()
                V.tensor_copy(cvhalo[:, q, :], cv[:, T:T + 2])
                V.tensor_scalar(tap, cv[:, 0:T], cw[:, q, 0:1], None, ALU.mult)
                for j in (1, 2):
                    dve.drain()
                    V.scalar_tensor_tensor(out=tap, in0=cv[:, j:j + T], scalar=cw[:, q, j:j + 1],
                                           in1=tap, op0=ALU.mult, op1=ALU.add)
                dve.drain()

            def conv_b(c, q):
                dve.wait_ge(unit_done, c * UNITS + 4 * q + 4)
                V.tensor_tensor(bcv, proj[1], tap, ALU.mult)
                dve.drain()
                V.tensor_copy(bh[:, q, :], bcv)
                dve.drain()
                V.tensor_tensor(bl[:, q, :], bcv, bh[:, q, :], ALU.subtract).then_inc(b_split, 1)
                dve.drain()

            def choose(n):
                dve.wait_ge(scored, n + 2)
                V.tensor_tensor(biased[:, :], sc[:, :], rbias[:, :], ALU.add)
                dve.drain()
                V.max(top[:, :], biased[:, :])
                dve.drain()
                V.max_index(idx[:, :], top[:, :], biased[:, :])
                dve.drain()
                V.tensor_copy(idxf[:, :], idx[:, :])
                dve.drain()
                V.tensor_tensor(hot[:, :, :], iota_e[:, None, :].to_broadcast([P, TOPK, NE]),
                                idxf[:, :, None].to_broadcast([P, TOPK, NE]), ALU.is_equal)
                dve.drain()
                dve.wait_ge(ranked, n + 1)
                V.tensor_tensor(hotx, hot[:, :, :], sc[:, None, :].to_broadcast([P, TOPK, NE]), ALU.mult)
                V.tensor_reduce(mask[:, :], hot[:, :, :].rearrange("p k e -> p e k"), AX.X, ALU.add
                                ).then_inc(masked, 1)
                dve.drain()
                V.tensor_reduce(w8[:, :], hotx, AX.X, ALU.add)
                dve.drain()
                V.tensor_reduce(den[:, :], w8[:, :], AX.X, ALU.add)
                dve.drain()
                V.reciprocal(den[:, :], den[:, :])
                dve.drain()
                dve.wait_ge(list_out, n * (16 * TOPK) + 16)
                V.tensor_copy(pay[:, :, 0], tokid[:, (slice(n, n + 1) if isinstance(n, int) else ds1(n))]
                              .to_broadcast([P, TOPK]))
                V.tensor_scalar(pay[:, :, :].bitcast(F32)[:, :, 1], w8[:, :], den[:, 0:1], SCALE,
                                ALU.mult, ALU.mult)
                dve.drain()

            def place(n):
                dve.wait_ge(ranked, n + 2)
                V.tensor_tensor(rank[:, :], banks[3][:, 0:NE], taken[:, :], ALU.add)
                dve.drain()
                V.tensor_tensor(taken[:, :], taken[:, :], banks[3][:, NE:2 * NE], ALU.add)
                V.tensor_tensor(total[:, :], total[:, :], banks[3][0:NE, 2 * NE:2 * NE + 1], ALU.add)
                V.tensor_tensor(hotx, hot[:, :, :], rank[:, None, :].to_broadcast([P, TOPK, NE]), ALU.mult)
                dve.drain()
                V.tensor_reduce(r8[:, :], hotx, AX.X, ALU.add)
                dve.drain()
                V.scalar_tensor_tensor(out=dest[:, :], in0=idxf[:, :], scalar=float(ROWS),
                                       in1=r8[:, :], op0=ALU.mult, op1=ALU.add).then_inc(dest_ready, 1)
                dve.drain()

            def front(c, before=None):
                base = c * UNITS
                for q in range(G):
                    k = 4 * q
                    split_lo(base + k + 2, k)
                    pool_group(c, q)
                    split_lo(base + k + 3, k + 1)
                    split_lo(base + k + 4, k + 2)
                    conv_cv(c, q)
                    split_lo(base + k + 5, k + 3)
                    conv_b(c, q)
                    a_low(c, q)
                with dve.Fori(0, MT // 2) as i:
                    if before is not None:
                        y_scale(i, i + before * TT)
                    for d in range(2):
                        k = MERGE0 + 3 * d
                        m = i * 2 + d
                        ub = i * 6 + base
                        split_lo(ub + (k + 2), k)
                        if before is not None and d == 1:
                            choose(i + before * TT)
                        split_lo(ub + (k + 3), k + 1)
                        split_lo(ub + (k + 4), k + 2)
                        dve.wait_ge(gate_a, m + (c * MT + 2))
                        dve.wait_ge(gate_b, m + (c * MT + 2))
                        dve.wait_ge(unit_done, ub + (k + 3))
                        V.tensor_tensor(m1, siga[:, :], ps_a[:, :], ALU.mult)
                        V.tensor_tensor(m2, sigb[:, :], ps_b[:, :], ALU.mult).then_inc(branches_read, 1)
                        dve.drain()
                        V.tensor_tensor(m1, m1, m2, ALU.add)
                        dve.drain()
                        mm = mh[:, ds1(m), :].rearrange("p a t -> p (a t)")
                        V.tensor_copy(mm, m1)
                        dve.drain()
                        V.tensor_tensor(ml[:, ds1(m), :].rearrange("p a t -> p (a t)"), m1, mm,
                                        ALU.subtract).then_inc(merged, 1)
                        dve.drain()
                    if before is not None:
                        place(i + before * TT)

            def back(c):
                base = c * UNITS + BACK0
                with dve.Fori(0, 2) as h:
                    for v in range(4):
                        ub = h * 4 + base
                        s = v // 2
                        n = h * 2 + ((c + 1) * TT + s)
                        if v == 3:
                            dve.wait_ge(res_in, (c + 1) * 16)
                            for i in range(TT):
                                if i < TT - 1:
                                    dve.wait_ge(wo_done, h * 3 + (c * 6 + i + 1))
                                else:
                                    dve.wait_ge(unit_done, ub + 4)
                                part = x2[:, i, bass.ds(h * (D // 2), D // 2)]
                                V.tensor_tensor(part, part, banks[i][:, :], ALU.add
                                                ).then_inc(x2_added, 1)
                        split_lo(ub + (v + 2), v)
                        if v % 2 == 0:
                            x_low(n, bass.ds(h * (2 * P) + s * P, P))
                        else:
                            x_scale(n + 1, xin[1 - s][:, :], 1 - s, bass.ds(h * 2 + s + 1, 1))

            dve.sem_inc(branches_read, 1)
            dve.sem_inc(masked, 1)
            dve.sem_inc(dest_ready, 1)
            dve.sem_inc(x2_added, TT)
            V.memset(uhalo[:, :, :], 0.0)
            V.memset(cvhalo[:, :, :], 0.0)
            V.memset(taken[:, :], float(ROWS))
            V.memset(total[:, :], 0.0).then_inc(halo_zero, 1)
            dve.wait_ge(gmix_in, 16)
            for i in range(TT):
                if i >= 2:
                    dve.wait_ge(x_turned, i - 1)
                x_scale(i, x2[:, i, :], i % 2, slice(i, i + 1))
                if i == 1:
                    split_lo(0, 0)
                    split_lo(1, 1)
                if i >= 1:
                    x_low(i - 1, slice((i - 1) * P, i * P))
            x_low(TT - 1, slice((TT - 1) * P, TT * P))
            dve.wait_ge(const_in, NCONST)
            dve.wait_ge(grp_hi, 1)
            V.tensor_tensor(wgl[:, :, :], wg[:, :, :], wgh[:, :, :], ALU.subtract).then_inc(grp_split, 1)
            x_scale(TT, xin[0][:, :], 0, slice(TT, TT + 1))
            front(0)
            back(0)
            with dve.Fori(0, NCH - 1) as b:
                front(b + 1, b)
                back(b + 1)
            n = (NCH - 1) * TT
            y_scale(0, n)
            for q in range(TT):
                if q < TT - 1:
                    y_scale(q + 1, n + q + 1)
                choose(n + q)
                place(n + q)

            V.tensor_scalar(total[:, :], total[:, :], float(P - 1), None, ALU.add)
            dve.drain()
            V.tensor_copy(nblk_i[:, :], total[:, :])
            dve.drain()
            V.tensor_scalar(nblk_i[:, :], nblk_i[:, :], 7, None, ALU.logical_shift_right)
            V.tensor_tensor(over[:, 0:NE], tri[0:NE, 0:NE], ident[0:NE, 0:NE], ALU.add)
            dve.drain()
            V.tensor_scalar(nblk[:, :], nblk_i[:, :], 1, None, ALU.max).then_inc(tab_a, 1)
            dve.wait_ge(tab_b, 1)
            V.tensor_scalar(bend[:, :], banks[0][0:NE, 0:1], float(SHARED_BLOCKS), None, ALU.add)
            dve.drain()
            V.tensor_scalar(over[:, :], iota_j[:, :], bend[:, 0:1], None, ALU.is_ge).then_inc(tab_c, 1)
            dve.wait_ge(tab_d, 1)
            V.tensor_tensor(eid_f[:, :], banks[1][0:1, 0:NB], from16[:, :], ALU.add)
            V.scalar_tensor_tensor(out=bst_f[:, :], in0=from16[:, :], scalar=float(SHARED_BLOCKS),
                                   in1=banks[2][0:1, 0:NB], op0=ALU.mult, op1=ALU.add)
            dve.drain()
            V.tensor_scalar(table[:, 0:NB], eid_f[:, :], float(NE), None, ALU.min)
            V.scalar_tensor_tensor(out=row_f[:, :], in0=eid_f[:, :], scalar=float(ROWS // P),
                                   in1=iota_j[0:1, :], op0=ALU.mult, op1=ALU.add)
            V.tensor_tensor(first_f[:, :], bst_f[:, :], iota_j[0:1, :], ALU.is_equal)
            V.tensor_scalar(over[0:1, :], eid_f[:, :], NE - 0.5, None, ALU.is_lt)
            V.tensor_scalar(pairs_f[:, :], bst_f[:, NB - 1:NB], -1.0, None, ALU.add)
            dve.drain()
            V.tensor_tensor(row_f[:, :], row_f[:, :], bst_f[:, :], ALU.subtract)
            V.tensor_tensor(first_f[:, :], first_f[:, :], over[0:1, :], ALU.mult)
            V.tensor_scalar(eid_f[:, :], eid_f[:, :], 1.0, None, ALU.add)
            V.tensor_copy(table[:, 3 * NB:3 * NB + 1], pairs_f[:, :])
            dve.drain()
            V.tensor_copy(table[:, NB:2 * NB], row_f[:, :])
            V.tensor_tensor(table[:, 2 * NB:3 * NB], first_f[:, :], eid_f[:, :], ALU.mult)
            V.tensor_scalar(table[:, 3 * NB + 1:3 * NB + 2], table[:, 3 * NB:3 * NB + 1], 1, None,
                            ALU.logical_shift_right)
            dve.drain()


def mixture(nc, sem, marks, table, acc, h2_dram, lists, experts, ident_in):
    list_blocks = lists.rearrange("(b p) two -> b p two", p=P)
    KP = KD // 2

    with ExitStack() as ctx:
        def sb(name, shape, dt=F32):
            return ctx.enter_context(nc.sbuf_tensor(name, shape, dt))

        ident = sb("eye2", [P, P])
        raw = sb("expert_raw", [P, PIECES, D])
        wh = sb("expert_hi", [P, 2 * PIECES, D], F32R)
        wl = sb("expert_lo", [P, 2 * PIECES, D], F32R)
        gidx = [sb(f"gidx{s}", [P, 2], I32) for s in range(2)]
        sidx = [sb(f"sidx{s}", [P, 2], I32) for s in range(2)]
        xs = [sb(f"xs{s}", [P, D]) for s in range(2)]
        xh = [sb(f"xh{s}", [P, KD, P], F32R) for s in range(2)]
        xl = [sb(f"xl{s}", [P, KD, P], F32R) for s in range(2)]
        sg = sb("sg", [P, H])
        hid = sb("hid", [P, H])
        hth = [sb(f"hth{s}", [P, 2, P], F32R) for s in range(2)]
        htl = [sb(f"htl{s}", [P, 2, P], F32R) for s in range(2)]
        y = [sb(f"y{s}", [P, D]) for s in range(2)]

        ps_x = ctx.enter_context(nc.psum_tensor("ps_x", [P, KD, P], F32))
        ps_gu = [ctx.enter_context(nc.psum_tensor(f"ps_gu{s}", [P, 512], F32)) for s in range(2)]
        ps_h = ctx.enter_context(nc.psum_tensor("ps_h", [P, 2, P], F32))
        ps_y = ctx.enter_context(nc.psum_tensor("ps_y", [P, D], F32))

        ident_ready = sem("ident_ready")
        piece_in = [sem(f"piece_in{p}") for p in range(PIECES)]
        piece_hi = sem("piece_hi")
        piece_ready = sem("piece_ready")
        gidx_in = [sem(f"gidx_in{s}") for s in range(2)]
        sidx_in = [sem(f"sidx_in{s}") for s in range(2)]
        xs_in = [sem(f"xs_in{s}") for s in range(2)]
        xs_turned = sem("xs_turned")
        xs_hi = sem("xs_hi")
        xs_split = sem("xs_split")
        gu_done = sem("gu_done")
        gate_sig = sem("gate_sig")
        hid_ready = sem("hid_ready")
        hid_turned = sem("hid_turned")
        hid_hi = sem("hid_hi")
        hid_split = sem("hid_split")
        down_done = sem("down_done")
        y_ready = sem("y_ready")
        y_out = [sem(f"y_out{s}") for s in range(2)]

        block = ctx.enter_context(nc.Block())

        def pairs(eng):
            return eng.value_load(table[0:1, 3 * NB + 1:3 * NB + 2],
                                  min_val=(SHARED_BLOCKS + NE - 1) // 2, max_val=NBMAX // 2)

        def expert_of(eng, j):
            at = slice(j, j + 1) if isinstance(j, int) else ds1(j)
            return eng.value_load(table[0:1, at], min_val=0, max_val=NE)

        def to_split(eng, j):
            at = bass.ds(j + 2 * NB, 1)
            return eng.value_load(table[0:1, at], min_val=0, max_val=NE)

        @block.sync
        def _(sp):
            def list_rows(j):
                at = slice(NB + j, NB + j + 1) if isinstance(j, int) else bass.ds(j + NB, 1)
                row = sp.value_load(table[0:1, at], min_val=0, max_val=(LISTS * ROWS // P - 1))
                return list_blocks[ds1(row)].rearrange("a p two -> p (a two)")

            def gather_list(j, s):
                sp.dma_start(gidx[s][:, :], list_rows(j)).then_inc(gidx_in[s], 16)

            def scatter_list(j, s):
                sp.dma_start(sidx[s][:, :], list_rows(j)).then_inc(sidx_in[s], 16)

            def load_expert(e):
                for p in range(PIECES):
                    wait(sp, piece_ready, (e - 1) * PIECES + p + 1)
                    src = experts[e] if isinstance(e, int) else experts[ds1(e % (NE + 1))].rearrange(
                        "a p f d -> p (a f) d")
                    sp.dma_start(raw[:, p, :], src[:, p, :]).then_inc(piece_in[p], 16)

            load_expert(0)
            sp.dma_start(ident[:, :], ident_in).then_inc(ident_ready, 16)
            for j in range(2):
                gather_list(j, j)
            scatter_list(0, 0)
            load_expert(1)
            for j in range(2):
                sp.wait_ge(xs_in[j], 16)
                gather_list(j + 2, j)
            load_expert(2)
            sp.wait_ge(xs_in[0], 32)
            gather_list(4, 0)
            n = pairs(sp)
            with sp.Fori(0, n) as i:
                for d in (1, 2):
                    j = i * 2 + d
                    s = d % 2
                    if d == 1:
                        sp.wait_ge(y_out[1], i * 16 + 16)
                    else:
                        sp.wait_ge(y_out[0], i * 16 + 32)
                    scatter_list(j, s)
                    sp.wait_ge(xs_in[s], i * 16 + (32 if d == 1 else 48))
                    gather_list(j + 4, s)
                    e = to_split(sp, j)
                    with sp.If(e > 0):
                        load_expert(e + 1)
            sp.wait_ge(y_out[1], n * 16 + 16)
            scatter_list(n * 2 + 1, 1)
            for p in range(PIECES):
                sp.wait_ge(piece_in[p], 16 * (NE + 2))

        @block.gpsimd
        def _(pool):
            def gather(s):
                nc.gpsimd.indirect_dma_start(
                    xs[s][:, :], None, h2_dram,
                    bass.IndirectOffsetOnAxis(ap=gidx[s][:, 0:1], axis=0)).then_inc(xs_in[s], 16)

            def scatter(s):
                nc.gpsimd.indirect_dma_start(
                    acc, bass.IndirectOffsetOnAxis(ap=sidx[s][:, 0:1], axis=0), y[s][:, :], None,
                    compute_op=ALU.add).then_inc(y_out[s], 16)

            for s in range(2):
                pool.dma_start(y[s][:, :], h2_dram[S:S + P, :]).then_inc(y_out[s], 16)
            for j in range(4):
                pool.wait_ge(gidx_in[j % 2], 16 * (j // 2 + 1))
                if j >= 2:
                    pool.wait_ge(xs_turned, j - 1)
                gather(j % 2)
            n = pairs(pool)
            with pool.Fori(0, n) as i:
                for d in (1, 2):
                    s = d % 2
                    pool.wait_ge(gidx_in[1 - s], i * 16 + 48)
                    pool.wait_ge(xs_turned, i * 2 + (d + 2))
                    carry(pool, marks)
                    gather(1 - s)
                    pool.wait_ge(y_ready, i * 2 + (d + 1))
                    pool.wait_ge(sidx_in[1 - s], i * 16 + 16)
                    pool.wait_ge(y_out[s], i * 16 + 16 * d)
                    carry(pool, marks)
                    scatter(1 - s)
            pool.wait_ge(y_ready, n * 2 + 2)
            pool.wait_ge(sidx_in[0], n * 16 + 16)
            pool.wait_ge(y_out[1], n * 16 + 16)
            carry(pool, marks)
            scatter(0)
            pool.wait_ge(y_ready, n * 2 + 3)
            pool.wait_ge(sidx_in[1], n * 16 + 16)
            pool.wait_ge(y_out[0], n * 16 + 32)
            carry(pool, marks)
            scatter(1)
            pool.wait_ge(y_out[1], n * 16 + 32)
            pool.wait_ge(xs_in[0], n * 16 + 32)
            pool.wait_ge(xs_in[1], n * 16 + 32)
            pool.wait_ge(gidx_in[0], n * 16 + 48)
            carry(pool, marks)

        @block.tensor
        def _(pe):
            def three(out_, sh, sl, vh, vl, first, last):
                nc.tensor.matmul(out_, sl, vh, start=first, stop=False)
                nc.tensor.matmul(out_, sh, vl, start=False, stop=False)
                return nc.tensor.matmul(out_, sh, vh, start=False, stop=last)

            def turn(j, s, filled):
                pe.wait_ge(xs_in[s], filled)
                wait(pe, xs_split, j)
                for kd in range(KD):
                    last = nc.tensor.transpose(ps_x[:, kd, :], xs[s][:, kd * P:(kd + 1) * P],
                                               ident[:, :])
                last.then_inc(xs_turned, 1)

            def piece(slot, p):
                if isinstance(slot, int):
                    return wh[:, slot * PIECES + p, :], wl[:, slot * PIECES + p, :]
                return tuple(w[:, ds1(slot * PIECES + p), :].rearrange("q a f -> q (a f)")
                             for w in (wh, wl))

            def gate_up(j, s, e):
                pe.wait_ge(xs_split, j + 1)
                wait(pe, hid_ready, j - 1)
                pe.wait_ge(piece_ready, e * PIECES + KP)
                slot = e % 2
                for p in range(KP):
                    ph_, pl_ = piece(slot, p)
                    for b in range(2):
                        kd = 2 * p + b
                        last = three(ps_gu[s][:, :], xh[s][:, kd, :], xl[s][:, kd, :],
                                     ph_[:, b * 512:(b + 1) * 512], pl_[:, b * 512:(b + 1) * 512],
                                     kd == 0, kd == KD - 1)
                last.then_inc(gu_done, 1)

            def down(j, s, e):
                pe.wait_ge(hid_split, j + 1)
                pe.wait_ge(y_ready, j + 1)
                pe.wait_ge(piece_ready, e * PIECES + PIECES)
                slot = e % 2
                for kk in range(2):
                    ph_, pl_ = piece(slot, KP + kk)
                    for b in range(2):
                        last = three(ps_y[:, b * 512:(b + 1) * 512], hth[s][:, kk, :],
                                     htl[s][:, kk, :], ph_[:, b * 512:(b + 1) * 512],
                                     pl_[:, b * 512:(b + 1) * 512], kk == 0, kk == 1)
                last.then_inc(down_done, 1)

            def turn_hidden(j):
                pe.wait_ge(hid_ready, j + 1)
                wait(pe, hid_split, j)
                for kk in range(2):
                    last = nc.tensor.transpose(ps_h[:, kk, :], hid[:, kk * P:(kk + 1) * P], ident[:, :])
                last.then_inc(hid_turned, 1)

            pe.wait_ge(ident_ready, 16)
            pe.sem_inc(down_done, 1)
            n = pairs(pe)
            turn(0, 0, 16)
            turn(1, 1, 16)
            gate_up(0, 0, 0)
            turn(2, 0, 32)
            turn_hidden(0)
            gate_up(1, 1, expert_of(pe, 1))
            with pe.Fori(0, n) as i:
                e0, e2 = expert_of(pe, i * 2), expert_of(pe, i * 2 + 2)
                turn(i * 2 + 3, 1, i * 16 + 32)
                down(i * 2, 0, e0)
                turn_hidden(i * 2 + 1)
                gate_up(i * 2 + 2, 0, e2)
                e1, e3 = expert_of(pe, i * 2 + 1), expert_of(pe, i * 2 + 3)
                turn(i * 2 + 4, 0, i * 16 + 48)
                down(i * 2 + 1, 1, e1)
                turn_hidden(i * 2 + 2)
                gate_up(i * 2 + 3, 1, e3)
            down(n * 2, 0, expert_of(pe, n * 2))
            turn_hidden(n * 2 + 1)
            down(n * 2 + 1, 1, expert_of(pe, n * 2 + 1))

        @block.scalar
        def _(act):
            def copy(dst, src, **kw):
                return nc.scalar.activation(dst, src, ACT.Copy, **kw)

            def pieces_hi(e, lo, hi, j):
                if lo < KP:
                    wait(act, gu_done, j)
                if hi > KP:
                    act.wait_ge(down_done, j + 1)
                for p in range(lo, hi):
                    act.wait_ge(piece_in[p], (e + 1) * 16)
                    at = (e % 2) * PIECES + p
                    dst = wh[:, at, :] if isinstance(at, int) else wh[:, ds1(at), :].rearrange(
                        "q a f -> q (a f)")
                    copy(dst, raw[:, p, :]).then_inc(piece_hi, 1)

            def x_high(j, s):
                act.wait_ge(xs_turned, j + 1)
                wait(act, gu_done, j - 1)
                copy(xh[s][:, :, :], ps_x[:, :, :]).then_inc(xs_hi, 1)

            def gate_sigmoid(j, s):
                act.wait_ge(gu_done, j + 1)
                wait(act, hid_ready, j)
                nc.scalar.activation(sg[:, :], ps_gu[s][:, 0:H], ACT.Sigmoid).then_inc(gate_sig, 1)

            def hidden_high(j, s):
                act.wait_ge(hid_turned, j + 1)
                act.wait_ge(down_done, j)
                copy(hth[s][:, :, :], ps_h[:, :, :]).then_inc(hid_hi, 1)

            def output(j, s, listed, added):
                act.wait_ge(down_done, j + 2)
                act.wait_ge(sidx_in[s], listed)
                act.wait_ge(y_out[s], added)
                copy(y[s][:, :], ps_y[:, :], scale=sidx[s][:, :].bitcast(F32)[:, 1:2]
                     ).then_inc(y_ready, 1)

            act.sem_inc(y_ready, 1)
            pieces_hi(0, 0, PIECES, 0)
            x_high(0, 0)
            x_high(1, 1)
            gate_sigmoid(0, 0)
            x_high(2, 0)
            pieces_hi(1, 0, PIECES, 0)
            hidden_high(0, 0)
            n = pairs(act)
            with act.Fori(0, n) as i:
                for d in (1, 2):
                    j = i * 2 + d
                    s = d % 2
                    gate_sigmoid(j, s)
                    x_high(j + 2, s)
                    e = to_split(act, j)
                    with act.If(e > 0):
                        pieces_hi(e, 0, KP, j)
                    output(j - 1, 1 - s, i * 16 + 16, i * 16 + 16)
                    hidden_high(j, s)
                    with act.If(e > 0):
                        pieces_hi(e, KP, PIECES, j)
            gate_sigmoid(n * 2 + 1, 1)
            output(n * 2, 0, n * 16 + 16, n * 16 + 16)
            hidden_high(n * 2 + 1, 1)
            output(n * 2 + 1, 1, n * 16 + 16, n * 16 + 16)

        @block.vector
        def _(dve):
            V = nc.vector

            def pieces_lo(e, lo, hi):
                for p in range(lo, hi):
                    dve.wait_ge(piece_hi, e * PIECES + (p + 1))
                    at = (e % 2) * PIECES + p
                    h_, l_ = (w[:, at, :] if isinstance(at, int) else w[:, ds1(at), :].rearrange(
                        "q a f -> q (a f)") for w in (wh, wl))
                    V.tensor_tensor(l_, raw[:, p, :], h_, ALU.subtract).then_inc(piece_ready, 1)

            def x_low(j, s):
                dve.wait_ge(xs_hi, j + 1)
                V.tensor_tensor(xl[s][:, :, :], ps_x[:, :, :], xh[s][:, :, :], ALU.subtract
                                ).then_inc(xs_split, 1)

            def hidden(j, s):
                dve.wait_ge(gate_sig, j + 1)
                wait(dve, hid_turned, j)
                V.tensor_tensor(hid[:, :], ps_gu[s][:, 0:H], sg[:, :], ALU.mult)
                dve.drain()
                V.tensor_tensor(hid[:, :], hid[:, :], ps_gu[s][:, H:2 * H], ALU.mult
                                ).then_inc(hid_ready, 1)

            def hidden_low(j, s):
                dve.wait_ge(hid_hi, j + 1)
                V.tensor_tensor(htl[s][:, :, :], ps_h[:, :, :], hth[s][:, :, :], ALU.subtract
                                ).then_inc(hid_split, 1)

            pieces_lo(0, 0, PIECES)
            x_low(0, 0)
            x_low(1, 1)
            hidden(0, 0)
            x_low(2, 0)
            pieces_lo(1, 0, PIECES)
            hidden_low(0, 0)
            n = pairs(dve)
            with dve.Fori(0, n) as i:
                for d in (1, 2):
                    j = i * 2 + d
                    s = d % 2
                    hidden(j, s)
                    x_low(j + 2, s)
                    e = to_split(dve, j)
                    with dve.If(e > 0):
                        pieces_lo(e, 0, KP)
                    hidden_low(j, s)
                    with dve.If(e > 0):
                        pieces_lo(e, KP, PIECES)
            hidden(n * 2 + 1, 1)
            hidden_low(n * 2 + 1, 1)


def final_norm(nc, sem, marks, acc, g_final, out):
    R = 2
    a_groups = acc[0:S, :].rearrange("(n r p) d -> n p r d", p=P, r=R)
    o_groups = out.rearrange("(n r p) d -> n p r d", p=P, r=R)

    with ExitStack() as ctx:
        def sb(name, shape, dt=F32):
            return ctx.enter_context(nc.sbuf_tensor(name, shape, dt))

        gfin = sb("gfin", [P, D])
        a = sb("a", [P, NT, D])
        junk = sb("junk3", [P, D], BF16)
        mean = sb("mean3", [P, NT])
        rstd = sb("rstd3", [P, NT])
        minus_half = sb("minus_half3", [P, 1])
        g_in = sem("g_in")
        a_in = [sem(f"a_in{n}") for n in range(NT // R)]
        a_mean = sem("a_mean")
        a_rstd = sem("a_rstd")
        a_normed = sem("a_normed")
        o_out = sem("o_out")

        block = ctx.enter_context(nc.Block())

        @block.sync
        def _(sp):
            for g in range(NT // R):
                sp.dma_start(a[:, g * R:(g + 1) * R, :], a_groups[g]).then_inc(a_in[g], 16)
                if g == 0:
                    sp.dma_start(gfin[:, :], g_final).then_inc(g_in, 16)
            for g in range(NT // R):
                sp.wait_ge(a_normed, (g + 1) * R)
                sp.dma_start(o_groups[g], a[:, g * R:(g + 1) * R, :]).then_inc(o_out, 16)
            sp.wait_ge(o_out, 16 * NT // R)

        @block.gpsimd
        def _(pool):
            nc.gpsimd.memset(minus_half[:, :], -0.5)
            pool.drain()
            for g in range(NT // R):
                pool.wait_ge(a_mean, (g + 1) * R)
                carry(pool, marks)
                for n in range(g * R, (g + 1) * R):
                    last = inverse_root(nc, pool, rstd[:, n:n + 1], mean[:, n:n + 1], minus_half)
                last.then_inc(a_rstd, 1)

        @block.scalar
        def _(act):
            for n in range(NT):
                act.wait_ge(a_in[n // R], 16)
                carry(act, marks)
                act.drain()
                nc.scalar.activation(junk[:, :], a[:, n, :], ACT.Square, scale=float(D) ** -0.5,
                                     accum_out=mean[:, n:n + 1]).then_inc(a_mean, 1)

        @block.vector
        def _(dve):
            dve.wait_ge(g_in, 16)
            for n in range(NT):
                dve.wait_ge(a_rstd, n // R + 1)
                nc.vector.scalar_tensor_tensor(out=a[:, n, :], in0=a[:, n, :],
                                               scalar=rstd[:, n:n + 1], in1=gfin[:, :],
                                               op0=ALU.mult, op1=ALU.mult).then_inc(a_normed, 1)


def lay_out(x, g_mix, w_in, b_gate, w_pool_group, pool_scale, w_pool_out, conv_w, w_conv_out, w_o,
            g_ffn, w_router, router_bias, e_gate, e_up, e_down, s_gate, s_up, s_down, g_final):
    a = {k: np.asarray(v) for k, v in locals().items()}
    rows = lambda v: np.ascontiguousarray(np.broadcast_to(v.reshape(1, -1), (P, v.size)))
    slices = lambda w: w.reshape(-1, P, w.shape[1]).transpose(1, 0, 2)

    def column(w, m):
        return slices(w)[:, :, m * P:(m + 1) * P]

    w_in = a["w_in"]
    o = [0, G, 2 * G, 3 * G, 4 * G, 4 * G + MT]
    units = []
    for q in range(G):
        units += [column(w_in, o[n] + q) for n in (0, 2, 3, 1)]
    for m in range(MT):
        units += [column(w_in, o[4] + m), column(w_in, o[5] + m),
                  np.concatenate([column(a["w_pool_out"], m), column(a["w_conv_out"], m)], axis=1)]
    wo = slices(a["w_o"])
    for h in range(2):
        for v in range(4):
            units.append(wo[:, 2 * v:2 * v + 2, h * 512:(h + 1) * 512])
    units = np.stack([u.reshape(P, D) for u in units])

    def expert(gate, up, down):
        gu = np.concatenate([slices(gate), slices(up)], axis=2).reshape(P, KD // 2, D)
        return np.concatenate([gu, slices(down)], axis=1)

    experts = np.empty((NE + 1, P, PIECES, D), np.float32)
    experts[0] = expert(a["s_gate"], a["s_up"], a["s_down"])
    for e in range(NE):
        experts[e + 1] = expert(a["e_gate"][e], a["e_up"][e], a["e_down"][e])

    t = np.arange(HALO)
    inv = np.stack([1.0 / np.minimum(t + 1, w) for w in WINDOWS]).astype(np.float32)
    iotas = np.zeros((4, P, NB), np.float32)
    iotas[0] = 1.0
    iotas[1:3] = np.arange(NB)
    iotas[3] = np.arange(NB) >= SHARED_BLOCKS
    return {
        "x": a["x"].reshape(S, D),
        "units": units,
        "wgroup": np.ascontiguousarray(a["w_pool_group"].transpose(1, 0, 2)),
        "pool_scale": np.ascontiguousarray(a["pool_scale"].reshape(G, P).T),
        "conv_w": np.ascontiguousarray(a["conv_w"].reshape(3, G, P).transpose(2, 1, 0)),
        "b_gate": np.ascontiguousarray(a["b_gate"].reshape(2 * MT, P).T),
        "g_mix": rows(a["g_mix"]),
        "g_ffn": rows(a["g_ffn"]),
        "g_final": rows(a["g_final"]),
        "w_router": np.ascontiguousarray(slices(a["w_router"])),
        "router_bias": rows(a["router_bias"]),
        "experts": experts,
        "inv_count": np.ascontiguousarray(np.broadcast_to(inv, (P, G, HALO))),
        "ident": np.eye(P, dtype=np.float32),
        "tri": np.triu(np.ones((P, P), np.float32), 1),
        "iotas": iotas,
    }


def kernel(**inputs):
    import concourse.bacc as bacc
    from concourse.bass_utils import run_bass_kernel_spmd

    arrays = lay_out(**inputs)
    nc = bacc.Bacc("TRN2", target_bir_lowering=False, num_devices=1)
    args = {n: nc.dram_tensor(n, v.shape, mybir.dt.from_np(v.dtype), kind="ExternalInput").ap()
            for n, v in arrays.items()}
    out = nc.dram_tensor("out", (S, D), F32, kind="ExternalOutput").ap()
    build(nc, out=out, **args)
    r = run_bass_kernel_spmd(nc, [arrays], core_ids=[0])
    return r.results[0]["out"].reshape(1, S, D)
```

```python
from contextlib import ExitStack

import numpy as np

import concourse.bass as bass
from concourse import mybir

F32 = mybir.dt.float32
F32R = mybir.dt.float32r
BF16 = mybir.dt.bfloat16
I32 = mybir.dt.int32
U32 = mybir.dt.uint32
ALU = mybir.AluOpType
ACT = mybir.ActivationFunctionType
AX = mybir.AxisListType

P = 128
D = 1024
S = 2048
KD = D // P
T = 512
NCH = S // T
TT = T // P
NT = S // P
G = 4
WINDOWS = (2, 4, 8, 16)
HALO = 16
MT = D // P
UNITS = 48
MERGE0, BACK0 = 4 * G, 4 * G + 3 * MT
NE = 64
TOPK = 8
H = 256
SCALE = 2.5
EPS = 1e-6
SHARED_BLOCKS = S // P
NBMAX = S * TOPK // P + NE
NB = NBMAX + SHARED_BLOCKS + 4
ROWS = S
LISTS = NE + 2
SHARED_LIST = NE + 1
PIECES = 6


def wait(eng, sem, value):
    if isinstance(value, int) and value <= 0:
        return
    eng.wait_ge(sem, value)


def carry(eng, marks):
    eng.sem_inc(marks[eng.engine.name], 1)


def ds1(i):
    return bass.ds(i, 1)


def inverse_root(nc, pool, dst, src, minus_half):
    nc.gpsimd.tensor_scalar(dst, src, EPS, None, ALU.add)
    pool.drain()
    return nc.gpsimd.tensor_tensor(dst, dst, minus_half[:, :], ALU.pow)


def build(nc, x, units, wgroup, pool_scale, conv_w, b_gate, g_mix, g_ffn, g_final, w_router,
          router_bias, experts, inv_count, ident, tri, iotas, out):
    acc = nc.dram_tensor("acc", [S + P, D], F32, kind="Internal").ap()
    h2_dram = nc.dram_tensor("h2_dram", [S + P, D], F32, kind="Internal").ap()
    lists = nc.dram_tensor("lists", [LISTS * ROWS, 2], I32, kind="Internal").ap()

    with ExitStack() as ctx:
        def sem(name):
            return ctx.enter_context(nc.semaphore(name))

        marks = {n: sem(f"mark_{n}") for n in ("Pool", "PE", "DVE", "SP", "Activation")}
        table = ctx.enter_context(nc.sbuf_tensor("table", [1, 3 * NB + 2], I32))
        expert_raw = ctx.enter_context(nc.sbuf_tensor("expert_raw", [P, PIECES, D], F32))
        piece_in = [sem(f"piece_in{p}") for p in range(PIECES)]
        route(nc, sem, marks, table, expert_raw, piece_in, experts, acc, h2_dram, lists, x, units,
              wgroup, pool_scale, conv_w, b_gate, g_mix, g_ffn, w_router, router_bias, inv_count,
              ident, tri, iotas)
        mixture(nc, sem, marks, table, expert_raw, piece_in, acc, h2_dram, lists, experts, ident,
                g_final, out)


def route(nc, sem, marks, table, expert_raw, piece_in, experts, acc, h2_dram, lists, x, units,
          wgroup, pool_scale, conv_w, b_gate, g_mix, g_ffn, w_router, router_bias, inv_count,
          ident_in, tri_in, iotas):
    x_tiles = x.rearrange("(n p) d -> n p d", p=P)
    acc_chunks = acc[0:S, :].rearrange("(c i p) d -> c p i d", p=P, i=TT)
    x_chunks = x.rearrange("(c i p) d -> c p i d", p=P, i=TT)
    h2_tiles = h2_dram.rearrange("(n p) d -> n p d", p=P)

    with ExitStack() as ctx:
        def sb(name, shape, dt=F32):
            return ctx.enter_context(nc.sbuf_tensor(name, shape, dt))

        xin = [expert_raw[:, s, :] for s in range(2)]
        siga, sigb, csb, pooled = (expert_raw[:, 2 + k // 2, k % 2 * T:(k % 2 + 1) * T]
                                   for k in range(4))
        gmix = expert_raw[:, 4, :]
        icnt, uhalo = (expert_raw[:, 5, k * G * HALO:(k + 1) * G * HALO].rearrange(
            "p (g t) -> p g t", g=G) for k in range(2))
        ubuf = expert_raw[:, 5, 2 * G * HALO:2 * G * HALO + HALO + T]
        ident = sb("eye", [P, P])
        tri = sb("triangle", [P, P])
        ones = sb("ones", [P, P])
        iota_e = sb("iota_e", [P, NE])
        iota_j = sb("iota_j", [NE, NB])
        gffn = sb("gffn", [P, D])
        wr = sb("wr", [P, KD, NE])
        rbias = sb("rbias", [P, NE])
        pscale = sb("pscale", [P, G])
        cw = sb("cw", [P, G, 3])
        bg = sb("bg", [P, 2 * MT])
        wg = sb("wg", [P, G, P])
        wgh = sb("wgh", [P, G, P], F32R)
        wgl = sb("wgl", [P, G, P], F32R)
        raw = sb("raw", [P, 2, D])
        uh = [sb(f"uh{s}", [P, KD, P], F32R) for s in range(2)]
        ul = [sb(f"ul{s}", [P, KD, P], F32R) for s in range(2)]
        hh = sb("hh", [P, KD, T], F32R)
        hl = sb("hl", [P, KD, T], F32R)
        ah = sb("ah", [P, G, T], F32R)
        al = sb("al", [P, G, T], F32R)
        bh = sb("bh", [P, G, T], F32R)
        bl = sb("bl", [P, G, T], F32R)
        mh = sb("mh", [P, MT, T], F32R)
        ml = sb("ml", [P, MT, T], F32R)
        x2 = sb("x2", [P, TT, D])
        h2 = sb("h2", [P, D])
        h2t = sb("h2t", [P, KD, P])
        junk = sb("junk", [P, D], BF16)
        YCOL, YTAIL = TT + 1, TT + 2
        mean = sb("mean", [P, YTAIL + TT])
        rstd = sb("rstd", [P, YTAIL + TT])
        minus_half = sb("minus_half", [P, 1])
        win = [sb(f"win{s}", [P, HALO + T]) for s in range(2)]
        ph = sb("ph", [P, T], F32R)
        pl = sb("pl", [P, T], F32R)
        cv = sb("cv", [P, 2 + T])
        cvhalo = sb("cvhalo", [P, G, 2])
        tap = win[0][:, 0:T]
        bcv = pooled[:, :]
        m1 = win[0][:, 0:T]
        m2 = win[1][:, 0:T]
        sc = sb("sc", [P, NE])
        biased = sb("biased", [P, NE])
        top = sb("top", [P, TOPK])
        idx = sb("idx", [P, TOPK], U32)
        idxf = sb("idxf", [P, TOPK])
        hot = sb("hot", [P, TOPK, NE])
        hotx = win[1][:, 0:TOPK * NE].rearrange("p (k e) -> p k e", k=TOPK)
        mask = sb("mask", [P, NE])
        w8 = sb("w8", [P, TOPK])
        den = sb("den", [P, 1])
        rank = sb("rank", [P, NE])
        r8 = sb("r8", [P, TOPK])
        taken = sb("taken", [P, NE])
        total = sb("total", [NE, 1])
        tokid = sb("tokid", [P, NT], I32)
        pay = sb("pay", [P, TOPK, 2], I32)
        dest = sb("dest", [P, TOPK], I32)
        tail_pay = sb("tail_pay", [P, TT, TOPK, 2], I32)
        tail_dest = sb("tail_dest", [P, TT, TOPK], I32)
        blank = sb("blank", [P, P, 2], I32)
        shared_list = sb("shared_list", [P, S // P, 2], I32)
        nblk_i = sb("nblk_i", [NE, 1], I32)
        nblk = sb("nblk", [NE, 1])
        bend = sb("bend", [NE, 1])
        over = sb("over", [NE, NB])
        eid_f = sb("eid_f", [1, NB])
        bst_f = sb("bst_f", [1, NB])
        row_f = sb("row_f", [1, NB])
        first_f = sb("first_f", [1, NB])
        end_i = sb("end_i", [NE, 1], I32)
        odd = sb("odd", [NE, 1])

        banks = [ctx.enter_context(nc.psum_tensor(f"bank{b}", [P, 512], F32)) for b in range(4)]
        ps_t = ctx.enter_context(nc.psum_tensor("ps_t", [P, 2, 512], F32))
        proj = [ps_t[:, 0, :], ps_t[:, 1, :]]
        ps_t8 = ps_t[:, :, :].rearrange("p b (k t) -> p (b k) t", t=P)
        ps_a = ctx.enter_context(nc.psum_tensor("ps_a", [P, 512], F32))
        ps_b = ctx.enter_context(nc.psum_tensor("ps_b", [P, 512], F32))

        const_in = sem("const_in")
        halo_zero = sem("halo_zero")
        rows_made = sem("rows_made")
        dram_set = sem("dram_set")
        first_in = [sem("first_in0"), sem("first_in1")]
        gmix_in = sem("gmix_in")
        ident_in_sb = sem("ident_in_sb")
        raw_in = [sem("raw_in0"), sem("raw_in1")]
        unit_hi = sem("unit_hi")
        unit_ready = sem("unit_ready")
        unit_done = sem("unit_done")
        x_in = [sem("x_in0"), sem("x_in1")]
        res_in = sem("res_in")
        acc_out = sem("acc_out")
        h2_out = sem("h2_out")
        x_mean = sem("x_mean")
        x_rstd = sem("x_rstd")
        x_normed = sem("x_normed")
        x_turned = sem("x_turned")
        x_hi = sem("x_hi")
        x_split = sem("x_split")
        grp_hi = sem("grp_hi")
        grp_split = sem("grp_split")
        u_copied = sem("u_copied")
        pooled_split = sem("pooled_split")
        mixed_done = sem("mixed_done")
        a_hi = sem("a_hi")
        a_split = sem("a_split")
        c_copied = sem("c_copied")
        cv_done = sem("cv_done")
        b_split = sem("b_split")
        gate_a = sem("gate_a")
        gate_b = sem("gate_b")
        branches_read = sem("branches_read")
        merged = sem("merged")
        wo_done = sem("wo_done")
        half_done = sem("half_done")
        x2_added = sem("x2_added")
        y_mean = sem("y_mean")
        y_rstd = sem("y_rstd")
        y_normed = sem("y_normed")
        y_turned = sem("y_turned")
        y_copied = sem("y_copied")
        logits_done = sem("logits_done")
        scored = sem("scored")
        masked = sem("masked")
        ranked = sem("ranked")
        dest_ready = sem("dest_ready")
        list_out = sem("list_out")
        tab_a = sem("tab_a")
        tab_b = sem("tab_b")
        tab_c = sem("tab_c")
        tab_d = sem("tab_d")

        NCONST = 16 * 12
        SETS = 16 * 10

        TAIL_HALVES = [(0, 0), (1, 0), (2, 0), (0, 1), (1, 1), (2, 1), (3, 0), (3, 1)]

        def first_turned(i, half):
            bank = (proj[half] if i % 2 == 0 else banks[half][:, :])
            return bank.rearrange("p (k t) -> p k t", t=P)

        def tail_unit(w):
            if w < 2:
                return tuple(u[w][:, :, :].rearrange("p (a b) n -> p a (b n)", a=2) for u in (uh, ul))
            if w < 6:
                return tuple(t[:, 2 * (w - 2):2 * (w - 1), :] for t in (hh, hl))
            return tuple(t[:, 2 * (w - 6):2 * (w - 5), :] for t in (ah, al))

        block = ctx.enter_context(nc.Block())

        @block.sync
        def _(sp):
            def load_unit(k, s, c):
                sp.wait_ge(unit_ready, k + (c * UNITS - 1))
                sp.dma_start(raw[:, s, :], units[ds1(k % UNITS)].rearrange("a p f -> p (a f)")
                             ).then_inc(raw_in[s], 16)

            def load_units(c, lo, hi):
                with sp.Fori(0, (hi - lo) // 2) as i:
                    for s in range(2):
                        load_unit(i * 2 + (lo + s), s, c)

            for i in range(2):
                sp.dma_start(x2[:, i:i + 1, :], x_chunks[0][:, i:i + 1, :]).then_inc(first_in[i], 16)
                if i == 0:
                    sp.dma_start(gmix[:, :], g_mix).then_inc(gmix_in, 16)
            sp.dma_start(ident[:, :], ident_in).then_inc(ident_in_sb, 16)
            sp.dma_start(x2[:, 2:TT, :], x_chunks[0][:, 2:TT, :]).then_inc(res_in, 16)
            for k in range(2):
                sp.dma_start(raw[:, k, :], units[k]).then_inc(raw_in[k], 16)
            for dst, src in ((wg, wgroup), (icnt, inv_count), (pscale, pool_scale), (cw, conv_w),
                             (bg, b_gate), (tri, tri_in), (iota_j, iotas[2, 0:NE, :]),
                             (iota_e, iotas[1, :, 0:NE]),
                             (gffn, g_ffn), (wr, w_router), (rbias, router_bias)):
                sp.dma_start(dst[tuple(slice(None) for _ in dst.shape)], src).then_inc(const_in, 16)
            sp.dma_start(ones[:, :], iotas[0, :, 0:P]).then_inc(const_in, 16)

            load_units(0, 2, UNITS)
            with sp.Fori(0, NCH - 1) as b:
                c = b + 1
                load_units(c, 0, 6)
                sp.wait_ge(x2_added, c * 8 + 4)
                sp.dma_start(acc_chunks[ds1(b)].rearrange("a p i d -> p (a i) d"),
                             x2[:, :, :]).then_inc(acc_out, 16)
                load_units(c, 6, BACK0)
                sp.wait_ge(acc_out, c * 16)
                carry(sp, marks)
                sp.wait_ge(y_normed, c * TT)
                carry(sp, marks)
                sp.dma_start(x2[:, :, :], x_chunks[ds1(c)].rearrange("a p i d -> p (a i) d")
                             ).then_inc(res_in, 16)
                load_units(c, BACK0, UNITS)
            sp.wait_ge(x_normed, NCH * TT + 1)
            carry(sp, marks)
            sp.wait_ge(x_in[1], 16 * (NCH * TT // 2 - 1))
            carry(sp, marks)
            sp.wait_ge(branches_read, NCH * MT + 1)
            for p in range(PIECES):
                sp.dma_start(expert_raw[:, p, :], experts[0][:, p, :]).then_inc(piece_in[p], 16)
            sp.wait_ge(x2_added, NCH * 8 + 4)
            sp.dma_start(acc_chunks[NCH - 1], x2[:, :, :]).then_inc(acc_out, 16)
            sp.wait_ge(acc_out, NCH * 16)

        @block.gpsimd
        def _(pool):
            def x_load(n, s):
                pool.wait_ge(x_turned, n - 1)
                carry(pool, marks)
                pool.dma_start(xin[s][:, :], x_tiles[ds1(n % NT)].rearrange("a p d -> p (a d)")
                               ).then_inc(x_in[s], 16)

            def x_norm(n, col):
                pool.wait_ge(x_mean, n + 1)
                carry(pool, marks)
                inverse_root(nc, pool, rstd[:, col:col + 1], mean[:, col:col + 1], minus_half
                             ).then_inc(x_rstd, 1)

            def y_norm(n, col=YCOL):
                pool.wait_ge(y_mean, n + 1)
                carry(pool, marks)
                inverse_root(nc, pool, rstd[:, col:col + 1], mean[:, col:col + 1],
                             minus_half).then_inc(y_rstd, 1)

            def scatter(n, dest=dest, pay=pay):
                pool.wait_ge(dest_ready, n + 2)
                carry(pool, marks)
                for k in range(TOPK):
                    nc.gpsimd.indirect_dma_start(
                        lists, bass.IndirectOffsetOnAxis(ap=dest[:, k:k + 1], axis=0),
                        pay[:, k, :], None).then_inc(list_out, 16)

            nc.gpsimd.memset(minus_half[:, :], -0.5)
            pool.drain()
            for i in range(TT):
                x_norm(i, i)
            x_load(TT, 0)
            nc.gpsimd.memset(h2[:, :], 0.0)
            nc.gpsimd.iota(blank[:, :, 0], pattern=[[1, P]], base=S, channel_multiplier=0)
            nc.gpsimd.memset(blank[:, :, 1], 0)
            nc.gpsimd.iota(shared_list[:, :, 0], pattern=[[1, S // P]], base=0,
                           channel_multiplier=S // P)
            nc.gpsimd.memset(shared_list[:, :, :].bitcast(F32)[:, :, 1], 1.0)
            nc.gpsimd.iota(tokid[:, :], pattern=[[P, NT]], base=0, channel_multiplier=1
                           ).then_inc(rows_made, 1)
            pool.wait_ge(rows_made, 1)
            carry(pool, marks)
            pool.dma_start(acc[S:S + P, :], h2[:, :]).then_inc(dram_set, 16)
            pool.dma_start(lists[SHARED_LIST * ROWS:, :].rearrange("(p r) two -> p r two", p=P),
                           shared_list[:, :, :]).then_inc(dram_set, 16)
            at = 0
            while at < SHARED_LIST * ROWS:
                parts = min(P, (SHARED_LIST * ROWS - at) // P)
                rows = lists[at:at + parts * P, :].rearrange("(p r) two -> p r two", p=parts)
                last = at + parts * P == SHARED_LIST * ROWS
                pool.dma_start(rows, blank[0:parts, :, :]).then_inc(list_out if last else dram_set, 16)
                at += parts * P
            x_norm(TT, TT)
            x_load(TT + 1, 1)

            def prep(c):
                for i in range(TT):
                    x_norm(c * TT + (TT + 1 + i), i + 1)
                    x_load(c * TT + (TT + 2 + i), i % 2)

            prep(0)
            pool.wait_ge(dram_set, SETS)
            pool.wait_ge(list_out, 16)
            pool.wait_ge(h2_out, 16)
            carry(pool, marks)
            def routed(before):
                n = before * TT
                y_norm(n)
                with pool.Fori(0, TT - 1) as i:
                    y_norm(i + (n + 1))
                    scatter(i + n)
                scatter(n + (TT - 1))

            with pool.Fori(0, NCH - 2) as b:
                routed(b)
                prep(b + 1)
            routed(NCH - 2)
            n = (NCH - 1) * TT

            def tail_scatter(q):
                scatter(n + q, tail_dest[:, q, :], tail_pay[:, q, :, :])

            for q in range(3):
                y_norm(n + q, YTAIL + q)
            tail_scatter(0)
            y_norm(n + 3, YTAIL + 3)
            for q in range(1, TT):
                tail_scatter(q)
            pool.wait_ge(list_out, 16 * TOPK * NT + 16)
            for s in range(2):
                pool.wait_ge(x_in[s], 16 * (NCH * TT // 2 - 1))
            carry(pool, marks)

        @block.tensor
        def _(pe):
            def three(out_, sh, sl, vh, vl, first, last):
                nc.tensor.matmul(out_, sl, vh, start=first, stop=False)
                nc.tensor.matmul(out_, sh, vl, start=False, stop=False)
                return nc.tensor.matmul(out_, sh, vh, start=False, stop=last)

            def unit(u, k, out_):
                pe.wait_ge(unit_ready, u + 1)
                s = k % 2
                for kd in range(KD):
                    last = three(out_, uh[s][:, kd, :], ul[s][:, kd, :], hh[:, kd, :], hl[:, kd, :],
                                 kd == 0, kd == KD - 1)
                last.then_inc(unit_done, 1)

            def group(c, g):
                pe.wait_ge(pooled_split, c * G + g + 1)
                wait(pe, a_split, c * G + g)
                if g == 0:
                    pe.wait_ge(branches_read, c * MT + 1)
                three(ps_a[:, :], wgh[:, g, :], wgl[:, g, :], ph[:, :], pl[:, :], True, True
                      ).then_inc(mixed_done, 1)

            def turn_x(n, s):
                pe.wait_ge(x_normed, n + 1)
                wait(pe, x_split, n)
                for kd in range(KD):
                    last = nc.tensor.transpose(ps_t8[:, kd, :], xin[s][:, kd * P:(kd + 1) * P],
                                               ident[:, :])
                last.then_inc(x_turned, 1)

            def turn_y(n):
                pe.wait_ge(y_normed, n + 1)
                pe.wait_ge(y_copied, n + 1)
                for kd in range(KD):
                    last = nc.tensor.transpose(
                        banks[kd // 4][:, kd % 4 * P:(kd % 4 + 1) * P],
                        h2[:, kd * P:(kd + 1) * P], ident[:, :])
                last.then_inc(y_turned, 1)

            def router(n):
                pe.wait_ge(y_copied, n + 2)
                pe.wait_ge(scored, n + 1)
                for kd in range(KD):
                    last = nc.tensor.matmul(banks[2][:, 0:NE], h2t[:, kd, :], wr[:, kd, :],
                                            start=kd == 0, stop=kd == KD - 1)
                last.then_inc(logits_done, 1)

            def count(n):
                pe.wait_ge(masked, n + 2)
                pe.wait_ge(dest_ready, n + 1)
                nc.tensor.matmul(banks[3][:, 0:NE], tri[:, :], mask[:, :], start=True, stop=True)
                nc.tensor.matmul(banks[3][:, NE:2 * NE], ones[:, :], mask[:, :], start=True, stop=True)
                nc.tensor.matmul(banks[3][0:NE, 2 * NE:2 * NE + 1], mask[:, :], ones[:, 0:1],
                                 start=True, stop=True).then_inc(ranked, 1)

            def front(c, before=None):
                u = c * UNITS
                pe.wait_ge(x_split, (c + 1) * TT)
                carry(pe, marks)
                for q in range(G):
                    k = 4 * q
                    wait(pe, cv_done, c * G + q)
                    unit(u + k, k, proj[0])
                    wait(pe, b_split, c * G + q)
                    unit(u + k + 1, k + 1, proj[1])
                    pe.wait_ge(u_copied, c * G + q + 1)
                    unit(u + k + 2, k + 2, proj[0])
                    group(c, q)
                    pe.wait_ge(c_copied, c * G + q + 1)
                    unit(u + k + 3, k + 3, proj[1])
                if before is not None:
                    pe.wait_ge(x2_added, c * 8 + 4)
                    carry(pe, marks)
                with pe.Fori(0, MT // 2) as i:
                    for d in range(2):
                        k = MERGE0 + 3 * d
                        m = i * 2 + d
                        uu = i * 6 + (u + k)
                        if d == 0:
                            pe.wait_ge(cv_done, c * G + G)
                        pe.wait_ge(gate_a, m + (c * MT + 1))
                        unit(uu, k, proj[0])
                        if d == 0:
                            pe.wait_ge(b_split, c * G + G)
                        pe.wait_ge(gate_b, m + (c * MT + 1))
                        unit(uu + 1, k + 1, proj[1])
                        if before is not None and d == 0:
                            turn_y(i + before * TT)
                        pe.wait_ge(unit_ready, uu + 3)
                        pe.wait_ge(a_split, c * G + G)
                        pe.wait_ge(branches_read, m + (c * MT + 1))
                        s = (k + 2) % 2
                        for dst, vh, vl, k0 in ((ps_a, ah, al, 0), (ps_b, bh, bl, G)):
                            for g in range(G):
                                last = three(dst[:, :], uh[s][:, k0 + g, :], ul[s][:, k0 + g, :],
                                             vh[:, g, :], vl[:, g, :], g == 0, g == G - 1)
                        last.then_inc(unit_done, 1)
                        if before is not None:
                            (count if d else router)(i + before * TT)

            def back(c):
                u = c * UNITS + BACK0
                with pe.Fori(0, 2) as h:
                    for v in range(4):
                        s = v % 2
                        pe.wait_ge(unit_ready, h * 4 + (u + v + 1))
                        pe.wait_ge(merged, c * MT + 2 * v + 2)
                        vh = uh[s][:, :, :].rearrange("p (a b) n -> p a (b n)", a=2)
                        vl = ul[s][:, :, :].rearrange("p (a b) n -> p a (b n)", a=2)
                        for i in range(TT):
                            if v == 0:
                                pe.wait_ge(x2_added, h * 4 + (c * 8 + i + 1))
                            if v == 0 and i == TT - 1:
                                pe.wait_ge(dest_ready, c * TT + 1)
                            for kk in range(2):
                                kd = 2 * v + kk
                                tok = slice(i * P, (i + 1) * P)
                                last = three(banks[i][:, :], mh[:, kd, tok], ml[:, kd, tok],
                                             vh[:, kk, :], vl[:, kk, :], kd == 0, kd == KD - 1)
                            if v == 3 and i < TT - 1:
                                last.then_inc(wo_done, 1)
                        last.then_inc(unit_done, 1)
                        if v == 0:
                            pe.wait_ge(gate_a, c * MT + MT + 1)
                            pe.wait_ge(gate_b, c * MT + MT + 1)
                        if v % 2 == 0:
                            turn_x(h * 2 + ((c + 1) * TT + v // 2), v // 2)

            def tail(c):
                n = c * TT
                sums = [proj[0], proj[1], ps_a[:, :], ps_b[:, :]]

                def half(g, parts=range(4)):
                    i, h = TAIL_HALVES[g]
                    for v in parts:
                        pe.wait_ge(unit_ready, c * UNITS + BACK0 + h * 4 + v + 1)
                        if g == 0:
                            pe.wait_ge(merged, c * MT + 2 * v + 2)
                        if g < 4 and v == 0:
                            pe.wait_ge((gate_a, gate_b, branches_read, branches_read)[g],
                                       c * MT + MT + 1)
                        elif v == 0:
                            pe.wait_ge(x2_added, c * 8 + TT + g - 3)
                        vh, vl = tail_unit(h * 4 + v)
                        for kk in range(2):
                            kd = 2 * v + kk
                            tok = slice(i * P, (i + 1) * P)
                            last = three(sums[g % 4], mh[:, kd, tok], ml[:, kd, tok],
                                         vh[:, kk, :], vl[:, kk, :], kd == 0, kd == KD - 1)
                    if v == 3:
                        last.then_inc(half_done, 1)

                for v in range(4):
                    for g in range(3):
                        half(g, (v,))
                half(3)
                half(4)
                turn_y(n)
                half(5)
                router(n)
                turn_y(n + 1)
                half(6, (0, 1))
                count(n)
                half(6, (2, 3))
                router(n + 1)
                turn_y(n + 2)
                half(7)
                for q in (1, 2):
                    count(n + q)
                    router(n + q + 1)
                    if q == 1:
                        turn_y(n + 3)
                count(n + 3)

            pe.sem_inc(logits_done, 1)
            pe.sem_inc(ranked, 1)
            pe.wait_ge(ident_in_sb, 16)
            for i in range(TT):
                pe.wait_ge(x_normed, i + 1)
                wait(pe, x_split, i - 1)
                for kd in range(KD):
                    last = nc.tensor.transpose(first_turned(i, kd // 4)[:, kd % 4, :],
                                               xin[i % 2][:, kd * P:(kd + 1) * P], ident[:, :])
                last.then_inc(x_turned, 1)
            pe.wait_ge(const_in, NCONST)
            pe.wait_ge(grp_split, 1)
            front(0)
            back(0)
            with pe.Fori(0, NCH - 2) as b:
                front(b + 1, b)
                back(b + 1)
            front(NCH - 1, NCH - 2)
            tail(NCH - 1)
            pe.wait_ge(tab_a, 1)
            nc.tensor.matmul(banks[0][0:NE, 0:1], over[:, 0:NE], nblk[:, :], start=True, stop=True
                             ).then_inc(tab_b, 1)
            pe.wait_ge(tab_c, 1)
            nc.tensor.matmul(banks[1][0:1, 0:NB], ones[0:NE, 0:1], over[:, :], start=True, stop=True)
            nc.tensor.matmul(banks[2][0:1, 0:NB], nblk[:, 0:1], over[:, :], start=True, stop=True
                             ).then_inc(tab_d, 1)

        @block.scalar
        def _(act):
            def copy(dst, src, **kw):
                return nc.scalar.activation(dst, src, ACT.Copy, **kw)

            def split_hi(u, k):
                s = k % 2
                if isinstance(u, int):
                    act.wait_ge(raw_in[s], 16 * (u // 2 + 1))
                wait(act, unit_done, u - 1)
                copy(uh[s][:, :, :].rearrange("p k n -> p (k n)"), raw[:, s, :]).then_inc(unit_hi, 1)

            def split_next(base, k):
                u = base + k + 2
                if not isinstance(u, int):
                    act.wait_ge(raw_in[k % 2], 8 * base + 16 * (k // 2 + 2))
                split_hi(u, k)

            def square(src, col, signal):
                act.drain()
                nc.scalar.activation(junk[:, :], src, ACT.Square, scale=float(D) ** -0.5,
                                     accum_out=mean[:, col]).then_inc(signal, 1)

            def x_high(n, tok):
                act.wait_ge(x_turned, n + 1)
                copy(hh[:, :, tok], ps_t8[:, :, :]).then_inc(x_hi, 1)

            def y_square(i, added, col=YCOL):
                act.wait_ge(x2_added, added)
                src = x2[:, i, :] if isinstance(i, int) else x2[:, ds1(i), :].rearrange(
                    "p a d -> p (a d)")
                carry(act, marks)
                square(src, slice(col, col + 1), y_mean)

            def y_copy(n):
                act.wait_ge(y_turned, n + 1)
                act.wait_ge(logits_done, n + 1)
                for b in range(2):
                    last = copy(h2t[:, 4 * b:4 * b + 4, :].rearrange("p k t -> p (k t)"), banks[b][:, :])
                last.then_inc(y_copied, 1)
                act.dma_start(h2_tiles[n] if isinstance(n, int) else
                              h2_tiles[ds1(n)].rearrange("a p d -> p (a d)"),
                              h2[:, :]).then_inc(h2_out, 16)

            def score(n):
                act.wait_ge(logits_done, n + 2)
                act.wait_ge(masked, n + 1)
                nc.scalar.activation(sc[:, :], banks[2][:, 0:NE], ACT.Sigmoid).then_inc(scored, 1)

            def a_high(c, g):
                act.wait_ge(mixed_done, c * G + g + 1)
                copy(ah[:, g, :], ps_a[:, :], scale=pscale[:, g:g + 1]).then_inc(a_hi, 1)

            def front(c, before=None):
                base = c * UNITS
                for q in range(G):
                    k = 4 * q
                    act.wait_ge(unit_done, base + k + 1)
                    wait(act, pooled_split, c * G + q)
                    copy(ubuf[:, 0:HALO], uhalo[:, q, :])
                    copy(ubuf[:, HALO:], proj[0])
                    act.drain()
                    copy(uhalo[:, q, :], proj[0][:, T - HALO:T]).then_inc(u_copied, 1)
                    split_next(base, k)
                    act.wait_ge(unit_done, base + k + 2)
                    wait(act, cv_done, c * G + q)
                    copy(csb[:, :], proj[1]).then_inc(c_copied, 1)
                    split_next(base, k + 1)
                    split_next(base, k + 2)
                    a_high(c, q)
                    split_next(base, k + 3)
                with act.Fori(0, MT // 2) as i:
                    if before is not None:
                        y_square(i, c * 8 + 4)
                    for d in range(2):
                        k = MERGE0 + 3 * d
                        m = i * 2 + d
                        ub = i * 6 + base
                        for j, (sig, bank, sm) in enumerate(((siga, 0, gate_a), (sigb, 1, gate_b))):
                            act.wait_ge(unit_done, ub + (k + j + 1))
                            act.wait_ge(branches_read, m + (c * MT + 1))
                            nc.scalar.activation(sig[:, :], proj[bank], ACT.Sigmoid,
                                                 bias=bg[:, bass.ds(m + j * MT, 1)]).then_inc(sm, 1)
                            act.wait_ge(raw_in[(k + j) % 2], 8 * ub + 16 * ((k + j) // 2 + 2))
                            split_hi(ub + (k + j + 2), k + j)
                        if before is not None and d == 0:
                            y_copy(i + before * TT)
                        act.wait_ge(raw_in[k % 2], 8 * ub + 16 * ((k + 2) // 2 + 2))
                        split_hi(ub + (k + 4), k + 2)
                        if before is not None and d == 0:
                            score(i + before * TT)

            def back(c):
                base = c * UNITS + BACK0
                with act.Fori(0, 2) as h:
                    for v in range(4):
                        ub = h * 4 + base
                        act.wait_ge(raw_in[v % 2], 8 * ub + 16 * (v // 2 + 2))
                        split_hi(ub + (v + 2), v)
                        if v % 2 == 0:
                            s = v // 2
                            x_high(h * 2 + ((c + 1) * TT + s), bass.ds(h * (2 * P) + s * P, P))
                            act.wait_ge(x_in[1 - s], h * 16 + ((c + 1) * (8 * TT) + 16 * (s - 1)))
                            carry(act, marks)
                            square(xin[1 - s][:, :], bass.ds(h * 2 + s + 1, 1), x_mean)

            act.wait_ge(halo_zero, 1)
            nc.scalar.activation(junk[:, 0:HALO], uhalo[:, 0, :], ACT.Square)
            act.sem_inc(gate_a, 1)
            act.sem_inc(gate_b, 1)
            act.sem_inc(y_copied, 1)
            act.sem_inc(scored, 1)
            for i in range(TT):
                act.wait_ge(first_in[i] if i < 2 else res_in, 16)
                carry(act, marks)
                square(x2[:, i, :], slice(i, i + 1), x_mean)
            for i in range(TT):
                act.wait_ge(x_turned, i + 1)
                for half in range(2):
                    last = copy(hh[:, 4 * half:4 * half + 4, i * P:(i + 1) * P], first_turned(i, half))
                last.then_inc(x_hi, 1)
                if i < 2:
                    split_hi(i, i)
            act.wait_ge(const_in, NCONST)
            copy(wgh[:, :, :], wg[:, :, :]).then_inc(grp_hi, 1)
            act.wait_ge(rows_made, 1)
            act.dma_start(h2_dram[S:S + P, :], h2[:, :]).then_inc(h2_out, 16)
            act.wait_ge(x_in[0], 16)
            carry(act, marks)
            square(xin[0][:, :], slice(TT, TT + 1), x_mean)
            front(0)
            back(0)
            with act.Fori(0, NCH - 2) as b:
                front(b + 1, b)
                back(b + 1)
            front(NCH - 1, NCH - 2)
            c = NCH - 1
            n = c * TT
            u = c * UNITS + BACK0
            act.wait_ge(unit_done, u)
            for w in range(2, 8):
                act.wait_ge(raw_in[w % 2], 16 * ((u + w) // 2 + 1))
                copy(tail_unit(w)[0], raw[:, w % 2, :].rearrange("p (a n) -> p a n", a=2)
                     ).then_inc(unit_hi, 1)

            def tail_square(q):
                g = TAIL_HALVES.index((q, 1))
                y_square(q, c * 8 + TT + g + 1, YTAIL + q)

            tail_square(0)
            tail_square(1)
            y_copy(n)
            tail_square(2)
            score(n)
            y_copy(n + 1)
            score(n + 1)
            y_copy(n + 2)
            tail_square(3)
            score(n + 2)
            y_copy(n + 3)
            score(n + 3)
            act.wait_ge(h2_out, 16 * NT + 16)

        @block.vector
        def _(dve):
            V = nc.vector

            def split_lo(u, k):
                s = k % 2
                dve.wait_ge(unit_hi, u + 1)
                V.tensor_tensor(ul[s][:, :, :].rearrange("p k n -> p (k n)"), raw[:, s, :],
                                uh[s][:, :, :].rearrange("p k n -> p (k n)"), ALU.subtract
                                ).then_inc(unit_ready, 1)

            def x_scale(n, src, s, col):
                dve.wait_ge(x_rstd, n + 1)
                V.scalar_tensor_tensor(out=xin[s][:, :], in0=src, scalar=rstd[:, col],
                                       in1=gmix[:, :], op0=ALU.mult, op1=ALU.mult
                                       ).then_inc(x_normed, 1)

            def x_low(n, tok):
                dve.wait_ge(x_hi, n + 1)
                V.tensor_tensor(hl[:, :, tok], ps_t8[:, :, :], hh[:, :, tok], ALU.subtract
                                ).then_inc(x_split, 1)

            def y_scale(i, n, col=YCOL):
                dve.wait_ge(y_rstd, n + 1)
                dve.wait_ge(h2_out, n * 16 + 16)
                src = x2[:, i, :] if isinstance(i, int) else x2[:, ds1(i), :].rearrange(
                    "p a d -> p (a d)")
                V.scalar_tensor_tensor(out=h2[:, :], in0=src, scalar=rstd[:, col:col + 1],
                                       in1=gffn[:, :], op0=ALU.mult, op1=ALU.mult
                                       ).then_inc(y_normed, 1)

            def pool_group(c, g):
                w = WINDOWS[g]
                dve.wait_ge(u_copied, c * G + g + 1)
                src, width, turn = ubuf, 1, 0
                while width < w:
                    lo = 2 * width - 1 + (HALO - w)
                    V.tensor_tensor(win[turn][:, lo:], src[:, lo:], src[:, lo - width:HALO + T - width],
                                    ALU.add)
                    dve.drain()
                    src, width, turn = win[turn], 2 * width, 1 - turn
                V.scalar_tensor_tensor(out=pooled[:, :], in0=src[:, HALO:], scalar=1.0 / w,
                                       in1=ubuf[:, HALO:], op0=ALU.mult, op1=ALU.subtract)
                if isinstance(c, int) and c == 0:
                    dve.drain()
                    V.tensor_tensor(src[:, HALO:2 * HALO], src[:, HALO:2 * HALO], icnt[:, g, :], ALU.mult)
                    dve.drain()
                    V.tensor_tensor(pooled[:, 0:HALO], src[:, HALO:2 * HALO], ubuf[:, HALO:2 * HALO],
                                    ALU.subtract)
                dve.drain()
                wait(dve, mixed_done, c * G + g)
                V.tensor_copy(ph[:, :], pooled[:, :])
                dve.drain()
                V.tensor_tensor(pl[:, :], pooled[:, :], ph[:, :], ALU.subtract).then_inc(pooled_split, 1)
                dve.drain()

            def a_low(c, g):
                dve.wait_ge(a_hi, c * G + g + 1)
                V.scalar_tensor_tensor(out=al[:, g, :], in0=ps_a[:, :], scalar=pscale[:, g:g + 1],
                                       in1=ah[:, g, :], op0=ALU.mult, op1=ALU.subtract
                                       ).then_inc(a_split, 1)

            def conv_cv(c, q):
                dve.wait_ge(unit_done, c * UNITS + 4 * q + 3)
                dve.wait_ge(c_copied, c * G + q + 1)
                V.tensor_copy(cv[:, 0:2], cvhalo[:, q, :])
                V.tensor_tensor(cv[:, 2:], csb[:, :], proj[0], ALU.mult).then_inc(cv_done, 1)
                dve.drain()
                V.tensor_copy(cvhalo[:, q, :], cv[:, T:T + 2])
                V.tensor_scalar(tap, cv[:, 0:T], cw[:, q, 0:1], None, ALU.mult)
                for j in (1, 2):
                    dve.drain()
                    V.scalar_tensor_tensor(out=tap, in0=cv[:, j:j + T], scalar=cw[:, q, j:j + 1],
                                           in1=tap, op0=ALU.mult, op1=ALU.add)
                dve.drain()

            def conv_b(c, q):
                dve.wait_ge(unit_done, c * UNITS + 4 * q + 4)
                V.tensor_tensor(bcv, proj[1], tap, ALU.mult)
                dve.drain()
                V.tensor_copy(bh[:, q, :], bcv)
                dve.drain()
                V.tensor_tensor(bl[:, q, :], bcv, bh[:, q, :], ALU.subtract).then_inc(b_split, 1)
                dve.drain()

            def choose(n, pay=pay, reused=True):
                dve.wait_ge(scored, n + 2)
                V.tensor_tensor(biased[:, :], sc[:, :], rbias[:, :], ALU.add)
                dve.drain()
                V.max(top[:, :], biased[:, :])
                dve.drain()
                V.max_index(idx[:, :], top[:, :], biased[:, :])
                dve.drain()
                V.tensor_copy(idxf[:, :], idx[:, :])
                dve.drain()
                V.tensor_tensor(hot[:, :, :], iota_e[:, None, :].to_broadcast([P, TOPK, NE]),
                                idxf[:, :, None].to_broadcast([P, TOPK, NE]), ALU.is_equal)
                dve.drain()
                dve.wait_ge(ranked, n + 1)
                V.tensor_tensor(hotx, hot[:, :, :], sc[:, None, :].to_broadcast([P, TOPK, NE]), ALU.mult)
                V.tensor_reduce(mask[:, :], hot[:, :, :].rearrange("p k e -> p e k"), AX.X, ALU.add
                                ).then_inc(masked, 1)
                dve.drain()
                V.tensor_reduce(w8[:, :], hotx, AX.X, ALU.add)
                dve.drain()
                V.tensor_reduce(den[:, :], w8[:, :], AX.X, ALU.add)
                dve.drain()
                V.reciprocal(den[:, :], den[:, :])
                dve.drain()
                if reused:
                    dve.wait_ge(list_out, n * (16 * TOPK) + 16)
                V.tensor_copy(pay[:, :, 0], tokid[:, (slice(n, n + 1) if isinstance(n, int) else ds1(n))]
                              .to_broadcast([P, TOPK]))
                V.tensor_scalar(pay[:, :, :].bitcast(F32)[:, :, 1], w8[:, :], den[:, 0:1], SCALE,
                                ALU.mult, ALU.mult)
                dve.drain()

            def place(n, dest=dest):
                dve.wait_ge(ranked, n + 2)
                V.tensor_tensor(rank[:, :], banks[3][:, 0:NE], taken[:, :], ALU.add)
                dve.drain()
                V.tensor_tensor(taken[:, :], taken[:, :], banks[3][:, NE:2 * NE], ALU.add)
                V.tensor_tensor(total[:, :], total[:, :], banks[3][0:NE, 2 * NE:2 * NE + 1], ALU.add)
                V.tensor_tensor(hotx, hot[:, :, :], rank[:, None, :].to_broadcast([P, TOPK, NE]), ALU.mult)
                dve.drain()
                V.tensor_reduce(r8[:, :], hotx, AX.X, ALU.add)
                dve.drain()
                V.scalar_tensor_tensor(out=dest[:, :], in0=idxf[:, :], scalar=float(ROWS),
                                       in1=r8[:, :], op0=ALU.mult, op1=ALU.add).then_inc(dest_ready, 1)
                dve.drain()

            def front(c, before=None):
                base = c * UNITS
                last_chunk = isinstance(before, int)
                for q in range(G):
                    k = 4 * q
                    split_lo(base + k + 2, k)
                    pool_group(c, q)
                    split_lo(base + k + 3, k + 1)
                    split_lo(base + k + 4, k + 2)
                    conv_cv(c, q)
                    split_lo(base + k + 5, k + 3)
                    conv_b(c, q)
                    a_low(c, q)
                with dve.Fori(0, MT // 2) as i:
                    if before is not None:
                        y_scale(i, i + before * TT)
                    for d in range(2):
                        k = MERGE0 + 3 * d
                        m = i * 2 + d
                        ub = i * 6 + base
                        split_lo(ub + (k + 2), k)
                        if before is not None and d == 1:
                            choose(i + before * TT)
                        split_lo(ub + (k + 3), k + 1)
                        split_lo(ub + (k + 4), k + 2)
                        if before is not None and d == 1 and not last_chunk:
                            place(i + before * TT)
                        dve.wait_ge(gate_a, m + (c * MT + 2))
                        dve.wait_ge(gate_b, m + (c * MT + 2))
                        dve.wait_ge(unit_done, ub + (k + 3))
                        V.tensor_tensor(m1, siga[:, :], ps_a[:, :], ALU.mult)
                        V.tensor_tensor(m2, sigb[:, :], ps_b[:, :], ALU.mult).then_inc(branches_read, 1)
                        dve.drain()
                        V.tensor_tensor(m1, m1, m2, ALU.add)
                        dve.drain()
                        mm = mh[:, ds1(m), :].rearrange("p a t -> p (a t)")
                        V.tensor_copy(mm, m1)
                        dve.drain()
                        V.tensor_tensor(ml[:, ds1(m), :].rearrange("p a t -> p (a t)"), m1, mm,
                                        ALU.subtract).then_inc(merged, 1)
                        dve.drain()
                        if d == 1 and last_chunk:
                            place(i + before * TT)

            def back(c):
                base = c * UNITS + BACK0
                with dve.Fori(0, 2) as h:
                    for v in range(4):
                        ub = h * 4 + base
                        s = v // 2
                        n = h * 2 + ((c + 1) * TT + s)
                        if v == 3:
                            dve.wait_ge(res_in, (c + 1) * 16)
                            for i in range(TT):
                                if i < TT - 1:
                                    dve.wait_ge(wo_done, h * 3 + (c * 6 + i + 1))
                                else:
                                    dve.wait_ge(unit_done, ub + 4)
                                part = x2[:, i, bass.ds(h * (D // 2), D // 2)]
                                V.tensor_tensor(part, part, banks[i][:, :], ALU.add
                                                ).then_inc(x2_added, 1)
                        split_lo(ub + (v + 2), v)
                        if v % 2 == 0:
                            x_low(n, bass.ds(h * (2 * P) + s * P, P))
                        else:
                            x_scale(n + 1, xin[1 - s][:, :], 1 - s, bass.ds(h * 2 + s + 1, 1))

            dve.sem_inc(branches_read, 1)
            dve.sem_inc(masked, 1)
            dve.sem_inc(dest_ready, 1)
            dve.sem_inc(x2_added, TT)
            V.memset(uhalo[:, :, :], 0.0)
            V.memset(cvhalo[:, :, :], 0.0)
            V.memset(taken[:, :], 0.0)
            V.memset(total[:, :], 0.0).then_inc(halo_zero, 1)
            dve.wait_ge(gmix_in, 16)

            def first_low(i):
                dve.wait_ge(x_hi, i + 1)
                tok = slice(i * P, (i + 1) * P)
                for half in range(2):
                    ks = slice(4 * half, 4 * half + 4)
                    last = V.tensor_tensor(hl[:, ks, tok], first_turned(i, half), hh[:, ks, tok],
                                           ALU.subtract)
                last.then_inc(x_split, 1)

            for i in range(TT):
                if i >= 2:
                    dve.wait_ge(x_turned, i - 1)
                x_scale(i, x2[:, i, :], i % 2, slice(i, i + 1))
                if i >= 1:
                    first_low(i - 1)
                if i >= 2:
                    split_lo(i - 2, i - 2)
            first_low(TT - 1)
            dve.wait_ge(const_in, NCONST)
            dve.wait_ge(grp_hi, 1)
            V.tensor_tensor(wgl[:, :, :], wg[:, :, :], wgh[:, :, :], ALU.subtract).then_inc(grp_split, 1)
            x_scale(TT, xin[0][:, :], 0, slice(TT, TT + 1))
            front(0)
            back(0)
            with dve.Fori(0, NCH - 2) as b:
                front(b + 1, b)
                back(b + 1)
            front(NCH - 1, NCH - 2)
            c = NCH - 1
            n = c * TT
            sums = [proj[0], proj[1], ps_a[:, :], ps_b[:, :]]
            dve.wait_ge(res_in, NCH * 16)

            def low(w):
                dve.wait_ge(unit_hi, c * UNITS + BACK0 + w + 1)
                hi_, lo_ = tail_unit(w)
                V.tensor_tensor(lo_, raw[:, w % 2, :].rearrange("p (a n) -> p a n", a=2), hi_,
                                ALU.subtract).then_inc(unit_ready, 1)

            def add_half(g):
                i, h = TAIL_HALVES[g]
                dve.wait_ge(half_done, g + 1)
                part = x2[:, i, h * (D // 2):(h + 1) * (D // 2)]
                V.tensor_tensor(part, part, sums[g % 4], ALU.add).then_inc(x2_added, 1)

            def tail_scale(q):
                y_scale(q, n + q, YTAIL + q)

            def tail_choose(q):
                choose(n + q, tail_pay[:, q, :, :], False)

            def tail_place(q):
                place(n + q, tail_dest[:, q, :])

            for w in range(2, 6):
                low(w)
            add_half(0)
            low(6)
            add_half(1)
            low(7)
            add_half(2)
            add_half(3)
            tail_scale(0)
            add_half(4)
            add_half(5)
            tail_scale(1)
            tail_choose(0)
            tail_place(0)
            add_half(6)
            tail_scale(2)
            tail_choose(1)
            add_half(7)
            tail_place(1)
            tail_scale(3)
            tail_choose(2)
            tail_place(2)
            tail_choose(3)
            tail_place(3)

            V.tensor_scalar(total[:, :], total[:, :], float(P - 1), None, ALU.add)
            dve.drain()
            V.tensor_copy(nblk_i[:, :], total[:, :])
            dve.drain()
            V.tensor_scalar(nblk_i[:, :], nblk_i[:, :], 7, None, ALU.logical_shift_right)
            V.tensor_tensor(over[:, 0:NE], tri[0:NE, 0:NE], ident[0:NE, 0:NE], ALU.add)
            dve.drain()
            V.tensor_scalar(nblk[:, :], nblk_i[:, :], 1, None, ALU.max).then_inc(tab_a, 1)
            dve.wait_ge(tab_b, 1)
            V.tensor_copy(end_i[:, :], banks[0][0:NE, 0:1])
            dve.drain()
            V.tensor_scalar(end_i[:, :], end_i[:, :], 1, None, ALU.bitwise_and)
            dve.drain()
            V.tensor_copy(odd[:, :], end_i[:, :])
            dve.drain()
            V.tensor_tensor(odd[:, :], odd[:, :], ident[0:NE, NE - 1:NE], ALU.mult)
            dve.drain()
            V.tensor_tensor(bend[:, :], banks[0][0:NE, 0:1], odd[:, :], ALU.add)
            V.tensor_tensor(nblk[:, :], nblk[:, :], odd[:, :], ALU.add)
            dve.drain()
            V.tensor_scalar(over[:, :], iota_j[:, :], bend[:, 0:1], None, ALU.is_ge).then_inc(tab_c, 1)
            dve.wait_ge(tab_d, 1)
            eid_ps, first_ps = banks[1][0:1, 0:NB], banks[2][0:1, 0:NB]
            V.tensor_copy(table[:, 0:NB], eid_ps)
            V.tensor_copy(eid_f[:, :], eid_ps)
            V.tensor_tensor(row_f[:, :], iota_j[0:1, :], first_ps, ALU.subtract)
            V.tensor_tensor(first_f[:, :], first_ps, iota_j[0:1, :], ALU.is_equal)
            V.tensor_scalar(over[0:1, :], eid_ps, NE - 0.5, None, ALU.is_lt)
            V.tensor_copy(table[:, 3 * NB:3 * NB + 1], first_ps[:, NB - 1:NB])
            dve.drain()
            V.scalar_tensor_tensor(out=row_f[:, :], in0=eid_f[:, :], scalar=float(ROWS // P),
                                   in1=row_f[:, :], op0=ALU.mult, op1=ALU.add)
            V.tensor_scalar(eid_f[:, :], eid_f[:, :], 1.0, None, ALU.add)
            V.tensor_tensor(first_f[:, :], first_f[:, :], over[0:1, :], ALU.mult)
            V.tensor_scalar(table[:, 3 * NB + 1:3 * NB + 2], table[:, 3 * NB:3 * NB + 1], 1, None,
                            ALU.logical_shift_right)
            V.tensor_scalar(bst_f[:, :], over[0:1, :], -float(ROWS // P), float(ROWS // P),
                            ALU.mult, ALU.add)
            dve.drain()
            V.tensor_tensor(table[:, 2 * NB:3 * NB], first_f[:, :], eid_f[:, :], ALU.mult)
            V.tensor_tensor(row_f[:, :], row_f[:, :], bst_f[:, :], ALU.add)
            dve.drain()
            V.tensor_scalar(table[:, NB:2 * NB], row_f[:, :], float(LISTS * ROWS // P - 1), None, ALU.min)
            dve.drain()


def mixture(nc, sem, marks, table, raw, piece_in, acc, h2_dram, lists, experts, ident_in, g_final, out):
    acc_tiles = acc.rearrange("(n p) d -> n p d", p=P)
    out_tiles = out.rearrange("(n p) d -> n p d", p=P)
    list_blocks = lists.rearrange("(b p) two -> b p two", p=P)
    KP = KD // 2

    with ExitStack() as ctx:
        def sb(name, shape, dt=F32):
            return ctx.enter_context(nc.sbuf_tensor(name, shape, dt))

        ident = sb("eye2", [P, P])
        wh = sb("expert_hi", [P, 2 * PIECES, D], F32R)
        wl = sb("expert_lo", [P, 2 * PIECES, D], F32R)
        gidx = [sb(f"gidx{s}", [P, 2], I32) for s in range(2)]
        sidx = [sb(f"sidx{s}", [P, 2], I32) for s in range(2)]
        xs = [sb(f"xs{s}", [P, D]) for s in range(2)]
        xh = [sb(f"xh{s}", [P, KD, P], F32R) for s in range(2)]
        xl = [sb(f"xl{s}", [P, KD, P], F32R) for s in range(2)]
        sg = sb("sg", [P, H])
        hid = sb("hid", [P, H])
        hth = [sb(f"hth{s}", [P, 2, P], F32R) for s in range(2)]
        htl = [sb(f"htl{s}", [P, 2, P], F32R) for s in range(2)]
        y = [sb(f"y{s}", [P, D]) for s in range(2)]
        gfin = sb("gfin", [P, D])
        junk = sb("junk2", [P, D], BF16)
        mean = sb("mean2", [P, 2])
        rstd = sb("rstd2", [P, 2])
        minus_half = sb("minus_half2", [P, 1])

        ps_x = ctx.enter_context(nc.psum_tensor("ps_x", [P, KD, P], F32))
        ps_gu = [ctx.enter_context(nc.psum_tensor(f"ps_gu{s}", [P, 512], F32)) for s in range(2)]
        ps_h = ctx.enter_context(nc.psum_tensor("ps_h", [P, 2, P], F32))
        ps_y = ctx.enter_context(nc.psum_tensor("ps_y", [P, D], F32))

        ident_ready = sem("ident_ready")
        gfin_in = sem("gfin_in")
        piece_hi = sem("piece_hi")
        piece_ready = sem("piece_ready")
        gidx_in = [sem(f"gidx_in{s}") for s in range(2)]
        sidx_in = [sem(f"sidx_in{s}") for s in range(2)]
        xs_in = [sem(f"xs_in{s}") for s in range(2)]
        xs_turned = sem("xs_turned")
        xs_hi = sem("xs_hi")
        xs_split = sem("xs_split")
        gu_done = sem("gu_done")
        gate_sig = sem("gate_sig")
        hid_ready = sem("hid_ready")
        hid_turned = sem("hid_turned")
        hid_hi = sem("hid_hi")
        hid_split = sem("hid_split")
        down_done = sem("down_done")
        y_ready = sem("y_ready")
        y_out = [sem(f"y_out{s}") for s in range(2)]
        acc_in = [sem(f"acc_in{s}") for s in range(2)]
        z_added = sem("z_added")
        z_mean = sem("z_mean")
        z_rstd = sem("z_rstd")
        z_normed = sem("z_normed")

        SHARED_PAIRS = SHARED_BLOCKS // 2 - 1
        block = ctx.enter_context(nc.Block())

        def pairs(eng):
            return eng.value_load(table[0:1, 3 * NB + 1:3 * NB + 2], min_val=NE // 2,
                                  max_val=NBMAX // 2)

        def expert_of(eng, j):
            at = slice(j, j + 1) if isinstance(j, int) else ds1(j)
            return eng.value_load(table[0:1, at], min_val=0, max_val=NE)

        def to_split(eng, j):
            at = bass.ds(j + 2 * NB, 1)
            return eng.value_load(table[0:1, at], min_val=0, max_val=NE)

        @block.sync
        def _(sp):
            def list_rows(j):
                at = slice(NB + j, NB + j + 1) if isinstance(j, int) else bass.ds(j + NB, 1)
                row = sp.value_load(table[0:1, at], min_val=0, max_val=(LISTS * ROWS // P - 1))
                return list_blocks[ds1(row)].rearrange("a p two -> p (a two)")

            def gather_list(j, s):
                sp.dma_start(gidx[s][:, :], list_rows(j)).then_inc(gidx_in[s], 16)

            def scatter_list(j, s):
                sp.dma_start(sidx[s][:, :], list_rows(j)).then_inc(sidx_in[s], 16)

            def load_expert(e):
                for p in range(PIECES):
                    wait(sp, piece_ready, (e - 1) * PIECES + p + 1)
                    src = experts[e] if isinstance(e, int) else experts[ds1(e % (NE + 1))].rearrange(
                        "a p f d -> p (a f) d")
                    sp.dma_start(raw[:, p, :], src[:, p, :]).then_inc(piece_in[p], 16)

            sp.dma_start(ident[:, :], ident_in).then_inc(ident_ready, 16)
            for j in range(2):
                gather_list(j, j)
            for j in range(2):
                sp.wait_ge(xs_in[j], 16)
                gather_list(j + 2, j)
            scatter_list(0, 0)
            load_expert(1)
            sp.dma_start(gfin[:, :], g_final).then_inc(gfin_in, 16)
            sp.wait_ge(xs_in[0], 32)
            gather_list(4, 0)
            load_expert(2)
            n = pairs(sp)
            with sp.Fori(0, n) as i:
                for d in (1, 2):
                    j = i * 2 + d
                    s = d % 2
                    if d == 1:
                        sp.wait_ge(y_out[1], i * 16 + 16)
                    else:
                        sp.wait_ge(y_out[0], i * 16 + 32)
                    scatter_list(j, s)
                    sp.wait_ge(xs_in[s], i * 16 + (32 if d == 1 else 48))
                    gather_list(j + 4, s)
                    e = to_split(sp, j)
                    with sp.If(e > 0):
                        load_expert(e + 1)
            sp.wait_ge(y_out[0], n * 16 + 16)
            carry(sp, marks)
            sp.wait_ge(y_out[1], n * 16 + 16)
            carry(sp, marks)
            sp.dma_start(y[0][:, :], acc_tiles[0]).then_inc(acc_in[0], 16)
            with sp.Fori(0, SHARED_PAIRS) as m:
                i = m + n
                for d in (1, 2):
                    s = d % 2
                    sp.wait_ge(xs_in[s], i * 16 + (32 if d == 1 else 48))
                    gather_list(i * 2 + (d + 4), s)
                    sp.wait_ge(y_out[s], i * 16 + 16 * d)
                    sp.dma_start(y[s][:, :], acc_tiles[ds1(m * 2 + d)].rearrange("a p d -> p (a d)")
                                 ).then_inc(acc_in[s], 16)
            sp.wait_ge(y_out[1], (n + SHARED_PAIRS) * 16 + 16)
            sp.dma_start(y[1][:, :], acc_tiles[NT - 1]).then_inc(acc_in[1], 16)
            for p in range(PIECES):
                sp.wait_ge(piece_in[p], 16 * (NE + 2))
            for s in range(2):
                sp.wait_ge(sidx_in[s], n * 16 + 16 * (1 - s))
                carry(sp, marks)
                sp.wait_ge(gidx_in[s], (n + SHARED_PAIRS) * 16 + (48 if s == 0 else 32))
                carry(sp, marks)

        @block.gpsimd
        def _(pool):
            def gather(s):
                nc.gpsimd.indirect_dma_start(
                    xs[s][:, :], None, h2_dram,
                    bass.IndirectOffsetOnAxis(ap=gidx[s][:, 0:1], axis=0)).then_inc(xs_in[s], 16)

            def scatter(s):
                nc.gpsimd.indirect_dma_start(
                    acc, bass.IndirectOffsetOnAxis(ap=sidx[s][:, 0:1], axis=0), y[s][:, :], None,
                    compute_op=ALU.add).then_inc(y_out[s], 16)

            nc.gpsimd.memset(minus_half[:, :], -0.5)
            for j in range(4):
                if j == 2:
                    for s in range(2):
                        pool.dma_start(y[s][:, 0:P], h2_dram[S:S + P, 0:P]).then_inc(y_out[s], 16)
                pool.wait_ge(gidx_in[j % 2], 16 * (j // 2 + 1))
                if j >= 2:
                    pool.wait_ge(xs_turned, j - 1)
                gather(j % 2)
            n = pairs(pool)
            with pool.Fori(0, n) as i:
                for d in (1, 2):
                    s = d % 2
                    pool.wait_ge(gidx_in[1 - s], i * 16 + 48)
                    pool.wait_ge(xs_turned, i * 2 + (d + 2))
                    carry(pool, marks)
                    gather(1 - s)
                    pool.wait_ge(y_ready, i * 2 + (d + 1))
                    pool.wait_ge(sidx_in[1 - s], i * 16 + 16)
                    pool.wait_ge(y_out[s], i * 16 + 16 * d)
                    carry(pool, marks)
                    scatter(1 - s)
            def finish(t, s):
                pool.wait_ge(z_mean, t + 1)
                carry(pool, marks)
                inverse_root(nc, pool, rstd[:, s:s + 1], mean[:, s:s + 1], minus_half
                             ).then_inc(z_rstd, 1)
                pool.wait_ge(z_normed, t + 1)
                carry(pool, marks)
                at = out_tiles[t] if isinstance(t, int) else out_tiles[ds1(t)].rearrange(
                    "a p d -> p (a d)")
                pool.dma_start(at, y[s][:, :]).then_inc(y_out[s], 16)

            with pool.Fori(0, SHARED_PAIRS) as m:
                i = m + n
                for d in (1, 2):
                    s = d % 2
                    pool.wait_ge(gidx_in[1 - s], i * 16 + 48)
                    pool.wait_ge(xs_turned, i * 2 + (d + 2))
                    carry(pool, marks)
                    gather(1 - s)
                    finish(m * 2 + (d - 1), 1 - s)
            for t in (NT - 2, NT - 1):
                finish(t, t % 2)
            last = n + SHARED_PAIRS
            for s in range(2):
                pool.wait_ge(y_out[s], n * 16 + 16 * (1 + NT // 2))
                carry(pool, marks)
                pool.wait_ge(xs_in[s], last * 16 + 32)
                carry(pool, marks)

        @block.tensor
        def _(pe):
            def three(out_, sh, sl, vh, vl, first, last):
                nc.tensor.matmul(out_, sl, vh, start=first, stop=False)
                nc.tensor.matmul(out_, sh, vl, start=False, stop=False)
                return nc.tensor.matmul(out_, sh, vh, start=False, stop=last)

            def turn(j, s, filled):
                pe.wait_ge(xs_in[s], filled)
                wait(pe, xs_split, j)
                for kd in range(KD):
                    last = nc.tensor.transpose(ps_x[:, kd, :], xs[s][:, kd * P:(kd + 1) * P],
                                               ident[:, :])
                last.then_inc(xs_turned, 1)

            def piece(slot, p):
                if isinstance(slot, int):
                    return wh[:, slot * PIECES + p, :], wl[:, slot * PIECES + p, :]
                return tuple(w[:, ds1(slot * PIECES + p), :].rearrange("q a f -> q (a f)")
                             for w in (wh, wl))

            def gate_up(j, s, e, by_piece=False):
                pe.wait_ge(xs_split, j + 1)
                wait(pe, hid_ready, j - 1)
                if not by_piece:
                    pe.wait_ge(piece_ready, e * PIECES + KP)
                slot = e % 2
                for p in range(KP):
                    if by_piece:
                        pe.wait_ge(piece_ready, e * PIECES + p + 1)
                    ph_, pl_ = piece(slot, p)
                    for b in range(2):
                        kd = 2 * p + b
                        last = three(ps_gu[s][:, :], xh[s][:, kd, :], xl[s][:, kd, :],
                                     ph_[:, b * 512:(b + 1) * 512], pl_[:, b * 512:(b + 1) * 512],
                                     kd == 0, kd == KD - 1)
                last.then_inc(gu_done, 1)

            def down(j, s, e, shared=None):
                pe.wait_ge(hid_split, j + 1)
                if shared is not None:
                    pe.wait_ge(z_added, shared + 1)
                if shared is None or not isinstance(shared, int):
                    pe.wait_ge(y_ready, (j if shared is None else n * 2) + 1)
                pe.wait_ge(piece_ready, e * PIECES + PIECES)
                slot = e % 2
                for kk in range(2):
                    ph_, pl_ = piece(slot, KP + kk)
                    for b in range(2):
                        last = three(ps_y[:, b * 512:(b + 1) * 512], hth[s][:, kk, :],
                                     htl[s][:, kk, :], ph_[:, b * 512:(b + 1) * 512],
                                     pl_[:, b * 512:(b + 1) * 512], kk == 0, kk == 1)
                last.then_inc(down_done, 1)

            def turn_hidden(j):
                pe.wait_ge(hid_ready, j + 1)
                wait(pe, hid_split, j)
                for kk in range(2):
                    last = nc.tensor.transpose(ps_h[:, kk, :], hid[:, kk * P:(kk + 1) * P], ident[:, :])
                last.then_inc(hid_turned, 1)

            pe.wait_ge(ident_ready, 16)
            pe.sem_inc(down_done, 1)
            n = pairs(pe)
            turn(0, 0, 16)
            turn(1, 1, 16)
            gate_up(0, 0, 0, True)
            turn(2, 0, 32)
            turn_hidden(0)
            gate_up(1, 1, expert_of(pe, 1))
            with pe.Fori(0, n) as i:
                e0, e2 = expert_of(pe, i * 2), expert_of(pe, i * 2 + 2)
                turn(i * 2 + 3, 1, i * 16 + 32)
                down(i * 2, 0, e0)
                turn_hidden(i * 2 + 1)
                gate_up(i * 2 + 2, 0, e2)
                e1, e3 = expert_of(pe, i * 2 + 1), expert_of(pe, i * 2 + 3)
                turn(i * 2 + 4, 0, i * 16 + 48)
                down(i * 2 + 1, 1, e1)
                turn_hidden(i * 2 + 2)
                gate_up(i * 2 + 3, 1, e3)
            with pe.Fori(0, SHARED_PAIRS) as m:
                i = m + n
                turn(i * 2 + 3, 1, i * 16 + 32)
                down(i * 2, 0, NE, m * 2)
                turn_hidden(i * 2 + 1)
                gate_up(i * 2 + 2, 0, NE)
                turn(i * 2 + 4, 0, i * 16 + 48)
                down(i * 2 + 1, 1, NE, m * 2 + 1)
                turn_hidden(i * 2 + 2)
                gate_up(i * 2 + 3, 1, NE)
            i = n + SHARED_PAIRS
            down(i * 2, 0, NE, NT - 2)
            turn_hidden(i * 2 + 1)
            down(i * 2 + 1, 1, NE, NT - 1)

        @block.scalar
        def _(act):
            def copy(dst, src, **kw):
                return nc.scalar.activation(dst, src, ACT.Copy, **kw)

            def pieces_hi(e, lo, hi, j):
                if lo < KP:
                    wait(act, gu_done, j)
                if hi > KP:
                    act.wait_ge(down_done, j + 1)
                for p in range(lo, hi):
                    act.wait_ge(piece_in[p], (e + 1) * 16)
                    at = (e % 2) * PIECES + p
                    dst = wh[:, at, :] if isinstance(at, int) else wh[:, ds1(at), :].rearrange(
                        "q a f -> q (a f)")
                    copy(dst, raw[:, p, :]).then_inc(piece_hi, 1)

            def x_high(j, s):
                act.wait_ge(xs_turned, j + 1)
                wait(act, gu_done, j - 1)
                copy(xh[s][:, :, :], ps_x[:, :, :]).then_inc(xs_hi, 1)

            def gate_sigmoid(j, s):
                act.wait_ge(gu_done, j + 1)
                wait(act, hid_ready, j)
                nc.scalar.activation(sg[:, :], ps_gu[s][:, 0:H], ACT.Sigmoid).then_inc(gate_sig, 1)

            def hidden_high(j, s):
                act.wait_ge(hid_turned, j + 1)
                act.wait_ge(down_done, j)
                copy(hth[s][:, :, :], ps_h[:, :, :]).then_inc(hid_hi, 1)

            def output(j, s, listed, added):
                act.wait_ge(down_done, j + 2)
                act.wait_ge(sidx_in[s], listed)
                act.wait_ge(y_out[s], added)
                copy(y[s][:, :], ps_y[:, :], scale=sidx[s][:, :].bitcast(F32)[:, 1:2]
                     ).then_inc(y_ready, 1)

            act.sem_inc(y_ready, 1)
            pieces_hi(0, 0, PIECES, 0)
            x_high(0, 0)
            x_high(1, 1)
            gate_sigmoid(0, 0)
            x_high(2, 0)
            pieces_hi(1, 0, PIECES, 0)
            hidden_high(0, 0)
            n = pairs(act)
            with act.Fori(0, n) as i:
                for d in (1, 2):
                    j = i * 2 + d
                    s = d % 2
                    gate_sigmoid(j, s)
                    x_high(j + 2, s)
                    e = to_split(act, j)
                    with act.If(e > 0):
                        pieces_hi(e, 0, KP, j)
                    output(j - 1, 1 - s, i * 16 + 16, i * 16 + 16)
                    hidden_high(j, s)
                    with act.If(e > 0):
                        pieces_hi(e, KP, PIECES, j)
            def square(t, s):
                act.wait_ge(z_added, t + 2)
                carry(act, marks)
                act.drain()
                nc.scalar.activation(junk[:, :], y[s][:, :], ACT.Square, scale=float(D) ** -0.5,
                                     accum_out=mean[:, s:s + 1]).then_inc(z_mean, 1)

            with act.Fori(0, SHARED_PAIRS) as m:
                i = m + n
                for d in (1, 2):
                    s = d % 2
                    gate_sigmoid(i * 2 + d, s)
                    x_high(i * 2 + (d + 2), s)
                    hidden_high(i * 2 + d, s)
                    square(m * 2 + (d - 1), 1 - s)
            j = (n + SHARED_PAIRS) * 2 + 1
            gate_sigmoid(j, 1)
            hidden_high(j, 1)
            square(NT - 2, 0)
            square(NT - 1, 1)

        @block.vector
        def _(dve):
            V = nc.vector

            def pieces_lo(e, lo, hi):
                for p in range(lo, hi):
                    dve.wait_ge(piece_hi, e * PIECES + (p + 1))
                    at = (e % 2) * PIECES + p
                    h_, l_ = (w[:, at, :] if isinstance(at, int) else w[:, ds1(at), :].rearrange(
                        "q a f -> q (a f)") for w in (wh, wl))
                    V.tensor_tensor(l_, raw[:, p, :], h_, ALU.subtract).then_inc(piece_ready, 1)

            def x_low(j, s):
                dve.wait_ge(xs_hi, j + 1)
                V.tensor_tensor(xl[s][:, :, :], ps_x[:, :, :], xh[s][:, :, :], ALU.subtract
                                ).then_inc(xs_split, 1)

            def hidden(j, s):
                dve.wait_ge(gate_sig, j + 1)
                wait(dve, hid_turned, j)
                V.tensor_tensor(hid[:, :], ps_gu[s][:, 0:H], sg[:, :], ALU.mult)
                dve.drain()
                V.tensor_tensor(hid[:, :], hid[:, :], ps_gu[s][:, H:2 * H], ALU.mult
                                ).then_inc(hid_ready, 1)

            def hidden_low(j, s):
                dve.wait_ge(hid_hi, j + 1)
                V.tensor_tensor(htl[s][:, :, :], ps_h[:, :, :], hth[s][:, :, :], ALU.subtract
                                ).then_inc(hid_split, 1)

            dve.sem_inc(z_added, 1)
            pieces_lo(0, 0, PIECES)
            x_low(0, 0)
            x_low(1, 1)
            hidden(0, 0)
            x_low(2, 0)
            pieces_lo(1, 0, PIECES)
            hidden_low(0, 0)
            dve.wait_ge(gfin_in, 16)
            n = pairs(dve)
            with dve.Fori(0, n) as i:
                for d in (1, 2):
                    j = i * 2 + d
                    s = d % 2
                    hidden(j, s)
                    x_low(j + 2, s)
                    e = to_split(dve, j)
                    with dve.If(e > 0):
                        pieces_lo(e, 0, KP)
                    hidden_low(j, s)
                    with dve.If(e > 0):
                        pieces_lo(e, KP, PIECES)
            def add_tile(t, s, j, loaded):
                dve.wait_ge(acc_in[s], loaded)
                dve.wait_ge(down_done, j + 2)
                V.tensor_tensor(y[s][:, :], y[s][:, :], ps_y[:, :], ALU.add).then_inc(z_added, 1)

            def scale_tile(t, s):
                dve.wait_ge(z_rstd, t + 1)
                V.scalar_tensor_tensor(out=y[s][:, :], in0=y[s][:, :], scalar=rstd[:, s:s + 1],
                                       in1=gfin[:, :], op0=ALU.mult, op1=ALU.mult
                                       ).then_inc(z_normed, 1)

            with dve.Fori(0, SHARED_PAIRS) as m:
                i = m + n
                for d in (1, 2):
                    s = d % 2
                    t = m * 2 + (d - 1)
                    hidden(i * 2 + d, s)
                    x_low(i * 2 + (d + 2), s)
                    add_tile(t, 1 - s, i * 2 + (d - 1), m * 16 + 16)
                    hidden_low(i * 2 + d, s)
                    scale_tile(t, 1 - s)
            j = (n + SHARED_PAIRS) * 2
            hidden(j + 1, 1)
            add_tile(NT - 2, 0, j, 8 * NT)
            hidden_low(j + 1, 1)
            scale_tile(NT - 2, 0)
            add_tile(NT - 1, 1, j + 1, 8 * NT)
            scale_tile(NT - 1, 1)


def lay_out(x, g_mix, w_in, b_gate, w_pool_group, pool_scale, w_pool_out, conv_w, w_conv_out, w_o,
            g_ffn, w_router, router_bias, e_gate, e_up, e_down, s_gate, s_up, s_down, g_final):
    a = {k: np.asarray(v) for k, v in locals().items()}
    rows = lambda v: np.ascontiguousarray(np.broadcast_to(v.reshape(1, -1), (P, v.size)))
    slices = lambda w: w.reshape(-1, P, w.shape[1]).transpose(1, 0, 2)

    def column(w, m):
        return slices(w)[:, :, m * P:(m + 1) * P]

    w_in = a["w_in"]
    o = [0, G, 2 * G, 3 * G, 4 * G, 4 * G + MT]
    units = []
    for q in range(G):
        units += [column(w_in, o[n] + q) for n in (0, 2, 3, 1)]
    for m in range(MT):
        units += [column(w_in, o[4] + m), column(w_in, o[5] + m),
                  np.concatenate([column(a["w_pool_out"], m), column(a["w_conv_out"], m)], axis=1)]
    wo = slices(a["w_o"])
    for h in range(2):
        for v in range(4):
            units.append(wo[:, 2 * v:2 * v + 2, h * 512:(h + 1) * 512])
    units = np.stack([u.reshape(P, D) for u in units])

    def expert(gate, up, down):
        gu = np.concatenate([slices(gate), slices(up)], axis=2).reshape(P, KD // 2, D)
        return np.concatenate([gu, slices(down)], axis=1)

    experts = np.empty((NE + 1, P, PIECES, D), np.float32)
    experts[NE] = expert(a["s_gate"], a["s_up"], a["s_down"])
    for e in range(NE):
        experts[e] = expert(a["e_gate"][e], a["e_up"][e], a["e_down"][e])

    t = np.arange(HALO)
    inv = np.stack([1.0 / np.minimum(t + 1, w) for w in WINDOWS]).astype(np.float32)
    iotas = np.zeros((3, P, NB), np.float32)
    iotas[0] = 1.0
    iotas[1:3] = np.arange(NB)
    return {
        "x": a["x"].reshape(S, D),
        "units": units,
        "wgroup": np.ascontiguousarray(a["w_pool_group"].transpose(1, 0, 2)),
        "pool_scale": np.ascontiguousarray(a["pool_scale"].reshape(G, P).T),
        "conv_w": np.ascontiguousarray(a["conv_w"].reshape(3, G, P).transpose(2, 1, 0)),
        "b_gate": np.ascontiguousarray(a["b_gate"].reshape(2 * MT, P).T),
        "g_mix": rows(a["g_mix"]),
        "g_ffn": rows(a["g_ffn"]),
        "g_final": rows(a["g_final"]),
        "w_router": np.ascontiguousarray(slices(a["w_router"])),
        "router_bias": rows(a["router_bias"]),
        "experts": experts,
        "inv_count": np.ascontiguousarray(np.broadcast_to(inv, (P, G, HALO))),
        "ident": np.eye(P, dtype=np.float32),
        "tri": np.triu(np.ones((P, P), np.float32), 1),
        "iotas": iotas,
    }


def kernel(**inputs):
    import concourse.bacc as bacc
    from concourse.bass_utils import run_bass_kernel_spmd

    arrays = lay_out(**inputs)
    nc = bacc.Bacc("TRN2", target_bir_lowering=False, num_devices=1)
    args = {n: nc.dram_tensor(n, v.shape, mybir.dt.from_np(v.dtype), kind="ExternalInput").ap()
            for n, v in arrays.items()}
    out = nc.dram_tensor("out", (S, D), F32, kind="ExternalOutput").ap()
    build(nc, out=out, **args)
    r = run_bass_kernel_spmd(nc, [arrays], core_ids=[0])
    return r.results[0]["out"].reshape(1, S, D)
```
